# Optimizing a Trainium2 kernel written in Bass

```python
import jax, jax.numpy as jnp
from jax import lax
import numpy as np
import math

D_MODEL = 1024
BATCH = 1
SEQ = 256
DEPTH = 2

HEAD_DIM = 64
A_HEADS = 8
A_KV_HEADS = 2
A_GROUP = A_HEADS // A_KV_HEADS
A_WINDOW = 128
A_BLOCK = 128
A_BAND_BLOCKS = 3
B_HEADS = 8
GRID_W = 64
B_MAX_ROWS = 8
B_WIN_C = 16
B_QBLOCK_C = 16
B_KBAND_C = 32
FFN_HIDDEN = -(-8 * D_MODEL // (3 * 256)) * 256
ROPE_THETA = 10000.0
EPS = 1e-6
NEG = -1e30

A_Q_W = A_HEADS * HEAD_DIM
A_KV_W = A_KV_HEADS * HEAD_DIM
B_W = B_HEADS * HEAD_DIM
IN_WIDTHS = [A_Q_W, A_KV_W, A_KV_W, B_W, B_W, B_W, D_MODEL, D_MODEL]
IN_COLS = sum(IN_WIDTHS)
IN_SPLITS = np.cumsum(IN_WIDTHS)[:-1].tolist()


def rms_norm(x, g):
    xf = x.astype(jnp.float32)
    y = xf * lax.rsqrt(jnp.mean(xf * xf, axis=-1, keepdims=True) + EPS)
    return (y * g.astype(jnp.float32)).astype(x.dtype)

def rope_tables(positions):
    half = HEAD_DIM // 2
    inv = ROPE_THETA ** (-jnp.arange(half, dtype=jnp.float32) / half)
    ang = positions.astype(jnp.float32)[:, None] * inv[None, :]
    return jnp.cos(ang)[None, :, None, :], jnp.sin(ang)[None, :, None, :]

def apply_rope(x, cos, sin):
    half = HEAD_DIM // 2
    xf = x.astype(jnp.float32)
    x1, x2 = xf[..., :half], xf[..., half:]
    out = jnp.concatenate([x1 * cos - x2 * sin, x2 * cos + x1 * sin], axis=-1)
    return out.astype(x.dtype)

def window_gqa(q, k, v, sink):
    b, s = q.shape[:2]
    nb = s // A_BLOCK
    pad = ((0, 0), (A_BLOCK, A_BLOCK), (0, 0), (0, 0))
    kp = jnp.pad(k, pad).reshape(b, nb + 2, A_BLOCK, A_KV_HEADS, HEAD_DIM)
    vp = jnp.pad(v, pad).reshape(b, nb + 2, A_BLOCK, A_KV_HEADS, HEAD_DIM)
    kb = jnp.concatenate([kp[:, o:o + nb] for o in range(A_BAND_BLOCKS)], axis=2)
    vb = jnp.concatenate([vp[:, o:o + nb] for o in range(A_BAND_BLOCKS)], axis=2)
    qb = q.reshape(b, nb, A_BLOCK, A_KV_HEADS, A_GROUP, HEAD_DIM)
    scores = jnp.einsum('bnqkgd,bnjkd->bnkgqj', qb, kb).astype(jnp.float32) * (HEAD_DIM ** -0.5)
    n_i = np.arange(nb)[:, None, None]
    r_i = np.arange(A_BLOCK)[None, :, None]
    j_i = np.arange(A_BAND_BLOCKS * A_BLOCK)[None, None, :]
    kpos = n_i * A_BLOCK - A_BLOCK + j_i
    qpos = n_i * A_BLOCK + r_i
    valid = (np.abs(kpos - qpos) <= A_WINDOW) & (kpos >= 0) & (kpos < s)
    scores = jnp.where(valid[None, :, None, None], scores, NEG)
    sink_col = jnp.broadcast_to(
        sink.astype(jnp.float32).reshape(A_KV_HEADS, A_GROUP)[None, None, :, :, None, None],
        scores.shape[:-1] + (1,))
    p = jax.nn.softmax(jnp.concatenate([scores, sink_col], axis=-1), axis=-1)[..., :-1]
    out = jnp.einsum('bnkgqj,bnjkd->bnqkgd', p.astype(v.dtype), vb)
    return out.reshape(b, s, A_Q_W)

def neighbourhood_attn(q, k, v, rel_bias):
    b, s = q.shape[:2]
    rows = s // GRID_W
    wr = min(B_MAX_ROWS, rows)
    ncb = GRID_W // B_QBLOCK_C
    r = np.arange(rows)
    rs = np.clip(r - wr // 2, 0, rows - wr)
    row_idx = rs[:, None] + np.arange(wr)[None, :]
    jb = np.arange(ncb)
    kc0 = np.clip(jb * B_QBLOCK_C - B_WIN_C // 2, 0, GRID_W - B_KBAND_C)
    col_idx = kc0[:, None] + np.arange(B_KBAND_C)[None, :]
    qcol = jb[:, None] * B_QBLOCK_C + np.arange(B_QBLOCK_C)[None, :]
    cs = np.clip(qcol - B_WIN_C // 2, 0, GRID_W - B_WIN_C)
    valid = (col_idx[:, None, :] >= cs[..., None]) & (col_idx[:, None, :] < cs[..., None] + B_WIN_C)
    dr_i = row_idx - r[:, None] + B_MAX_ROWS - 1
    dc_i = np.clip(col_idx[:, None, :] - qcol[..., None] + B_WIN_C - 1, 0, 2 * B_WIN_C - 2)
    bias = rel_bias[:, dr_i[:, None, None, :, None], dc_i[None, :, :, None, :]]
    bias = jnp.where(valid[None, None, :, :, None, :], bias.astype(jnp.float32), NEG)
    kg = k.reshape(b, rows, GRID_W, B_HEADS, HEAD_DIM)
    vg = v.reshape(b, rows, GRID_W, B_HEADS, HEAD_DIM)
    gr = row_idx[:, None, :, None]
    gc = col_idx[None, :, None, :]
    kb = kg[:, gr, gc]
    vb = vg[:, gr, gc]
    qg = q.reshape(b, rows, ncb, B_QBLOCK_C, B_HEADS, HEAD_DIM)
    scores = jnp.einsum('brjqhd,brjwkhd->bhrjqwk', qg, kb).astype(jnp.float32) * (HEAD_DIM ** -0.5)
    scores = scores + bias[None]
    shp = scores.shape
    p = jax.nn.softmax(scores.reshape(shp[:-2] + (wr * B_KBAND_C,)), axis=-1).reshape(shp)
    out = jnp.einsum('bhrjqwk,brjwkhd->brjqhd', p.astype(v.dtype), vb)
    return out.reshape(b, s, B_W)

def first_inputs(seed: int = 0) -> dict:
    key = jax.random.key(seed)
    ks = jax.random.split(key, 16)
    f32 = jnp.float32

    def w(k, shape, fan_in):
        return jax.random.normal(k, shape, f32) * (fan_in ** -0.5)

    def gain(k, shape):
        return 1.0 + 0.02 * jax.random.normal(k, shape, f32)

    return {
        "x": jax.random.normal(ks[0], (BATCH, SEQ, D_MODEL), f32),
        "positions": jnp.arange(SEQ, dtype=jnp.int32),
        "attn_norm_g": gain(ks[1], (DEPTH, D_MODEL)),
        "w_in": w(ks[2], (DEPTH, D_MODEL, IN_COLS), D_MODEL),
        "q_norm_a": gain(ks[3], (DEPTH, HEAD_DIM)),
        "k_norm_a": gain(ks[4], (DEPTH, HEAD_DIM)),
        "sink_a": 0.5 * jax.random.normal(ks[5], (DEPTH, A_HEADS), f32),
        "q_norm_b": gain(ks[6], (DEPTH, HEAD_DIM)),
        "k_norm_b": gain(ks[7], (DEPTH, HEAD_DIM)),
        "rel_bias_b": 0.1 * jax.random.normal(ks[8], (DEPTH, B_HEADS, 2 * B_MAX_ROWS - 1, 2 * B_WIN_C - 1), f32),
        "w_proj_a": w(ks[9], (DEPTH, A_Q_W, D_MODEL), A_Q_W),
        "w_proj_b": w(ks[10], (DEPTH, B_W, D_MODEL), B_W),
        "w_out": w(ks[11], (DEPTH, D_MODEL, D_MODEL), D_MODEL),
        "ffn_norm_g": gain(ks[12], (DEPTH, D_MODEL)),
        "w_gate": w(ks[13], (DEPTH, D_MODEL, FFN_HIDDEN), D_MODEL),
        "w_up": w(ks[14], (DEPTH, D_MODEL, FFN_HIDDEN), D_MODEL),
        "w_down": w(ks[15], (DEPTH, FFN_HIDDEN, D_MODEL), FFN_HIDDEN),
    }

def first_block(x, positions, attn_norm_g, w_in, q_norm_a, k_norm_a, sink_a, q_norm_b, k_norm_b,
              rel_bias_b, w_proj_a, w_proj_b, w_out, ffn_norm_g, w_gate, w_up, w_down):
    b, s, _ = x.shape
    cos, sin = rope_tables(positions)
    for l in range(DEPTH):
        h = rms_norm(x, attn_norm_g[l])
        z = jnp.einsum('bsd,dc->bsc', h, w_in[l])
        qa, ka, va, qb, kb, vb, ga, gb = jnp.split(z, IN_SPLITS, axis=-1)
        qa = apply_rope(rms_norm(qa.reshape(b, s, A_HEADS, HEAD_DIM), q_norm_a[l]), cos, sin)
        ka = apply_rope(rms_norm(ka.reshape(b, s, A_KV_HEADS, HEAD_DIM), k_norm_a[l]), cos, sin)
        va = va.reshape(b, s, A_KV_HEADS, HEAD_DIM)
        ya = jnp.einsum('bsc,cd->bsd', window_gqa(qa, ka, va, sink_a[l]), w_proj_a[l])
        qb = rms_norm(qb.reshape(b, s, B_HEADS, HEAD_DIM), q_norm_b[l])
        kb = rms_norm(kb.reshape(b, s, B_HEADS, HEAD_DIM), k_norm_b[l])
        vb = vb.reshape(b, s, B_HEADS, HEAD_DIM)
        yb = jnp.einsum('bsc,cd->bsd', neighbourhood_attn(qb, kb, vb, rel_bias_b[l]), w_proj_b[l])
        mixed = jax.nn.sigmoid(ga) * ya + jax.nn.sigmoid(gb) * yb
        x = x + jnp.einsum('bsd,de->bse', mixed, w_out[l])
        h = rms_norm(x, ffn_norm_g[l])
        u = jax.nn.silu(jnp.einsum('bsd,df->bsf', h, w_gate[l])) * jnp.einsum('bsd,df->bsf', h, w_up[l])
        x = x + jnp.einsum('bsf,fd->bsd', u, w_down[l])
    return x


N_HEADS_A = 8
HEAD_DIM_A = 64
D_A = N_HEADS_A * HEAD_DIM_A
ATTN_PATTERNS = ((128, 1), (512, 4), (2048, 16))
ATTN_BLOCK = 128
NUM_BUCKETS = 32
MAX_DISTANCE = 2048
N_HEADS_M = 4
HEAD_DIM_M = 128
D_M = N_HEADS_M * HEAD_DIM_M
CONV_K = 4
MLSTM_CHUNK = 128
P_IN = 3 * D_A + 2 * D_M
D_FF = 2816
N_EXPERTS = 8
TOP_K = 2
D_FF_E = 3584
N_DENSE = (DEPTH + 1) // 2
N_MOE = DEPTH // 2
ALPHA = (2.0 * DEPTH) ** 0.25
BETA = (8.0 * DEPTH) ** -0.25
LN_EPS = 1e-5


def layer_norm(x, g, b):
    xf = x.astype(jnp.float32)
    mu = xf.mean(-1, keepdims=True)
    var = jnp.square(xf - mu).mean(-1, keepdims=True)
    return ((xf - mu) * lax.rsqrt(var + LN_EPS) * g.astype(jnp.float32) + b.astype(jnp.float32)).astype(x.dtype)

def rel_bucket(dist):
    exact = NUM_BUCKETS // 2
    d = jnp.maximum(dist, exact).astype(jnp.float32)
    log_b = exact + (jnp.log(d / exact) / math.log(MAX_DISTANCE / exact) * (NUM_BUCKETS - exact)).astype(jnp.int32)
    return jnp.where(dist < exact, dist, jnp.minimum(log_b, NUM_BUCKETS - 1))

def strided_window_attention(q, k, v, rel_bias, window, dilation):
    B, S, H, hd = q.shape
    L = S // dilation
    W = window // dilation
    blk = ATTN_BLOCK
    nb = -(-L // blk)
    Lp = nb * blk

    def to_classes(t):
        t = t.reshape(B, L, dilation, H, hd).transpose(0, 2, 1, 3, 4).reshape(B * dilation, L, H, hd)
        return jnp.pad(t, ((0, 0), (0, Lp - L), (0, 0), (0, 0)))

    qc, kc, vc = to_classes(q), to_classes(k), to_classes(v)
    qb = qc.reshape(B * dilation, nb, blk, H, hd)

    def band(t):
        t = jnp.pad(t, ((0, 0), (blk, 0), (0, 0), (0, 0))).reshape(B * dilation, nb + 1, blk, H, hd)
        return jnp.concatenate([t[:, :-1], t[:, 1:]], axis=2)

    kb, vb = band(kc), band(vc)
    qi = jnp.arange(blk)[:, None]
    kj = jnp.arange(2 * blk)[None, :]
    rel = qi + blk - kj
    bias = rel_bias[rel_bucket(jnp.maximum(rel, 0) * dilation)]
    bias = bias.transpose(2, 0, 1).astype(jnp.float32)
    key_pos = jnp.arange(nb)[:, None] * blk - blk + kj
    mask = ((rel >= 0) & (rel <= W))[None] & (key_pos >= 0)[:, None, :]

    logits = jnp.einsum('bnqhd,bnkhd->bnhqk', qb.astype(jnp.float32), kb.astype(jnp.float32)) * (hd ** -0.5) + bias
    logits = jnp.where(mask[None, :, None], logits, -jnp.inf)
    m = logits.max(-1, keepdims=True)
    p = jnp.exp(logits - m)
    denom = p.sum(-1, keepdims=True)
    o = jnp.einsum('bnhqk,bnkhd->bnqhd', p / denom, vb.astype(jnp.float32))
    lse = (m + jnp.log(denom))[..., 0].transpose(0, 1, 3, 2)

    def from_classes(t):
        t = t.reshape((B * dilation, Lp) + t.shape[3:])[:, :L]
        t = t.reshape((B, dilation, L) + t.shape[2:])
        t = jnp.moveaxis(t, 1, 2)
        return t.reshape((B, S) + t.shape[3:])

    return from_classes(o), from_classes(lse)

def dilated_attention(q, k, v, rel_bias):
    outs, lses = [], []
    for window, dilation in ATTN_PATTERNS:
        o, lse = strided_window_attention(q, k, v, rel_bias, window, dilation)
        outs.append(o)
        lses.append(lse)
    wts = jax.nn.softmax(jnp.stack(lses), axis=0)
    return jnp.einsum('pbsh,pbshd->bshd', wts, jnp.stack(outs))

def mlstm_chunkwise(q, k, v, i_pre, log_f):
    B, S, H, hd = q.shape
    L = MLSTM_CHUNK
    nc = S // L
    k = k * (hd ** -0.5)
    tri = jnp.tril(jnp.ones((L, L), dtype=bool))

    def chunks(t):
        return jnp.moveaxis(t.reshape((B, nc, L) + t.shape[2:]), 1, 0)

    def step(carry, xs):
        C, n, m = carry
        qc, kc, vc, ic, fc = xs
        b = jnp.cumsum(fc, axis=1).transpose(0, 2, 1)
        ic = ic.transpose(0, 2, 1)
        Dm = jnp.where(tri, b[..., :, None] - b[..., None, :] + ic[..., None, :], -jnp.inf)
        inter = b + m[..., None]
        m_loc = jnp.maximum(inter, Dm.max(-1))
        Dexp = jnp.exp(Dm - m_loc[..., None])
        inter_w = jnp.exp(inter - m_loc)
        s = jnp.einsum('blhd,bshd->bhls', qc, kc) * Dexp
        num = inter_w[..., None] * jnp.einsum('blhd,bhde->bhle', qc, C) + jnp.einsum('bhls,bshe->bhle', s, vc)
        nq = inter_w * jnp.einsum('blhd,bhd->bhl', qc, n) + s.sum(-1)
        h = num / jnp.maximum(jnp.abs(nq), jnp.exp(-m_loc))[..., None]
        bL = b[..., -1]
        g = bL[..., None] - b + ic
        m_new = jnp.maximum(bL + m, g.max(-1))
        decay = jnp.exp(bL + m - m_new)
        w = jnp.exp(g - m_new[..., None])
        C = decay[..., None, None] * C + jnp.einsum('bhs,bshd,bshe->bhde', w, kc, vc)
        n = decay[..., None] * n + jnp.einsum('bhs,bshd->bhd', w, kc)
        return (C, n, m_new), h.transpose(0, 2, 1, 3)

    init = (jnp.zeros((B, H, hd, hd), jnp.float32), jnp.zeros((B, H, hd), jnp.float32),
            jnp.zeros((B, H), jnp.float32))
    _, hs = lax.scan(step, init, (chunks(q), chunks(k), chunks(v), chunks(i_pre), chunks(log_f)))
    return jnp.moveaxis(hs, 0, 1).reshape(B, S, H, hd)

def causal_conv(x, w, b):
    out = lax.conv_general_dilated(x, w[:, None, :].astype(x.dtype), window_strides=(1,),
                                   padding=[(CONV_K - 1, 0)], dimension_numbers=('NWC', 'WIO', 'NWC'),
                                   feature_group_count=x.shape[-1])
    return out + b

def token_mixer(x, rel_bias, w_in, w_gate, b_gate, conv_w, conv_b, w_qk_m, w_v_m, w_if, b_if,
                m_norm_g, w_br_a, w_br_m, w_o):
    B, S, _ = x.shape
    proj = x @ w_in
    q_a, k_a, v_a, x_m, z_m = jnp.split(proj, [D_A, 2 * D_A, 3 * D_A, 3 * D_A + D_M], axis=-1)

    ha = lambda t: t.reshape(B, S, N_HEADS_A, HEAD_DIM_A)
    y_a = dilated_attention(ha(q_a), ha(k_a), ha(v_a), rel_bias).reshape(B, S, D_A).astype(x.dtype)

    hm = lambda t: t.reshape(B, S, N_HEADS_M, HEAD_DIM_M)
    x_c = jax.nn.silu(causal_conv(x_m, conv_w, conv_b))
    q_m = jnp.einsum('bshd,hde->bshe', hm(x_c), w_qk_m[0])
    k_m = jnp.einsum('bshd,hde->bshe', hm(x_c), w_qk_m[1])
    v_m = jnp.einsum('bshd,hde->bshe', hm(x_m), w_v_m)
    qkv = jnp.concatenate([q_m.reshape(B, S, D_M), k_m.reshape(B, S, D_M), v_m.reshape(B, S, D_M)], axis=-1)
    gates = (qkv @ w_if + b_if).astype(jnp.float32)
    i_pre, f_pre = jnp.split(gates, 2, axis=-1)
    f32 = lambda t: t.astype(jnp.float32)
    h = mlstm_chunkwise(f32(q_m), f32(k_m), f32(v_m), i_pre, jax.nn.log_sigmoid(f_pre))
    mu = h.mean(-1, keepdims=True)
    var = jnp.square(h - mu).mean(-1, keepdims=True)
    h = ((h - mu) * lax.rsqrt(var + LN_EPS)).reshape(B, S, D_M) * m_norm_g.astype(jnp.float32)
    y_m = (jax.nn.sigmoid(f32(z_m)) * h).astype(x.dtype)

    g_a, g_m = jnp.split(jax.nn.sigmoid(x @ w_gate + b_gate), 2, axis=-1)
    merged = g_a * (y_a @ w_br_a) + g_m * (y_m @ w_br_m)
    return merged @ w_o

def swiglu(x, w13, w2):
    a, g = jnp.split(x @ w13, 2, axis=-1)
    return (jax.nn.silu(a) * g) @ w2

def moe_ffn(x, router_w, router_b, w13, w2):
    logits = (x @ router_w).astype(jnp.float32) + router_b.astype(jnp.float32)
    top_v, top_i = lax.top_k(logits, TOP_K)
    wts = jax.nn.softmax(top_v, axis=-1)
    gate = jnp.einsum('bsk,bske->bse', wts, jax.nn.one_hot(top_i, N_EXPERTS, dtype=jnp.float32)).astype(x.dtype)
    y = jnp.zeros_like(x)
    for e in range(N_EXPERTS):
        y = y + gate[..., e:e + 1] * swiglu(x, w13[e], w2[e])
    return y

def second_inputs(seed: int = 0) -> dict:
    key = jax.random.key(seed)
    ks = jax.random.split(key, 24)
    nrm = lambda k, shape, scale: jax.random.normal(k, shape, jnp.float32) * scale
    b_if = jnp.concatenate([nrm(ks[10], (DEPTH, N_HEADS_M), 0.1),
                            3.0 + 3.0 * jax.random.uniform(ks[11], (DEPTH, N_HEADS_M), jnp.float32)], axis=-1)
    return {
        "x": nrm(ks[0], (BATCH, SEQ, D_MODEL), 1.0),
        "rel_bias": nrm(ks[1], (NUM_BUCKETS, N_HEADS_A), 0.2),
        "w_in": nrm(ks[2], (DEPTH, D_MODEL, P_IN), D_MODEL ** -0.5),
        "w_gate": nrm(ks[3], (DEPTH, D_MODEL, 2 * D_MODEL), D_MODEL ** -0.5),
        "b_gate": nrm(ks[4], (DEPTH, 2 * D_MODEL), 0.02),
        "conv_w": nrm(ks[5], (DEPTH, CONV_K, D_M), CONV_K ** -0.5),
        "conv_b": nrm(ks[6], (DEPTH, D_M), 0.02),
        "w_qk_m": nrm(ks[7], (DEPTH, 2, N_HEADS_M, HEAD_DIM_M, HEAD_DIM_M), HEAD_DIM_M ** -0.5),
        "w_v_m": nrm(ks[8], (DEPTH, N_HEADS_M, HEAD_DIM_M, HEAD_DIM_M), HEAD_DIM_M ** -0.5),
        "w_if": nrm(ks[9], (DEPTH, 3 * D_M, 2 * N_HEADS_M), (3 * D_M) ** -0.5),
        "b_if": b_if,
        "m_norm_g": 1.0 + nrm(ks[12], (DEPTH, D_M), 0.02),
        "w_br_a": nrm(ks[13], (DEPTH, D_A, D_MODEL), D_A ** -0.5),
        "w_br_m": nrm(ks[14], (DEPTH, D_M, D_MODEL), D_M ** -0.5),
        "w_o": nrm(ks[15], (DEPTH, D_MODEL, D_MODEL), BETA * D_MODEL ** -0.5),
        "ln_g": 1.0 + nrm(ks[16], (DEPTH, 2, D_MODEL), 0.02),
        "ln_b": nrm(ks[17], (DEPTH, 2, D_MODEL), 0.02),
        "ffn_w13": nrm(ks[18], (N_DENSE, D_MODEL, 2 * D_FF), D_MODEL ** -0.5),
        "ffn_w2": nrm(ks[19], (N_DENSE, D_FF, D_MODEL), BETA * D_FF ** -0.5),
        "router_w": nrm(ks[20], (N_MOE, D_MODEL, N_EXPERTS), D_MODEL ** -0.5),
        "router_b": nrm(ks[21], (N_MOE, N_EXPERTS), 0.01),
        "exp_w13": nrm(ks[22], (N_MOE, N_EXPERTS, D_MODEL, 2 * D_FF_E), D_MODEL ** -0.5),
        "exp_w2": nrm(ks[23], (N_MOE, N_EXPERTS, D_FF_E, D_MODEL), BETA * D_FF_E ** -0.5),
    }

def second_block(x, rel_bias, w_in, w_gate, b_gate, conv_w, conv_b, w_qk_m, w_v_m, w_if, b_if, m_norm_g,
              w_br_a, w_br_m, w_o, ln_g, ln_b, ffn_w13, ffn_w2, router_w, router_b, exp_w13, exp_w2):
    for l in range(DEPTH):
        y = token_mixer(x, rel_bias, w_in[l], w_gate[l], b_gate[l], conv_w[l], conv_b[l], w_qk_m[l],
                        w_v_m[l], w_if[l], b_if[l], m_norm_g[l], w_br_a[l], w_br_m[l], w_o[l])
        x = layer_norm(ALPHA * x + y, ln_g[l, 0], ln_b[l, 0])
        j = l // 2
        if l % 2 == 0:
            y = swiglu(x, ffn_w13[j], ffn_w2[j])
        else:
            y = moe_ffn(x, router_w[j], router_b[j], exp_w13[j], exp_w2[j])
        x = layer_norm(ALPHA * x + y, ln_g[l, 1], ln_b[l, 1])
    return x


def setup_inputs(seed=0):
    out = dict(first_inputs(seed))
    for name, value in second_inputs(seed + 1).items():
        if name != "x":
            out[name + "_2"] = value
    return out


def reference(
    x, positions, attn_norm_g, w_in, q_norm_a, k_norm_a, sink_a, q_norm_b, k_norm_b, rel_bias_b,
    w_proj_a, w_proj_b, w_out, ffn_norm_g, w_gate, w_up, w_down, rel_bias_2, w_in_2, w_gate_2,
    b_gate_2, conv_w_2, conv_b_2, w_qk_m_2, w_v_m_2, w_if_2, b_if_2, m_norm_g_2, w_br_a_2,
    w_br_m_2, w_o_2, ln_g_2, ln_b_2, ffn_w13_2, ffn_w2_2, router_w_2, router_b_2, exp_w13_2,
    exp_w2_2,
):
    x = first_block(
        x, positions, attn_norm_g, w_in, q_norm_a, k_norm_a, sink_a, q_norm_b, k_norm_b,
        rel_bias_b, w_proj_a, w_proj_b, w_out, ffn_norm_g, w_gate, w_up, w_down,
    )
    return second_block(
        x, rel_bias_2, w_in_2, w_gate_2, b_gate_2, conv_w_2, conv_b_2, w_qk_m_2, w_v_m_2,
        w_if_2, b_if_2, m_norm_g_2, w_br_a_2, w_br_m_2, w_o_2, ln_g_2, ln_b_2, ffn_w13_2,
        ffn_w2_2, router_w_2, router_b_2, exp_w13_2, exp_w2_2,
    )


_drawn_inputs = setup_inputs


def setup_inputs(seed=0):
    import zlib

    import numpy as np

    out = dict(_drawn_inputs(seed))
    spreads = {}
    factors = {'attn_norm_g': 7.415,
     'q_norm_a': 8.0,
     'k_norm_a': 8.0,
     'sink_a': 8.0,
     'q_norm_b': 8.0,
     'k_norm_b': 8.0,
     'rel_bias_b': 2.836,
     'rel_bias_2': 3.507,
     'b_gate_2': 8.0,
     'conv_b_2': 8.0,
     'm_norm_g_2': 25.453,
     'router_b_2': 8.0}
    for name, (base, spread) in spreads.items():
        noise = np.random.default_rng([zlib.crc32(name.encode()), seed]).standard_normal(out[name].shape)
        drawn = base * np.exp(spread * noise) if base else spread * noise
        out[name] = __import__('jax').numpy.asarray(drawn.astype(out[name].dtype))
    for name, factor in factors.items():
        out[name] = (out[name] * factor).astype(out[name].dtype)
    return out
```

```python
import concourse.bass as bass
from concourse import mybir
from contextlib import ExitStack
import math
import numpy as np

NEG = -1e30
EPS = 1e-6
LN_EPS = 1e-5
ALPHA = 4.0 ** 0.25
NSLOT = 5
SLOT = 4096


def col_slot(parts):
    return ("cols", parts)


def row_slot(name, index, k0, k1):
    return ("rows", (name, index, k0, k1))


def layer_one_slots(l):
    s = []
    for a, b in ((0, 512), (512, 768), (768, 1280), (1280, 1792), (1792, 2304)):
        s.append(col_slot([("w_in", (l,), a, b)]))
    for j in range(4):
        s.append(col_slot([("w_in", (l,), 2304 + 256 * j, 2560 + 256 * j),
                           ("w_in", (l,), 3328 + 256 * j, 3584 + 256 * j)]))
    for j in range(2):
        s.append(col_slot([("w_proj_a", (l,), 512 * j, 512 * j + 512), ("w_proj_b", (l,), 512 * j, 512 * j + 512)]))
    for j in range(2):
        s.append(row_slot("w_out", (l,), 4 * j, 4 * j + 4))
    for j in range(11):
        s.append(col_slot([("w_gate", (l,), 256 * j, 256 * j + 256), ("w_up", (l,), 256 * j, 256 * j + 256)]))
    for j in range(6):
        s.append(row_slot("w_down", (l,), 4 * j, min(22, 4 * j + 4)))
    return s


def layer_two_slots(l):
    s = []
    for j in range(5):
        s.append(col_slot([("w_in_2", (l,), 512 * j, 512 * j + 512)]))
    for j in range(4):
        s.append(col_slot([("w_gate_2", (l,), 256 * j, 256 * j + 256),
                           ("w_gate_2", (l,), 1024 + 256 * j, 1280 + 256 * j)]))
    s.append(("mlstm", l))
    for j in range(2):
        s.append(col_slot([("w_br_a_2", (l,), 512 * j, 512 * j + 512), ("w_br_m_2", (l,), 512 * j, 512 * j + 512)]))
    for j in range(2):
        s.append(row_slot("w_o_2", (l,), 4 * j, 4 * j + 4))
    if l == 0:
        for j in range(11):
            s.append(col_slot([("ffn_w13_2", (0,), 256 * j, 256 * j + 256),
                               ("ffn_w13_2", (0,), 2816 + 256 * j, 3072 + 256 * j)]))
        for j in range(6):
            s.append(row_slot("ffn_w2_2", (0,), 4 * j, min(22, 4 * j + 4)))
    else:
        for e in range(8):
            for j in range(14):
                s.append(col_slot([("exp_w13_2", (0, e), 256 * j, 256 * j + 256),
                                   ("exp_w13_2", (0, e), 3584 + 256 * j, 3840 + 256 * j)]))
            for j in range(7):
                s.append(row_slot("exp_w2_2", (0, e), 4 * j, 4 * j + 4))
    return s


ROWS_OF = {"w_in": 1024, "w_proj_a": 512, "w_proj_b": 512, "w_out": 1024, "w_gate": 1024, "w_up": 1024,
           "w_down": 2816, "w_in_2": 1024, "w_gate_2": 1024, "w_br_a_2": 512, "w_br_m_2": 512, "w_o_2": 1024,
           "ffn_w13_2": 1024, "ffn_w2_2": 2816, "exp_w13_2": 1024, "exp_w2_2": 3584}


def slot_words(s):
    if s[0] == "cols":
        return sum(ROWS_OF[n] // 128 * (b - a) for n, _, a, b in s[1])
    if s[0] == "rows":
        return (s[1][3] - s[1][2]) * 1024
    return 8 * 128 + 4 * 128 + 96


VEC = {}
_at = 0
for _n, _c in (("attn_g", 16), ("ffn_g", 16), ("b_gate", 32), ("conv_w", 32), ("conv_b", 8), ("m_g", 8), ("qk_b", 4)):
    VEC[_n] = _at
    _at += _c
NVEC = _at
ROWV = 4 * 64 + 16 + 16 + 8
C_ID, C_J, C_JJ, C_ONE, C_TRI, C_CAUS, C_MA, C_MB, C_INV, C_IOTA = 0, 128, 256, 384, 512, 640, 896, 1408, 1472, 1504
NCONST = 1512


def constants():
    c = np.zeros((128, NCONST), np.float32)
    p = np.arange(128)[:, None]
    q = np.arange(128)[None, :]
    c[:, C_ID:C_ID + 128] = p == q
    c[:, C_J:C_J + 128] = p + q == 127
    c[:, C_JJ:C_JJ + 128] = (p // 64 == q // 64) & (p % 64 + q % 64 == 63)
    c[:, C_ONE:C_ONE + 128] = 1.0
    c[:, C_TRI:C_TRI + 128] = p <= q
    c[:, C_CAUS + 128:C_CAUS + 256] = np.where(q <= p, 0.0, NEG)
    c[:, C_MA + 128:C_MA + 256] = np.where(q <= p, 0.0, NEG)
    c[:, C_MA + 256:C_MA + 384] = np.where(q >= p, 0.0, NEG)
    k = np.arange(64)[None, :]
    cs = np.clip(p % 64 - 8, 0, 48)
    c[:, C_MB:C_MB + 64] = np.where((k >= cs) & (k < cs + 16), 0.0, NEG)
    c[:, C_INV:C_INV + 32] = (np.float32(10000.0) ** (-np.arange(32, dtype=np.float32) / np.float32(32)))[None, :]
    c[:, C_IOTA:C_IOTA + 8] = 8.0 - np.arange(8)[None, :]
    return c


def distance_constants():
    one = np.zeros((32, 384), np.float32)
    ln = np.full((8, 384), NEG, np.float32)
    for j in range(256):
        d = 255 - j
        if d < 16:
            b = d
        else:
            b = min(31, 16 + int(np.float32(np.log(np.float32(d) / np.float32(16))) / math.log(2048 / 16) * 16))
        one[b, j] = 1.0
        n = (d <= 128) + (d % 4 == 0) + (d % 16 == 0)
        if n:
            ln[:, j] = math.log(n)
    return one, ln


def program(nc, x_d, pos_d, ws_d, vec_d, row_d, ln_d, rel_d, relb_d, rw_d, cst_d, one_d, lnc_d, out_d):
    f32 = mybir.dt.float32
    ALU = mybir.AluOpType
    ACT = mybir.ActivationFunctionType
    AX = mybir.AxisListType

    scr = nc.dram_tensor("scratch_rel", (8, 384), f32).ap()

    ctx = ExitStack()
    with ctx:
        def sb(name, n, dt=f32):
            return ctx.enter_context(nc.sbuf_tensor(name, [128, n], dt))

        class Queue:

            def __init__(self, engine, name):
                self.e = engine
                self.sem = ctx.enter_context(nc.semaphore(name))
                self.n = 0
                self.seen = {}

            def wait(self, waits):
                for sem, v in flat(waits):
                    if self.seen.get(id(sem), 0) < v:
                        self.e.wait_ge(sem, v)
                        self.seen[id(sem)] = v

            def __call__(self, fn, *waits, sig=True):
                self.wait(waits)
                ins = fn(self.e)
                if sig:
                    ins.then_inc(self.sem, 1)
                    self.n += 1
                    return (self.sem, self.n)

            def dma(self, out, in_, mark, *waits):
                self.wait(waits)
                self.e.dma_start(out, in_).then_inc(mark[0], 16)
                return mark

        def flat(ws):
            out = []
            for w in ws:
                if w is None:
                    continue
                if isinstance(w, list):
                    out += flat(w)
                else:
                    out.append(w)
            return out

        P, V, A = Queue(nc.tensor, "s_pe"), Queue(nc.vector, "s_dve"), Queue(nc.scalar, "s_act")
        G, S = Queue(nc.gpsimd, "s_pool"), Queue(nc.sync, "s_sp")

        ring = [sb(f"ring{i}", SLOT) for i in range(NSLOT)]
        ring_sem = [ctx.enter_context(nc.semaphore(f"s_ring{i}")) for i in range(NSLOT)]
        ring_free = [None] * NSLOT
        X = sb("X", 2048)
        HT = sb("HT", 2048)
        U = sb("U", 7168)
        GT = sb("GT", 4096)
        LB = [sb("L0", 2048), sb("L1", 2048)]
        PT = sb("PT", 2048)
        BIAS = sb("BIAS", 3072)
        QT = sb("QT", 3584)
        O = sb("O", 1024)
        CST = sb("CST", NCONST)
        VECS = sb("VECS", NVEC)
        ROW = sb("ROW", ROWV)
        RW = sb("RW", 64)
        CS = sb("CS", 512)
        TRIG = sb("TRIG", 256)
        SM = sb("SM", 512)
        POSI = sb("POSI", 2, mybir.dt.int32)
        banks = [ctx.enter_context(nc.psum_tensor(f"bank{i}", [128, 512], f32)) for i in range(8)]
        free_banks = [(b, None) for b in banks]

        def take():
            return free_banks.pop(0)

        def give(b, *marks):
            free_banks.append((b, flat(marks)))

        ident = CST[:, C_ID:C_ID + 128]
        ones = CST[:, C_ONE:C_ONE + 128]
        tri = CST[:, C_TRI:C_TRI + 128]
        XV = X[:, :].rearrange("p (t n) -> p t n", t=2)
        HTV = HT[:, :].rearrange("p (k n) -> p k n", k=8)

        small_at = [0]

        def small(n):
            if small_at[0] + n > 448:
                small_at[0] = 0
            a = small_at[0]
            small_at[0] += n
            return SM[:, a:a + n]

        HALF = SM[:, 448:449]
        PW = SM[:, 449:481]

        one_sem = {}

        def load(name, out, in_, *waits, q=None):
            if name not in one_sem:
                one_sem[name] = [ctx.enter_context(nc.semaphore("s_" + name)), 0]
            one_sem[name][1] += 16
            (q or A).dma(out, in_, (one_sem[name][0], one_sem[name][1]), *waits)
            return (one_sem[name][0], one_sem[name][1])

        x_m = load("x", XV, x_d.rearrange("a (t p) n -> p (a t) n", p=128), q=S)
        cst_m = load("cst", CST[:, :], cst_d)
        load("small", VECS[:, :], vec_d)
        load("small", ROW[:, :], bass.AP(row_d.tensor, 0, [[0, 128], [1, ROWV]]))
        load("small", RW[:, :], rw_d)
        load("small", POSI[:, :], pos_d)
        load("small", PT[0:32, 0:384], one_d)
        load("small", PT[0:32, 384:392], rel_d)
        small_m = load("small", PT[0:8, 512:896], lnc_d)

        offset = [0]
        count = [0]

        def weights(s):
            n = slot_words(s)
            i = count[0] % NSLOT
            mark = (ring_sem[i], 16 * (count[0] // NSLOT + 1))
            S.dma(ring[i][:, 0:n], bass.AP(ws_d.tensor, offset[0], [[n, 128], [1, n]]), mark, ring_free[i])
            ring_free[i] = None
            offset[0] += 128 * n
            count[0] += 1

            def done(m):
                ring_free[i] = m
            return ring[i], mark, done

        pending = []

        def plan(slots):
            pending.extend(slots)

        def next_weights():
            return weights(pending.pop(0))

        alt = [0]

        def evac(out, in_, *waits, scale=None, eng=None):
            alt[0] += 1
            if eng is None:
                eng = A if alt[0] % 2 else V
            if eng is A:
                return A(lambda e: e.activation(out, in_, ACT.Copy, scale=1.0 if scale is None else scale), *waits)
            if scale is None:
                return V(lambda e: e.tensor_copy(out, in_), *waits)
            return V(lambda e: e.tensor_scalar(out, in_, scale, None, ALU.mult), *waits)

        def mm(out, l, r, st, sp, *waits, sig=False):
            return P(lambda e: e.matmul(out, l, r, start=st, stop=sp), *waits, sig=sig)

        def tr(out, in_, *waits, sig=False):
            return P(lambda e: e.transpose(out, in_, ident), *waits, sig=sig)

        zero = V(lambda e: e.memset(HALF, 0.0))
        zero = V(lambda e: e.memset(PW, -0.5), zero)

        def rpow(out, in_, *waits):
            n = in_.shape[1]
            return G(lambda e: e.tensor_tensor(out, in_, PW[:, 0:n], ALU.pow), zero, *waits)

        def rope_tables():
            F = small(2)
            m = V(lambda e: e.tensor_copy(F, POSI[:, :]), small_m)
            ang = TRIG[:, 0:64]
            for t in range(2):
                m2 = V(lambda e, t=t: e.tensor_scalar(TRIG[:, 32 * t:32 * t + 32], CST[:, C_INV:C_INV + 32],
                                                      F[:, t:t + 1], None, ALU.mult), m, cst_m)
            two_pi = 2 * math.pi
            parts = []
            rest = two_pi
            for _ in range(3):
                e2 = 2.0 ** (math.floor(math.log2(rest)) - 7)
                c = math.floor(rest / e2) * e2
                parts.append(c)
                rest -= c
            parts.append(rest)
            tabs = []
            for j, quarter in enumerate((0.0, 0.25)):
                K = LB[1][:, 64 * j:64 * j + 64]
                R = LB[1][:, 128 + 64 * j:192 + 64 * j]
                m = V(lambda e: e.tensor_scalar(K, ang, 1.0 / two_pi, quarter, ALU.mult, ALU.add), m2)
                m = V(lambda e: e.tensor_scalar(K, K, 12582912.0, None, ALU.add), m)
                m = V(lambda e: e.tensor_scalar(K, K, -12582912.0, None, ALU.add), m)
                src = ang
                for c in parts:
                    m = V(lambda e, c=c, src=src: e.scalar_tensor_tensor(R, K, -c, src, ALU.mult, ALU.add), m)
                    src = R
                if quarter:
                    m = V(lambda e: e.tensor_scalar(R, R, math.pi / 2, None, ALU.add), m)
                pi = 3.1415925
                m = V(lambda e: e.tensor_scalar(R, R, pi, -pi, ALU.min, ALU.max), m)
                dst = TRIG[:, 64 + 64 * j:128 + 64 * j]
                tabs.append(A(lambda e: e.activation(dst, R, ACT.Sin), m))
            return tabs

        trig_m = rope_tables()

        def distance_table():
            b, fr = take()
            m = mm(b[0:8, 0:384], PT[0:32, 384:392], PT[0:32, 0:384], True, True, small_m, fr, sig=True)
            m = V(lambda e: e.tensor_tensor(PT[0:8, 512:896], b[0:8, 0:384], PT[0:8, 512:896], ALU.add), m)
            give(b, m)
            return load("scr", scr, PT[0:8, 512:896], m)

        scr_m = distance_table()

        def flip(raw, j, n, after, add=None):
            ms = []
            for c in range(n // 512):
                b, fr = take()
                m = mm(b[:, :], j, raw[:, 512 * c:512 * c + 512], True, True, after, fr, cst_m, sig=True)
                o = BIAS[:, 512 * c:512 * c + 512]
                if add is None:
                    m = evac(o, b[:, :], m)
                else:
                    m = V(lambda e, o=o, b=b: e.tensor_tensor(
                        o.rearrange("p (a k) -> p a k", k=64), b[:, :].rearrange("p (a k) -> p a k", k=64),
                        add[:, None, :].to_broadcast([128, 8, 64]), ALU.add), m)
                give(b, m)
                ms.append(m)
            return ms

        def bias_one(l, *waits):
            m = None
            for s in range(2):
                for h in range(8):
                    m = load("bias", U[64 * s:64 * s + 64, 384 * h:384 * h + 384].rearrange("p (j k) -> p j k", j=6),
                             bass.AP(relb_d.tensor, ((l * 8 + h) * 15 + 5 - s) * 127, [[1, 64], [127, 6], [1, 64]]),
                             *waits)
            return flip(U, CST[:, C_JJ:C_JJ + 128], 3072, m, CST[:, C_MB:C_MB + 64])

        def bias_two(*waits):
            m = load("bias", U[:, 0:2048].rearrange("p (h k) -> p h k", h=8),
                     bass.AP(scr.tensor, 0, [[1, 128], [384, 8], [1, 256]]), scr_m, *waits)
            return flip(U, CST[:, C_J:C_J + 128], 2048, m)

        def to_features(src, dst, marks, scale=None):
            out = []
            for c2 in range(4):
                b, fr = take()
                for c in (2 * c2, 2 * c2 + 1):
                    for t in range(2):
                        m = tr(b[:, 256 * (c % 2) + 128 * t:256 * (c % 2) + 128 * t + 128],
                               src[:, t, 128 * c:128 * c + 128], marks, fr, cst_m, sig=(c % 2 and t))
                ms = []
                for c in (2 * c2, 2 * c2 + 1):
                    ms.append(evac(dst[:, c, :], b[:, 256 * (c % 2):256 * (c % 2) + 256], m, small_m,
                                   scale=None if scale is None else scale[:, c:c + 1], eng=(A, V)[c2 % 2]))
                give(b, ms)
                out += ms
            return out

        def rms_features(g, x_m):
            ss, ms, rs = small(2), small(2), small(2)
            m = []
            for t in range(2):
                m.append(A(lambda e, t=t: e.activation(LB[0][:, 1024 * t:1024 * t + 1024], XV[:, t, :], ACT.Square,
                                                       accum_out=ss[:, t:t + 1]), x_m))
            m = V(lambda e: e.tensor_scalar(ms, ss, 1.0 / 1024, EPS, ALU.mult, ALU.add), m)
            m = rpow(rs, ms, m)
            hv = LB[0][:, :].rearrange("p (t n) -> p t n", t=2)
            hm = [A(lambda e: e.activation(hv[:, 0, :], XV[:, 0, :], ACT.Copy, scale=rs[:, 0:1]), m),
                  V(lambda e: e.tensor_scalar(hv[:, 1, :], XV[:, 1, :], rs[:, 1:2], None, ALU.mult), m)]
            return to_features(hv, HTV, hm, scale=g)

        def by_tokens(lhs, marks, n, sink):
            slot, wm, done = next_weights()
            w = slot[:, 0:8 * n].rearrange("p (k n) -> p k n", k=8)
            bs = []
            for t in range(2):
                b, fr = take()
                for k in range(8):
                    m = mm(b[:, 0:n], lhs[:, k, 128 * t:128 * t + 128], w[:, k, :], k == 0, k == 7,
                           wm, marks[k], fr, sig=(k == 7))
                bs.append((t, b, m))
            done(m)
            for t, b, m in bs:
                give(b, sink(t, b, m))

        def by_features(rhs, marks, kt, parts, width, sink):
            slot, wm, done = next_weights()
            w = slot[:, 0:kt * parts * width].rearrange("p (k a n) -> p k a n", k=kt, a=parts)
            if parts == 1:
                for c2 in range(width // 256):
                    b, fr = take()
                    for c in (2 * c2, 2 * c2 + 1):
                        for k in range(kt):
                            m = mm(b[:, 256 * (c % 2):256 * (c % 2) + 256], w[:, k, 0, 128 * c:128 * c + 128],
                                   rhs[0][:, k, :], k == 0, k == kt - 1, wm, marks[0][k], fr,
                                   sig=(k == kt - 1 and c % 2 == 1))
                    if c2 == width // 256 - 1:
                        done(m)
                    give(b, sink(c2, b, m))
                return
            for c in range(width // 128):
                b, fr = take()
                for a in range(2):
                    for k in range(kt):
                        m = mm(b[:, 256 * a:256 * a + 256], w[:, k, a, 128 * c:128 * c + 128], rhs[a][:, k, :],
                               k == 0, k == kt - 1, wm, marks[a][k], fr, sig=(k == kt - 1 and a == 1))
                if c == width // 128 - 1:
                    done(m)
                give(b, sink(c, b, m))

        def down(src, marks, kts, sink):
            held = [[take() for _ in range(2)] for _ in range(2)]
            k = 0
            while k < kts:
                slot, wm, done = next_weights()
                n = min(4, kts - k)
                w = slot[:, 0:n * 1024].rearrange("p (k n) -> p k n", k=n)
                for i in range(n):
                    for t in range(2):
                        for h in range(2):
                            b, fr = held[t][h]
                            last = k + i == kts - 1
                            m = mm(b[:, :], src[:, k + i, 128 * t:128 * t + 128], w[:, i, 512 * h:512 * h + 512],
                                   k + i == 0, last, wm, marks[k + i], fr, sig=(last or (i == n - 1 and t and h)))
                            if last:
                                give(b, sink(t, h, b, m))
                done(m)
                k += n

        tm_free = [None] * 4

        def swiglu(lhs, marks, slots, dst):
            out = []
            for j in range(slots):
                def sink(c, b, m, j=j):
                    f = 2 * j + c
                    T = LB[1][:, 256 * (f % 4):256 * (f % 4) + 256]
                    M = LB[1][:, 1024 + 256 * (f % 4):1280 + 256 * (f % 4)]
                    m1 = A(lambda e: e.activation(T, b[:, 0:256], ACT.Tanh, scale=0.5), m, tm_free[f % 4])
                    m2 = V(lambda e: e.scalar_tensor_tensor(M, T, 1.0, b[:, 0:256], ALU.add, ALU.mult), m1,
                           tm_free[f % 4])
                    m3 = V(lambda e: e.tensor_tensor(dst[:, f, :], M, b[:, 256:512], ALU.mult), m2)
                    tm_free[f % 4] = m3
                    out.append(m3)
                    return m3
                by_features([lhs, lhs], [marks, marks], 8, 2, 256, sink)
            return out

        def add_to_x(x_marks, scale=0.5, alpha=None):
            new = []
            pre = x_marks
            if alpha is not None:
                pre = [V(lambda e: e.tensor_scalar(X[:, :], X[:, :], alpha, None, ALU.mult), x_marks)]

            def sink(t, h, b, m):
                o = XV[:, t, 512 * h:512 * h + 512]
                m = V(lambda e: e.scalar_tensor_tensor(o, b[:, :], scale, o, ALU.mult, ALU.add), m, pre)
                new.append(m)
                return m
            return sink, new

        def gates(lhs, marks, bias=None):
            for j in range(4):
                def sink(c, b, m, j=j):
                    f = 2 * j + c
                    if bias is None:
                        return A(lambda e: e.activation(GT[:, 512 * f:512 * f + 512], b[:, :], ACT.Tanh, scale=0.5), m)
                    for a in range(2):
                        r = A(lambda e, a=a: e.activation(GT[:, 512 * f + 256 * a:512 * f + 256 * a + 256],
                                                          b[:, 256 * a:256 * a + 256], ACT.Tanh, scale=0.5,
                                                          bias=bias[:, 8 * a + f:8 * a + f + 1]), m, bias_m)
                    return r
                by_features([lhs, lhs], [marks, marks], 8, 2, 256, sink)
                yield

        def mix(oa, ob, ma, mb, gt_m):
            out = []
            for j in range(2):
                def sink(c, b, m, j=j):
                    f = 4 * j + c
                    g = GT[:, 512 * f:512 * f + 512]
                    m = V(lambda e: e.scalar_tensor_tensor(g, g, 1.0, b[:, :], ALU.add, ALU.mult), m, gt_m)
                    r = V(lambda e: e.tensor_tensor(g[:, 0:256], g[:, 0:256], g[:, 256:512], ALU.add), m)
                    out.append(r)
                    return m
                by_features([oa, ob], [ma, mb], 4, 2, 512, sink)
            return out

        pt_free = [None]

        def transpose_p(src, heads, kts, m_src):
            marks = []
            blocks = [(h, i) for h in range(heads) for i in range(kts)]
            for c in range(0, len(blocks), 4):
                b, fr = take()
                part = blocks[c:c + 4]
                for n, (h, i) in enumerate(part):
                    m = tr(b[:, 128 * n:128 * n + 128], src(h, i), m_src[h], fr, cst_m, sig=(n == len(part) - 1))
                n = 128 * len(part)
                m = evac(PT[:, 128 * c:128 * c + n], b[:, 0:n], m, pt_free[0])
                give(b, m)
                marks += [m] * len(part)
            return marks

        def attention(q, k, v, bias, kts_of, q_m, k_m, v_m, sinks=None, l_free=None):
            state = {}

            def scores(t):
                kts = kts_of(t)
                n = 128 * kts
                L = LB[t]
                mx, nm, su = small(8), small(8), small(8)
                ms = []
                for h2 in range(4):
                    b, fr = take()
                    h0 = 4 * (h2 // 2) + h2 % 2
                    for i in range(2):
                        h = h0 + 2 * i
                        m = mm(b[:, 256 * i:256 * i + n], q(h, t), k(h)[:, 0:n], True, True,
                               q_m, k_m, fr, sig=(i == 1))
                    for i in range(2):
                        h = h0 + 2 * i
                        m = V(lambda e, h=h, b=b: e.tensor_tensor_reduce(
                            L[:, 256 * h:256 * h + n], b[:, 256 * i:256 * i + n], bias(h, t), 1.0,
                            NEG if sinks is None else sinks[:, h:h + 1], ALU.add, ALU.max, mx[:, h:h + 1]),
                            m, bias_marks, small_m)
                    give(b, m)
                m = V(lambda e: e.tensor_scalar(nm, mx, -1.0, None, ALU.mult), m)
                for h in range(8):
                    ms.append(A(lambda e, h=h: e.activation(L[:, 256 * h:256 * h + n], L[:, 256 * h:256 * h + n],
                                                            ACT.Exp, bias=nm[:, h:h + 1],
                                                            accum_out=su[:, h:h + 1]), m))
                last = ms[-1]
                if sinks is not None:
                    es = small(8)
                    m = V(lambda e: e.tensor_tensor(es, sinks, nm, ALU.add), m, small_m)
                    m = A(lambda e: e.activation(es, es, ACT.Exp), m)
                    last = V(lambda e: e.tensor_tensor(su, su, es, ALU.add), m, last)
                rs = small(8)
                last = V(lambda e: e.reciprocal(rs, su), last)
                state[t] = (ms, rs, last, kts)

            def values(t, dst):
                ms, rs, rm, kts = state[t]
                L = LB[t]
                pm = transpose_p(lambda h, i: L[:, 256 * h + 128 * i:256 * h + 128 * i + 128], 8, kts, ms)
                b, fr = take()
                for h in range(8):
                    for i in range(kts):
                        m = mm(b[:, 64 * h:64 * h + 64], PT[:, 128 * (h * kts + i):128 * (h * kts + i) + 128],
                               v(h, i), i == 0, i == kts - 1, pm[h * kts + i], v_m, fr,
                               sig=(h == 7 and i == kts - 1))
                pt_free[0] = m
                o = O[:, 512 * t:512 * t + 512]
                m = V(lambda e: e.tensor_tensor(o.rearrange("p (h d) -> p h d", h=8),
                                                b[:, :].rearrange("p (h d) -> p h d", h=8),
                                                rs[:, :, None].to_broadcast([128, 8, 64]), ALU.mult), m, rm)
                give(b, m)
                b, fr = take()
                for c in range(4):
                    m2 = tr(b[:, 128 * c:128 * c + 128], o[:, 128 * c:128 * c + 128], m, fr, sig=(c == 3))
                m2 = evac(dst[:, :, 128 * t:128 * t + 128], b[:, :].rearrange("p (c n) -> p c n", c=4), m2)
                give(b, m2)
                return m2
            return scores, values

        for i in (0, 2):
            c = VECS[:, VEC["qk_b"] + i:VEC["qk_b"] + i + 1]
            qkb_m = G(lambda e: e.tensor_scalar(c, c, 0.125, None, ALU.mult), small_m)
        for l in range(2):
            plan(layer_one_slots(l))
            bias_marks = bias_one(l, x_m if l else None)
            h_m = rms_features(VECS[:, VEC["attn_g"] + 8 * l:VEC["attn_g"] + 8 * l + 8], x_m)
            QA = [U[:, 768 * t:768 * t + 768] for t in range(2)]
            QB = [U[:, 1536 + 1536 * t:3072 + 1536 * t] for t in range(2)]
            free_m = bias_marks

            got = {}

            def keep(key, dst):
                def sink(t, b, m):
                    n = dst(t).shape[1]
                    got[key, t] = evac(dst(t), b[:, 0:n], m, free_m)
                    return got[key, t]
                return sink

            by_tokens(HTV, h_m, 512, keep("qa", lambda t: QA[t][:, 0:512]))
            by_tokens(HTV, h_m, 256, keep("kva", lambda t: QA[t][:, 512:768]))
            by_tokens(HTV, h_m, 512, keep("qb", lambda t: QB[t][:, 0:512]))
            by_tokens(HTV, h_m, 512, keep("kb", lambda t: QB[t][:, 512:1024]))
            by_tokens(HTV, h_m, 512, keep("vb", lambda t: QB[t][:, 1024:1536]))
            gate_steps = gates(HTV, h_m)

            rt_m = []
            for t in range(2):
                sn = TRIG[:, 64 + 32 * t:96 + 32 * t]
                co = TRIG[:, 128 + 32 * t:160 + 32 * t]
                for w in range(2):
                    g = ROW[:, 128 * l + 64 * w:128 * l + 64 * w + 64]
                    base = 256 * t + 128 * w
                    for hf in range(2):
                        a = base + 32 * hf
                        rt_m.append(G(lambda e, a=a, co=co, g=g, hf=hf: e.tensor_tensor(
                            CS[:, a:a + 32], co, g[:, 32 * hf:32 * hf + 32], ALU.mult), trig_m, small_m, x_m))
                        a = base + 64 + 32 * hf
                        m = G(lambda e, a=a, sn=sn, g=g, hf=hf: e.tensor_tensor(
                            CS[:, a:a + 32], sn, g[:, 32 - 32 * hf:64 - 32 * hf], ALU.mult), trig_m, small_m, x_m)
                        if hf == 0:
                            m = G(lambda e, a=a: e.tensor_scalar(CS[:, a:a + 32], CS[:, a:a + 32], -1.0, None,
                                                                 ALU.mult), m)
                        rt_m.append(m)

            def norm(view, heads, marks):
                sq = PT[:, 0:64 * heads]
                ss, ms, rs = small(heads), small(heads), small(heads)
                m = A(lambda e: e.activation(sq, view, ACT.Square), marks, pt_free[0])
                m = V(lambda e: e.tensor_reduce(ss, sq.rearrange("p (h d) -> p h d", h=heads), AX.X, ALU.add), m)
                pt_free[0] = [pt_free[0], m]
                m = V(lambda e: e.tensor_scalar(ms, ss, 1.0 / 64, EPS, ALU.mult, ALU.add), m)
                m = rpow(rs, ms, m)
                vv = view.rearrange("p (h d) -> p h d", h=heads)
                return V(lambda e: e.tensor_tensor(vv, vv, rs[:, :, None].to_broadcast([128, heads, 64]),
                                                   ALU.mult), m)

            KD = LB[0]
            qa_m, ka_m = [], []
            for t in range(2):
                m = norm(QA[t][:, 0:640], 10, [got["qa", t], got["kva", t]])
                tmp = LB[1][:, 0:640]
                tmp2 = LB[1][:, 640:1280]
                r = [m, qa_m, ka_m]
                for w, (h0, h1) in enumerate(((0, 8), (8, 10))):
                    n = h1 - h0
                    xq = QA[t][:, 64 * h0:64 * h1].rearrange("p (h d) -> p h d", h=n)
                    t1 = tmp[:, 64 * h0:64 * h1].rearrange("p (h d) -> p h d", h=n)
                    t2 = tmp2[:, 64 * h0:64 * h1].rearrange("p (h d) -> p h d", h=n)
                    cg = CS[:, 256 * t + 128 * w:256 * t + 128 * w + 64]
                    sg = CS[:, 256 * t + 128 * w + 64:256 * t + 128 * w + 128]
                    ms = [V(lambda e, t1=t1, xq=xq, cg=cg, n=n: e.tensor_tensor(
                        t1, xq, cg[:, None, :].to_broadcast([128, n, 64]), ALU.mult), r, rt_m)]
                    for hf in range(2):
                        ms.append(G(lambda e, t2=t2, xq=xq, sg=sg, n=n, hf=hf: e.tensor_tensor(
                            t2[:, :, 32 * hf:32 * hf + 32], xq[:, :, 32 - 32 * hf:64 - 32 * hf],
                            sg[:, None, 32 * hf:32 * hf + 32].to_broadcast([128, n, 32]), ALU.mult), r, rt_m))
                    if w == 0:
                        qa_m.append(V(lambda e, xq=xq, t1=t1, t2=t2: e.tensor_tensor(xq, t1, t2, ALU.add), ms))
                    else:
                        for d in range(2):
                            o = KD[:, 256 * t:256 * t + 256].rearrange("p (g d n) -> p g d n", g=2, d=2)[:, :, d, :]
                            ka_m.append(V(lambda e, o=o, t1=t1, t2=t2: e.tensor_tensor(o, t1, t2, ALU.add), ms, h_m))
            next(gate_steps)
            qb_m = []
            for t in range(2):
                qb_m.append(norm(QB[t][:, 0:1024], 16, [got["qb", t], got["kb", t]]))
            next(gate_steps)

            def fold(dst, srcs, marks, scale):
                out = []
                n = srcs[0].shape[1] // 128
                for c2 in range(n // 2):
                    b, fr = take()
                    for c in (2 * c2, 2 * c2 + 1):
                        for t in range(2):
                            m = tr(b[:, 256 * (c % 2) + 128 * t:256 * (c % 2) + 128 * t + 128],
                                   srcs[t][:, 128 * c:128 * c + 128], marks, fr, sig=(c % 2 and t))
                    m = evac(dst[:, 512 * c2:512 * c2 + 512], b[:, :], m, scale=scale)
                    give(b, m)
                    out.append(m)
                return out

            qta = fold(QT[:, 0:1024], [QA[t][:, 0:512] for t in range(2)], qa_m, 0.125)
            kta = fold(QT[:, 1024:1536], [KD[:, 256 * t:256 * t + 256] for t in range(2)], ka_m, None)
            qkb = VECS[:, VEC["qk_b"] + 2 * l:VEC["qk_b"] + 2 * l + 2]
            qtb = fold(QT[:, 1536:2560], [QB[t][:, 0:512] for t in range(2)], qb_m + [qkb_m], qkb[:, 0:1])
            ktb = fold(QT[:, 2560:3584], [QB[t][:, 512:1024] for t in range(2)], qb_m, qkb[:, 1:2])

            def qa_of(h, t):
                return QT[64 * (h % 2):64 * (h % 2) + 64, 256 * (h // 2) + 128 * t:256 * (h // 2) + 128 * t + 128]

            def ka_of(h):
                return QT[64 * (h % 2):64 * (h % 2) + 64, 1024 + 256 * (h // 4):1280 + 256 * (h // 4)]

            def qb_of(h, t):
                a = 1536 + 256 * (h // 2) + 128 * t
                return QT[64 * (h % 2):64 * (h % 2) + 64, a:a + 128]

            def kb_of(h):
                a = 2560 + 256 * (h // 2)
                return QT[64 * (h % 2):64 * (h % 2) + 64, a:a + 256]

            sc_a, va_a = attention(qa_of, ka_of, lambda h, i: QA[i][:, 640 + 64 * (h // 4):704 + 64 * (h // 4)],
                                   lambda h, t: CST[:, C_MA + 256 * t:C_MA + 256 * t + 256], lambda t: 2,
                                   qta, kta, [got["kva", 0], got["kva", 1]],
                                   sinks=ROW[:, 256 + 8 * l:264 + 8 * l])
            BV = BIAS[:, :].rearrange("p (h j k) -> p h j k", h=8, j=6)
            sc_b, va_b = attention(qb_of, kb_of, lambda h, i: QB[i][:, 1024 + 64 * h:1088 + 64 * h],
                                   lambda h, t: BIAS[:, 384 * h + 128 - 128 * t:384 * h + 384 - 128 * t],
                                   lambda t: 2, qtb, ktb, [got["vb", 0], got["vb", 1]])
            sc_a(0)
            next(gate_steps)
            sc_a(1)
            for _ in gate_steps:
                pass
            gt_m = (A.sem, A.n)
            oa = HT[:, 0:1024].rearrange("p (c n) -> p c n", c=4)
            ob = HT[:, 1024:2048].rearrange("p (c n) -> p c n", c=4)
            oam = [va_a(0, oa)]
            sc_b(0)
            oam.append(va_a(1, oa))
            sc_b(1)
            obm = [va_b(0, ob), va_b(1, ob)]
            mm_ = mix(oa, ob, [oam] * 4, [obm] * 4, gt_m)
            sink, new = add_to_x([x_m])
            down(GT[:, :].rearrange("p (c n) -> p c n", c=8), mm_, 8, sink)
            x_m = new
            h_m = rms_features(VECS[:, VEC["ffn_g"] + 8 * l:VEC["ffn_g"] + 8 * l + 8], x_m)
            UV = U[:, :].rearrange("p (f n) -> p f n", f=28)
            u_m = swiglu(HTV, h_m, 11, UV)
            sink, new = add_to_x(x_m)
            down(UV, u_m, 22, sink)
            x_m = new

        def layer_norm(l, i, x_marks):
            gb = load("ln", PT[:, :], bass.AP(ln_d.tensor, (2 * l + i) * 2048, [[0, 128], [1, 2048]]),
                      x_marks, pt_free[0])
            out = []
            for t in range(2):
                st, ag, ve, rs = small(12), small(2), small(1), small(1)
                for h in range(2):
                    m = V(lambda e, h=h, t=t: e.bn_stats(st[:, 6 * h:6 * h + 6], XV[:, t, 512 * h:512 * h + 512]),
                          x_marks)
                m = V(lambda e: e.bn_aggr(ag, st), m)
                m = V(lambda e: e.tensor_scalar(ve, ag[:, 1:2], LN_EPS, None, ALU.add), m)
                m = rpow(rs, ve, m)
                xt = XV[:, t, :]
                m = V(lambda e: e.tensor_scalar(xt, xt, ag[:, 0:1], rs[:, 0:1], ALU.subtract, ALU.mult), m)
                m = V(lambda e: e.tensor_tensor(xt, xt, PT[:, 0:1024], ALU.mult), m, gb)
                m = V(lambda e: e.tensor_tensor(xt, xt, PT[:, 1024:2048], ALU.add), m)
                out.append(m)
            pt_free[0] = out
            return out

        HB = small(0)
        bg_m = G(lambda e: e.tensor_scalar(VECS[:, VEC["b_gate"]:VEC["b_gate"] + 32],
                                           VECS[:, VEC["b_gate"]:VEC["b_gate"] + 32], 0.5, None, ALU.mult), small_m)
        bias_m = bg_m
        bias_marks = bias_two(x_m)
        for l in range(2):
            plan(layer_two_slots(l))
            x_f = to_features(XV, HTV, x_m)
            R = [U[:, 1024 * i:1024 * i + 1024] for i in range(7)]
            XM, XC, ZT, QM, KM, VM, VT = R

            def pairs(dst, out, scale=None, wait=None):
                def sink(c, b, m):
                    m = evac(dst[:, 512 * c:512 * c + 512], b[:, :], m, wait, scale=scale)
                    out.append(m)
                    return m
                return sink
            q_m, k_m, v_m, xm_m, z_m = [], [], [], [], []
            by_features([HTV], [x_f], 8, 1, 512, pairs(QT[:, 0:1024], q_m, 0.125))
            by_features([HTV], [x_f], 8, 1, 512, pairs(QT[:, 1024:2048], k_m))

            def vsink(t, b, m):
                m = evac(QT[:, 2048 + 512 * t:2560 + 512 * t], b[:, :], m)
                v_m.append(m)
                return m
            by_tokens(HTV, x_f, 512, vsink)
            sc, va = attention(
                lambda h, t: QT[64 * (h % 2):64 * (h % 2) + 64,
                                256 * (h // 2) + 128 * t:256 * (h // 2) + 128 * t + 128],
                lambda h: QT[64 * (h % 2):64 * (h % 2) + 64, 1024 + 256 * (h // 2):1280 + 256 * (h // 2)],
                lambda h, i: QT[:, 2048 + 512 * i + 64 * h:2112 + 512 * i + 64 * h],
                lambda h, t: BIAS[:, 256 * h + 128 * (1 - t):256 * h + 256], lambda t: t + 1, q_m, k_m, v_m)
            sc(0)
            by_features([HTV], [x_f], 8, 1, 512, pairs(XM, xm_m, wait=bias_marks))

            def zsink(c, b, m):
                z = ZT[:, 512 * c:512 * c + 512]
                m = A(lambda e: e.activation(z, b[:, :], ACT.Tanh, scale=0.5), m, bias_marks)
                z_m.append(V(lambda e: e.tensor_scalar(z, z, 1.0, 0.5, ALU.add, ALU.mult), m))
                return m
            by_features([HTV], [x_f], 8, 1, 512, zsink)
            sc(1)
            gate_steps = gates(HTV, x_f, VECS[:, VEC["b_gate"] + 16 * l:VEC["b_gate"] + 16 * l + 16])
            xc_m = []
            for h in range(4):
                c = XC[:, 256 * h:256 * h + 256]
                xm = XM[:, 256 * h:256 * h + 256]

                def cw(j, h=h):
                    a = VEC["conv_w"] + 16 * l + 4 * j + h
                    return VECS[:, a:a + 1]
                cb = VECS[:, VEC["conv_b"] + 4 * l + h:VEC["conv_b"] + 4 * l + h + 1]
                m = V(lambda e, c=c, xm=xm, cw=cw, cb=cb: e.tensor_scalar(c, xm, cw(3), cb, ALU.mult, ALU.add),
                      xm_m, small_m)
                for d in (1, 2, 3):
                    m = V(lambda e, c=c, xm=xm, cw=cw, d=d: e.scalar_tensor_tensor(
                        c[:, d:256], xm[:, 0:256 - d], cw(3 - d), c[:, d:256], ALU.mult, ALU.add), m)
                tt = KM[:, 256 * h:256 * h + 256]
                m1 = A(lambda e, c=c, tt=tt: e.activation(tt, c, ACT.Tanh, scale=0.5), m)
                xc_m.append(V(lambda e, c=c, tt=tt: e.scalar_tensor_tensor(c, tt, 1.0, c, ALU.add, ALU.mult), m1))
            next(gate_steps)
            next(gate_steps)
            next(gate_steps)
            next(gate_steps)
            gt_m = (A.sem, A.n)
            oa = HT[:, 0:1024].rearrange("p (c n) -> p c n", c=4)
            ob = HT[:, 1024:2048].rearrange("p (c n) -> p c n", c=4)
            oam = [va(0, oa)]

            slot, wm, done = next_weights()
            wqk = slot[:, 0:1024].rearrange("p (a n) -> p a n", a=8)
            wv = slot[:, 1024:1536].rearrange("p (a n) -> p a n", a=4)
            wif = slot[:, 1536:1632].rearrange("p (a n) -> p a n", a=12)
            got = {}
            for key, w0, src, dst, scale, ms in (("q", 0, XC, QM, 0.5, xc_m), ("k", 4, XC, KM, 0.5, xc_m),
                                                 ("v", None, XM, VM, None, xm_m)):
                for h2 in range(2):
                    b, fr = take()
                    for h in (2 * h2, 2 * h2 + 1):
                        w = wv[:, h, :] if w0 is None else wqk[:, w0 + h, :]
                        m = mm(b[:, 256 * (h % 2):256 * (h % 2) + 256], w, src[:, 256 * h:256 * h + 256],
                               True, True, wm, ms, fr, sig=(h % 2 == 1))
                    m = evac(dst[:, 512 * h2:512 * h2 + 512], b[:, :], m, scale=scale)
                    give(b, m)
                    got.setdefault(key, []).append(m)
            vt_m = []
            for t in range(2):
                b, fr = take()
                for h in range(4):
                    m = mm(b[:, 128 * h:128 * h + 128], XM[:, 256 * h + 128 * t:256 * h + 128 * t + 128],
                           wv[:, h, :], True, True, wm, xm_m, fr, sig=(h == 3))
                m = evac(VT[:, 512 * t:512 * t + 512], b[:, :], m)
                give(b, m)
                vt_m.append(m)
            IF = SM[:, 484:500].rearrange("p (t n) -> p t n", t=2)
            FL = small(8).rearrange("p (t n) -> p t n", t=2)
            ab, lg = small(8), small(8)
            b, fr = take()
            for t in range(2):
                n = 0
                for key, src in (("q", QM), ("k", KM), ("v", VM)):
                    for h in range(4):
                        m = mm(b[:, 8 * t:8 * t + 8], src[:, 256 * h + 128 * t:256 * h + 128 * t + 128],
                               wif[:, n, :], n == 0, n == 11, got[key], fr, wm, sig=(n == 11 and t == 1))
                        n += 1
            done(m)
            m = V(lambda e, b=b: e.tensor_tensor(IF, b[:, 0:16].rearrange("p (t n) -> p t n", t=2),
                                            ROW[:, None, 272 + 8 * l:280 + 8 * l].to_broadcast([128, 2, 8]),
                                            ALU.add), m)
            give(b, m)
            fp = IF[:, :, 4:8]
            abv = ab.rearrange("p (t n) -> p t n", t=2)
            m1 = V(lambda e: e.scalar_tensor_tensor(abv, fp, -1.0, fp, ALU.mult, ALU.max), m)
            m1 = A(lambda e: e.activation(ab, ab, ACT.Exp, scale=-1.0), m1)
            m1 = A(lambda e: e.activation(lg, ab, ACT.Ln, bias=1.0), m1)
            if_m = V(lambda e: e.scalar_tensor_tensor(FL, fp, 0.0, lg.rearrange("p (t n) -> p t n", t=2),
                                                      ALU.min, ALU.subtract), m1)
            FN = small(8).rearrange("p (t n) -> p t n", t=2)
            fn_m = V(lambda e: e.tensor_scalar(FN, FL, -1.0, None, ALU.mult), if_m)
            oam.append(va(1, oa))
            b, fr = take()
            m = mm(b[:, 0:4], tri, FL[:, 0, :], True, True, if_m, fr)
            m = mm(b[:, 4:8], ones, FL[:, 0, :], True, False)
            m = mm(b[:, 4:8], tri, FL[:, 1, :], False, True, sig=True)
            BC = SM[:, 500:508]
            bc_m = V(lambda e, b=b: e.tensor_copy(BC, b[:, 0:8]), m)
            give(b, bc_m)
            rows = []
            for h2 in range(2):
                b, fr = take()
                for h in (2 * h2, 2 * h2 + 1):
                    o = 256 * (h % 2)

                    def bc(v, t, c):
                        return v[:, t, c:c + 1].to_broadcast([128, 128])
                    mm(b[:, o:o + 128], bc(IF, 0, h), ident, True, False, fn_m, fr)
                    mm(b[:, o:o + 128], bc(FN, 0, h), tri, False, True)
                    mm(b[:, o + 128:o + 256], bc(IF, 1, h), ident, True, False)
                    mm(b[:, o + 128:o + 256], bc(FN, 0, h), ones, False, False)
                    m = mm(b[:, o + 128:o + 256], bc(FN, 1, h), tri, False, True, sig=(h % 2 == 1))
                rows.append((b, m))
            mst = {}
            for t in range(2):
                n = 128 * (t + 1)
                mx, nm = small(4), small(4)
                L = LB[t]
                for h in range(4):
                    b, rm = rows[h // 2]
                    m = V(lambda e, h=h, b=b: e.tensor_tensor_reduce(
                        L[:, 256 * h:256 * h + n], b[:, 256 * (h % 2):256 * (h % 2) + n],
                        CST[:, C_CAUS + 256 - n:C_CAUS + 256], 1.0, 0.0, ALU.add, ALU.max, mx[:, h:h + 1]),
                        rm, oam)
                    if t == 1 and h % 2:
                        give(b, m)
                m = V(lambda e: e.tensor_scalar(nm, mx, -1.0, None, ALU.mult), m)
                em = []
                for h in range(4):
                    em.append(A(lambda e, h=h: e.activation(L[:, 256 * h:256 * h + n], L[:, 256 * h:256 * h + n],
                                                            ACT.Exp, bias=nm[:, h:h + 1]), m))
                gd = small(4)
                m = V(lambda e, t=t: e.tensor_tensor(gd, nm, BC[:, 4 * t:4 * t + 4], ALU.subtract), m, bc_m)
                gd_m = A(lambda e: e.activation(gd, gd, ACT.Exp), m)
                nq = small(4)
                pm = []
                for h2 in range(2):
                    b, fr = take()
                    for h in (2 * h2, 2 * h2 + 1):
                        o = 256 * (h % 2)
                        m = mm(b[:, o:o + n], QM[:, 256 * h + 128 * t:256 * h + 128 * t + 128],
                               KM[:, 256 * h:256 * h + n], True, True, fr, sig=(h % 2 == 1))
                    for h in (2 * h2, 2 * h2 + 1):
                        o = 256 * (h % 2)
                        m = V(lambda e, h=h, b=b, o=o: e.scalar_tensor_tensor(
                            L[:, 256 * h:256 * h + n], b[:, o:o + n], 128 ** -0.5, L[:, 256 * h:256 * h + n],
                            ALU.mult, ALU.mult, accum_out=nq[:, h:h + 1]), m, em[h])
                        pm.append(m)
                    give(b, m)
                m = V(lambda e: e.scalar_tensor_tensor(nq, nq, -1.0, nq, ALU.mult, ALU.max), m)
                m = V(lambda e: e.tensor_tensor(nq, nq, gd, ALU.max), m, gd_m)
                rq = small(4)
                m = V(lambda e: e.reciprocal(rq, nq), m)
                mst[t] = (pm, rq, m)
            obm = []
            for t in range(2):
                pm, rq, rqm = mst[t]
                L = LB[t]
                kts = t + 1
                tm = transpose_p(lambda h, i: L[:, 256 * h + 128 * i:256 * h + 128 * i + 128], 4, kts, pm)
                b, fr = take()
                for h in range(4):
                    for i in range(kts):
                        m = mm(b[:, 128 * h:128 * h + 128], PT[:, 128 * (h * kts + i):128 * (h * kts + i) + 128],
                               VT[:, 512 * i + 128 * h:512 * i + 128 * h + 128], i == 0, i == kts - 1,
                               tm[h * kts + i], vt_m, fr, sig=(h == 3 and i == kts - 1))
                pt_free[0] = m
                o = O[:, 512 * t:512 * t + 512]
                ov = o.rearrange("p (h d) -> p h d", h=4)
                m = V(lambda e, ov=ov, b=b, rq=rq: e.tensor_tensor(
                    ov, b[:, :].rearrange("p (h d) -> p h d", h=4),
                    rq[:, :, None].to_broadcast([128, 4, 128]), ALU.mult), m, rqm, oam)
                give(b, m)
                st, ag, ve, rs = small(24), small(8), small(4), small(4)
                for h in range(4):
                    m2 = V(lambda e, h=h: e.bn_stats(st[:, 6 * h:6 * h + 6], o[:, 128 * h:128 * h + 128]), m)
                for h in range(4):
                    m3 = V(lambda e, h=h: e.bn_aggr(ag[:, 2 * h:2 * h + 2], st[:, 6 * h:6 * h + 6]), m2)
                m4 = V(lambda e: e.tensor_scalar(ve, ag.rearrange("p (h a) -> p h a", a=2)[:, :, 1], LN_EPS, None,
                                                 ALU.add), m3)
                m4 = rpow(rs, ve, m4)
                for h in range(4):
                    m = V(lambda e, h=h: e.tensor_scalar(o[:, 128 * h:128 * h + 128], o[:, 128 * h:128 * h + 128],
                                                         ag[:, 2 * h:2 * h + 1], rs[:, h:h + 1],
                                                         ALU.subtract, ALU.mult), m4)
                b, fr = take()
                for c in range(4):
                    m2 = tr(b[:, 128 * c:128 * c + 128], o[:, 128 * c:128 * c + 128], m, fr, sig=(c == 3))
                for h in range(4):
                    g = VECS[:, VEC["m_g"] + 4 * l + h:VEC["m_g"] + 4 * l + h + 1]
                    m = V(lambda e, h=h, g=g, b=b, t=t: e.scalar_tensor_tensor(
                        ob[:, h, 128 * t:128 * t + 128], b[:, 128 * h:128 * h + 128], g,
                        ZT[:, 256 * h + 128 * t:256 * h + 128 * t + 128], ALU.mult, ALU.mult), m2, z_m)
                give(b, m)
                obm.append(m)

            mm_ = mix(oa, ob, [oam] * 4, [obm] * 4, gt_m)
            sink, new = add_to_x(x_m, alpha=ALPHA)
            down(GT[:, :].rearrange("p (c n) -> p c n", c=8), mm_, 8, sink)
            x_m = layer_norm(l, 0, new)
            x_f = to_features(XV, HTV, x_m)
            UV = U[:, :].rearrange("p (f n) -> p f n", f=28)
            if l == 0:
                u_m = swiglu(HTV, x_f, 11, UV)
                sink, new = add_to_x([x_m, x_f], alpha=ALPHA)
                down(UV, u_m, 22, sink)
                x_m = new
            else:
                gw = SM[:, 484:500]
                gm = []
                for t in range(2):
                    b, fr = take()
                    for k in range(8):
                        m = mm(b[:, 0:8], HTV[:, k, 128 * t:128 * t + 128], RW[:, 8 * k:8 * k + 8], k == 0, k == 7,
                               x_f[k], fr, sig=(k == 7))
                    lo, s1, f1, s2, tmp = small(8), small(8), small(8), small(8), small(8)
                    v1, v2, d, a1, a2, i1 = (small(1) for _ in range(6))
                    io = CST[:, C_IOTA:C_IOTA + 8]
                    m = V(lambda e, b=b: e.tensor_tensor(lo, b[:, 0:8], ROW[:, 288:296], ALU.add), m)
                    give(b, m)

                    def first_of(src, val, sel, m):
                        m = V(lambda e: e.tensor_reduce(val, src, AX.X, ALU.max), m)
                        m = V(lambda e: e.scalar_tensor_tensor(tmp, src, val[:, 0:1], io, ALU.is_equal, ALU.mult), m)
                        m = V(lambda e: e.tensor_reduce(i1, tmp, AX.X, ALU.max), m)
                        return V(lambda e: e.tensor_scalar(sel, io, i1[:, 0:1], None, ALU.is_equal), m)
                    m = first_of(lo, v1, s1, m)
                    m = V(lambda e: e.scalar_tensor_tensor(f1, s1, -3e38, lo, ALU.mult, ALU.add), m)
                    m = first_of(f1, v2, s2, m)
                    m = V(lambda e: e.tensor_tensor(d, v2, v1, ALU.subtract), m)
                    m = A(lambda e: e.activation(d, d, ACT.Exp), m)
                    m = V(lambda e: e.tensor_scalar(a1, d, 2.0, 2.0, ALU.mult, ALU.add), m)
                    m = V(lambda e: e.reciprocal(a1, a1), m)
                    m = V(lambda e: e.tensor_tensor(a2, a1, d, ALU.mult), m)
                    m = V(lambda e: e.tensor_scalar(s1, s1, a1[:, 0:1], None, ALU.mult), m)
                    m = V(lambda e, t=t: e.scalar_tensor_tensor(gw[:, 8 * t:8 * t + 8], s2, a2[:, 0:1], s1,
                                                                ALU.mult, ALU.add), m)
                    gm.append(m)
                pre = V(lambda e: e.tensor_scalar(X[:, :], X[:, :], ALPHA, None, ALU.mult), x_m, x_f)
                x_m = [pre]
                for ex in range(8):
                    u_m = swiglu(HTV, x_f, 14, UV)
                    new = []

                    def sink(t, h, b, m, ex=ex, prev=x_m):
                        o = XV[:, t, 512 * h:512 * h + 512]
                        m = V(lambda e: e.scalar_tensor_tensor(o, b[:, :], gw[:, 8 * t + ex:8 * t + ex + 1], o,
                                                               ALU.mult, ALU.add), m, prev, gm)
                        new.append(m)
                        return m
                    down(UV, u_m, 28, sink)
                    x_m = new
            x_m = layer_norm(l, 1, x_m)

        out_m = load("out", out_d.rearrange("a (t p) n -> p (a t) n", p=128), XV, x_m, q=S)

        S.wait([out_m, scr_m])


def kernel(**inputs):
    import numpy as _np
    import concourse.bacc as _bacc
    from concourse import mybir as _mybir
    from concourse.bass_utils import run_bass_kernel_spmd as _run

    I = {k: _np.asarray(v) for k, v in inputs.items()}

    def tiles(w):
        return w.reshape(w.shape[0] // 128, 128, w.shape[1]).transpose(1, 0, 2)

    def lay(s):
        if s[0] == "cols":
            parts = [tiles(I[n][idx][:, a:b]) for n, idx, a, b in s[1]]
            return _np.stack(parts, axis=2).reshape(128, -1)
        if s[0] == "rows":
            n, idx, k0, k1 = s[1]
            return tiles(I[n][idx][128 * k0:128 * k1]).reshape(128, -1)
        l = s[1]
        return _np.concatenate([I["w_qk_m_2"][l].reshape(8, 128, 128).transpose(1, 0, 2).reshape(128, -1),
                                I["w_v_m_2"][l].transpose(1, 0, 2).reshape(128, -1),
                                tiles(I["w_if_2"][l]).reshape(128, -1)], axis=1)

    slots = layer_one_slots(0) + layer_one_slots(1) + layer_two_slots(0) + layer_two_slots(1)
    ws = _np.concatenate([lay(s).ravel() for s in slots])

    def cols(a):
        return a.reshape(-1, 128).T
    twice = lambda a: _np.concatenate([a, a])
    vec = _np.ascontiguousarray(_np.concatenate(
        [cols(I[n]) for n in ("attn_norm_g", "ffn_norm_g", "b_gate_2", "conv_w_2", "conv_b_2", "m_norm_g_2")]
        + [_np.stack([twice(I[n][l]) for l in range(2) for n in ("q_norm_b", "k_norm_b")], axis=1)], axis=1))
    row = _np.concatenate([I["q_norm_a"][0], I["k_norm_a"][0], I["q_norm_a"][1], I["k_norm_a"][1],
                           I["sink_a"].ravel(), I["b_if_2"].ravel(), I["router_b_2"].ravel()])
    ln = _np.ascontiguousarray(_np.stack([I["ln_g_2"], I["ln_b_2"]], axis=2)).ravel()
    relb = _np.zeros((2, 8, 15, 127), _np.float32)
    relb[..., 48:79] = I["rel_bias_b"]
    one, lnc = distance_constants()
    arrays = {"x": I["x"], "pos": _np.ascontiguousarray(I["positions"].reshape(2, 128).T), "ws": ws, "vec": vec, "row": row, "ln": ln,
              "rel": I["rel_bias_2"], "relb": relb,
              "rw": _np.ascontiguousarray(tiles(I["router_w_2"][0]).reshape(128, 64)),
              "cst": constants(), "one": one, "lnc": lnc}
    nc = _bacc.Bacc("TRN2", target_bir_lowering=False, num_devices=1)
    ins, args = {}, []
    for name, a in arrays.items():
        a = _np.ascontiguousarray(a)
        ins[f"in_{name}"] = a
        args.append(nc.dram_tensor(f"in_{name}", a.shape, _mybir.dt.from_np(a.dtype), kind="ExternalInput").ap())
    out = nc.dram_tensor("out_0", (1, 256, 1024), _mybir.dt.float32, kind="ExternalOutput").ap()
    program(nc, *args, out)
    r = _run(nc, [ins], core_ids=[0])
    return r.results[0]["out_0"]
```

```python
import concourse.bass as bass
from concourse import mybir
from contextlib import ExitStack
import math
import numpy as np

NEG = -1e30
EPS = 1e-6
LN_EPS = 1e-5
ALPHA = 4.0 ** 0.25
NRAW = 3
NSET = 3
SLOT = 2048
F_CHUNKS = [(512 * i, 512 * i + 512) for i in range(5)] + [(2560, 2816)]
E_CHUNKS = [(512 * i, 512 * i + 512) for i in range(7)]



def tall(name, index, c0, c1):
    if c1 - c0 <= 256:
        return [[(name, index, 0, 8, c0, c1)]]
    return [[(name, index, 4 * i, 4 * i + 4, c0, c1)] for i in range(2)]


def wide(name, index, tiles):
    return [[(name, index, k, k + 2, 0, 1024)] for k in range(0, tiles, 2)]


def hidden(gate, up, chunks):
    s = []
    for c0, c1 in chunks:
        for name, index, off in (gate, up):
            s += tall(name, index, off + c0, off + c1)
    return s


def layer_one_slots(l):
    i = (l,)
    s = []
    for a, b in ((0, 512), (512, 768), (768, 1280), (1280, 1792), (1792, 2304)):
        s += tall("w_in", i, a, b)
    for j in range(8):
        s.append([("w_in", i, 0, 8, 2304 + 128 * j, 2432 + 128 * j), ("w_in", i, 0, 8, 3328 + 128 * j, 3456 + 128 * j)])
    for j in range(4):
        s.append([(n, i, 0, 4, 256 * j, 256 * j + 256) for n in ("w_proj_a", "w_proj_b")])
    s += wide("w_out", i, 8)
    s += hidden(("w_gate", i, 0), ("w_up", i, 0), F_CHUNKS)
    return s + wide("w_down", i, 22)


def expert_slots(e):
    i = (0, e)
    return hidden(("exp_w13_2", i, 0), ("exp_w13_2", i, 3584), E_CHUNKS) + wide("exp_w2_2", i, 28)


def layer_two_slots(l):
    i = (l,)
    s = []
    for j in range(4):
        s += tall("w_in_2", i, 256 * j, 256 * j + 256)
    s += tall("w_in_2", i, 1024, 1536)
    for j in range(4):
        s += tall("w_in_2", i, 1536 + 256 * j, 1792 + 256 * j)
    for j in range(8):
        s.append([("w_gate_2", i, 0, 8, 1024 * k + 128 * j, 1024 * k + 128 * j + 128) for k in range(2)])
    s.append("mlstm")
    for j in range(4):
        s.append([(n, i, 0, 4, 256 * j, 256 * j + 256) for n in ("w_br_a_2", "w_br_m_2")])
    s += wide("w_o_2", i, 8)
    if l == 0:
        s += hidden(("ffn_w13_2", (0,), 0), ("ffn_w13_2", (0,), 2816), F_CHUNKS)
        s += wide("ffn_w2_2", (0,), 22)
    else:
        for e in range(8):
            s += expert_slots(e)
    return s


def slot_words(s):
    if s == "mlstm":
        return 8 * 128 + 4 * 128 + 96
    return sum((r1 - r0) * (c1 - c0) for _, _, r0, r1, c0, c1 in s)


VEC = {}
_at = 0
for _n, _c in (("attn_g", 16), ("ffn_g", 16), ("b_gate", 32), ("conv_w", 32), ("conv_b", 8), ("m_g", 8), ("qk_b", 4)):
    VEC[_n] = _at
    _at += _c
NVEC = _at
ROWV = 4 * 64 + 16 + 16 + 8
C_ID, C_J, C_JJ, C_ONE, C_TRI, C_CAUS, C_MA, C_MB, C_INV, C_IOTA, C_ROW = 0, 128, 256, 384, 512, 640, 896, 1408, 1472, 1504, 1512
NCONST = 1640


def constants():
    c = np.zeros((128, NCONST), np.float32)
    p = np.arange(128)[:, None]
    q = np.arange(128)[None, :]
    c[:, C_ID:C_ID + 128] = p == q
    c[:, C_J:C_J + 128] = p + q == 127
    c[:, C_JJ:C_JJ + 128] = (p // 64 == q // 64) & (p % 64 + q % 64 == 63)
    c[:, C_ONE:C_ONE + 128] = 1.0
    c[:, C_TRI:C_TRI + 128] = p <= q
    c[:, C_CAUS + 128:C_CAUS + 256] = np.where(q <= p, 0.0, NEG)
    c[:, C_MA + 128:C_MA + 256] = np.where(q <= p, 0.0, NEG)
    c[:, C_MA + 256:C_MA + 384] = np.where(q >= p, 0.0, NEG)
    k = np.arange(64)[None, :]
    cs = np.clip(p % 64 - 8, 0, 48)
    c[:, C_MB:C_MB + 64] = np.where((k >= cs) & (k < cs + 16), 0.0, NEG)
    c[:, C_INV:C_INV + 32] = (np.float32(10000.0) ** (-np.arange(32, dtype=np.float32) / np.float32(32)))[None, :]
    c[:, C_IOTA:C_IOTA + 8] = 8.0 - np.arange(8)[None, :]
    c[:, C_ROW:C_ROW + 128] = q
    return c


def distance_constants():
    one = np.zeros((32, 384), np.float32)
    ln = np.full((8, 384), NEG, np.float32)
    for j in range(256):
        d = 255 - j
        if d < 16:
            b = d
        else:
            b = min(31, 16 + int(np.float32(np.log(np.float32(d) / np.float32(16))) / math.log(2048 / 16) * 16))
        one[b, j] = 1.0
        n = (d <= 128) + (d % 4 == 0) + (d % 16 == 0)
        if n:
            ln[:, j] = math.log(n)
    return one, ln


def program(nc, x_d, pos_d, ws_d, vec_d, row_d, ln_d, rel_d, relb_d, rw_d, cst_d, one_d, lnc_d, out_d):
    f32 = mybir.dt.float32
    ALU = mybir.AluOpType
    ACT = mybir.ActivationFunctionType
    AX = mybir.AxisListType

    scr = nc.dram_tensor("scratch_rel", (8, 384), f32).ap()

    ctx = ExitStack()
    with ctx:
        def sb(name, n, dt=f32):
            return ctx.enter_context(nc.sbuf_tensor(name, [128, n], dt))

        class Queue:

            def __init__(self, engine, name):
                self.e = engine
                self.sem = ctx.enter_context(nc.semaphore(name))
                self.n = 0
                self.seen = {}

            def wait(self, waits):
                for sem, v in flat(waits):
                    if self.seen.get(id(sem), 0) < v:
                        self.e.wait_ge(sem, v)
                        self.seen[id(sem)] = v

            def __call__(self, fn, *waits, sig=True):
                self.wait(waits)
                ins = fn(self.e)
                if sig:
                    ins.then_inc(self.sem, 1)
                    self.n += 1
                    return (self.sem, self.n)

            def dma(self, out, in_, mark, *waits):
                self.wait(waits)
                self.e.dma_start(out, in_).then_inc(mark[0], 16)
                return mark

        def flat(ws):
            out = []
            for w in ws:
                if w is None:
                    continue
                if isinstance(w, list):
                    out += flat(w)
                else:
                    out.append(w)
            return out

        P, V, A = Queue(nc.tensor, "s_pe"), Queue(nc.vector, "s_dve"), Queue(nc.scalar, "s_act")
        G, S = Queue(nc.gpsimd, "s_pool"), Queue(nc.sync, "s_sp")

        f32r = mybir.dt.float32r
        raws = [sb(f"raw{i}", SLOT) for i in range(NRAW)]
        raw_sem = [ctx.enter_context(nc.semaphore(f"s_raw{i}")) for i in range(NRAW)]
        raw_free = [None] * NRAW
        sets = [(sb(f"wh{i}", SLOT, f32r), sb(f"wl{i}", SLOT, f32r)) for i in range(NSET)]
        set_free = [None] * NSET
        rest_sems = {n: ctx.enter_context(nc.semaphore("s_rest_" + n)) for n in "pvag"}
        rest_raw = [ctx.enter_context(nc.semaphore(f"s_rest_raw{i}")) for i in range(NRAW)]
        X = sb("X", 2048)
        HH, HL = sb("HH", 2048, f32r), sb("HL", 2048, f32r)
        BIAS = sb("BIAS", 3072)
        CST = sb("CST", NCONST)
        VECS = sb("VECS", NVEC)
        ROW = sb("ROW", ROWV)
        RW = sb("RW", 64)
        RWS = sb("RWS", 128, f32r)
        CS = sb("CS", 512)
        TRIG = sb("TRIG", 192)
        SM = sb("SM", 544)
        FLAG = sb("FLAG", 1, mybir.dt.int32)
        POSI = sb("POSI", 2, mybir.dt.int32)
        arena_at = (nc.sbuf_base + 31) // 32 * 32
        ARENA = sb("ARENA", 22016)

        def at(name, offset, n, dt=f32):
            assert offset + n <= 22016
            return nc.alloc_sbuf_tensor_at(name, [128, n], dt, offset=arena_at + 4 * offset)

        U = at("U", 0, 7168)
        GT = at("GT", 7168, 4096)
        LB = [at("L0", 11264, 2048), at("L1", 13312, 2048)]
        PT = at("PT", 15360, 2048)
        QT = at("QT", 17408, 3584)
        O = at("O", 20992, 1024)
        MH, ML = at("MH", 0, 2048, f32r), at("ML", 2048, 2048, f32r)
        FH, FL_ = at("FH", 0, 5632, f32r), at("FL", 5632, 5632, f32r)
        TT = [at("TT0", 11264, 512), at("TT1", 11776, 512)]
        TM = [at("TM0", 12288, 512), at("TM1", 12800, 512)]
        TU = [at("TU0", 13312, 512), at("TU1", 13824, 512)]
        EH, EL = at("EH", 0, 3584, f32r), at("EL", 3584, 3584, f32r)
        XH, XL = at("XH", 7168, 2048, f32r), at("XL", 9216, 2048, f32r)
        YH, YL = at("YH", 14336, 1024, f32r), at("YL", 15360, 1024, f32r)
        GH = [at(f"GH{i}", 16384 + 1024 * i, 1024, f32r) for i in range(2)]
        GL = [at(f"GL{i}", 18432 + 1024 * i, 1024, f32r) for i in range(2)]
        SEL = [at(f"SEL{i}", 20480 + 256 * i, 256) for i in range(2)]
        SELR = [at(f"SELR{i}", 20992 + 256 * i, 256, f32r) for i in range(2)]
        SELT = [at(f"SELT{i}", 21504 + 256 * i, 256, f32r) for i in range(2)]
        banks = [ctx.enter_context(nc.psum_tensor(f"bank{i}", [128, 512], f32)) for i in range(8)]
        free_banks = [(b, None) for b in banks]

        def take():
            return free_banks.pop(0)

        def give(b, *marks):
            free_banks.append((b, flat(marks)))

        ident = CST[:, C_ID:C_ID + 128]
        ones = CST[:, C_ONE:C_ONE + 128]
        tri = CST[:, C_TRI:C_TRI + 128]
        XV = X[:, :].rearrange("p (t n) -> p t n", t=2)
        HV = tuple(h[:, :].rearrange("p (k n) -> p k n", k=8) for h in (HH, HL))

        small_at = [0]

        def small(n):
            if small_at[0] + n > 448:
                small_at[0] = 0
            a = small_at[0]
            small_at[0] += n
            return SM[:, a:a + n]

        HALF = SM[:, 448:449]
        PW = SM[:, 449:481]

        one_sem = {}

        def load(name, out, in_, *waits, q=None):
            if name not in one_sem:
                one_sem[name] = [ctx.enter_context(nc.semaphore("s_" + name)), 0]
            one_sem[name][1] += 16
            (q or A).dma(out, in_, (one_sem[name][0], one_sem[name][1]), *waits)
            return (one_sem[name][0], one_sem[name][1])

        x_m = load("x", XV, x_d.rearrange("a (t p) n -> p (a t) n", p=128), q=S)
        cst_m = load("cst", CST[:, :], cst_d)
        load("small", VECS[:, :], vec_d)
        load("small", ROW[:, :], bass.AP(row_d.tensor, 0, [[0, 128], [1, ROWV]]))
        load("small", RW[:, :], rw_d)
        load("small", POSI[:, :], pos_d)
        load("small", PT[0:32, 0:384], one_d)
        load("small", PT[0:32, 384:392], rel_d)
        small_m = load("small", PT[0:8, 512:896], lnc_d)

        offset = [0]
        count = [0, 0]
        pending = []
        ready = []

        def plan(slots):
            pending.extend(slots)

        def fetch():
            s = pending.pop(0)
            n = slot_words(s)
            i = count[0] % NRAW
            mark = (raw_sem[i], 16 * (count[0] // NRAW + 1))
            S.dma(raws[i][:, 0:n], bass.AP(ws_d.tensor, offset[0], [[n, 128], [1, n]]), mark, raw_free[i])
            offset[0] += 128 * n
            count[0] += 1
            if s == "mlstm":
                def done(m):
                    raw_free[i] = m
                ready.append((raws[i], None, mark, done))
                return
            j = count[1] % NSET
            count[1] += 1
            h, lo = sets[j]
            if count[1] % 4 == 4:
                mh = V(lambda e: e.tensor_copy(h[:, 0:n], raws[i][:, 0:n]), mark, set_free[j])
            else:
                mh = A(lambda e: e.activation(h[:, 0:n], raws[i][:, 0:n], ACT.Copy), mark, set_free[j])
            ml = V(lambda e: e.tensor_tensor(lo[:, 0:n], raws[i][:, 0:n], h[:, 0:n].bitcast(f32), ALU.subtract),
                   mh, mark, set_free[j])
            raw_free[i] = ml

            def done(m):
                set_free[j] = m
            ready.append((h, lo, [mh, ml], done))

        def next_weights():
            while len(ready) < NSET and pending:
                if len(ready) and (pending[0] == "mlstm" or ready[-1][1] is None):
                    break
                fetch()
            return ready.pop(0)

        alt = [0]

        def evac(out, in_, *waits, scale=None, eng=None):
            alt[0] += 1
            if eng is None:
                eng = A if alt[0] % 2 else V
            if eng is A:
                return A(lambda e: e.activation(out, in_, ACT.Copy, scale=1.0 if scale is None else scale), *waits)
            if scale is None:
                return V(lambda e: e.tensor_copy(out, in_), *waits)
            return V(lambda e: e.tensor_scalar(out, in_, scale, None, ALU.mult), *waits)

        def mm(out, l, r, st, sp, *waits, sig=False):
            return P(lambda e: e.matmul(out, l, r, start=st, stop=sp), *waits, sig=sig)

        def mm3(out, l, r, st, sp, *waits, sig=False):
            P(lambda e: e.matmul(out, l[0], r[0], start=st, stop=False), *waits, sig=False)
            P(lambda e: e.matmul(out, l[0], r[1], start=False, stop=False), sig=False)
            return P(lambda e: e.matmul(out, l[1], r[0], start=False, stop=sp), sig=sig)

        def parts(dst, src, *waits, scale=None):
            m = A(lambda e: e.activation(dst[0], src, ACT.Copy, scale=1.0 if scale is None else scale), *waits)
            hi = dst[0].bitcast(f32)
            if scale is None:
                return V(lambda e: e.tensor_tensor(dst[1], src, hi, ALU.subtract), m, *waits)
            return V(lambda e: e.scalar_tensor_tensor(dst[1], src, scale, hi, ALU.mult, ALU.subtract), m, *waits)

        def tr(out, in_, *waits, sig=False):
            return P(lambda e: e.transpose(out, in_, ident), *waits, sig=sig)

        zero = V(lambda e: e.memset(HALF, 0.0))
        zero = V(lambda e: e.memset(PW, -0.5), zero)

        def rpow(out, in_, *waits):
            n = in_.shape[1]
            return G(lambda e: e.tensor_tensor(out, in_, PW[:, 0:n], ALU.pow), zero, *waits)

        def rope_tables():
            F = small(2)
            m = V(lambda e: e.tensor_copy(F, POSI[:, :]), small_m)
            ang = TRIG[:, 0:64]
            for t in range(2):
                m2 = V(lambda e, t=t: e.tensor_scalar(TRIG[:, 32 * t:32 * t + 32], CST[:, C_INV:C_INV + 32],
                                                      F[:, t:t + 1], None, ALU.mult), m, cst_m)
            two_pi = 2 * math.pi
            parts = []
            rest = two_pi
            for _ in range(3):
                e2 = 2.0 ** (math.floor(math.log2(rest)) - 7)
                c = math.floor(rest / e2) * e2
                parts.append(c)
                rest -= c
            parts.append(rest)
            tabs = []
            for j, quarter in enumerate((0.0, 0.25)):
                K = LB[1][:, 64 * j:64 * j + 64]
                R = LB[1][:, 128 + 64 * j:192 + 64 * j]
                m = V(lambda e: e.tensor_scalar(K, ang, 1.0 / two_pi, quarter, ALU.mult, ALU.add), m2)
                m = V(lambda e: e.tensor_scalar(K, K, 12582912.0, None, ALU.add), m)
                m = V(lambda e: e.tensor_scalar(K, K, -12582912.0, None, ALU.add), m)
                src = ang
                for c in parts:
                    m = V(lambda e, c=c, src=src: e.scalar_tensor_tensor(R, K, -c, src, ALU.mult, ALU.add), m)
                    src = R
                if quarter:
                    m = V(lambda e: e.tensor_scalar(R, R, math.pi / 2, None, ALU.add), m)
                pi = 3.1415925
                m = V(lambda e: e.tensor_scalar(R, R, pi, -pi, ALU.min, ALU.max), m)
                dst = TRIG[:, 64 + 64 * j:128 + 64 * j]
                tabs.append(A(lambda e: e.activation(dst, R, ACT.Sin), m))
            return tabs

        trig_m = rope_tables()

        def distance_table():
            b, fr = take()
            m = mm(b[0:8, 0:384], PT[0:32, 384:392], PT[0:32, 0:384], True, True, small_m, fr, sig=True)
            m = V(lambda e: e.tensor_tensor(PT[0:8, 512:896], b[0:8, 0:384], PT[0:8, 512:896], ALU.add), m)
            give(b, m)
            return load("scr", scr, PT[0:8, 512:896], m)

        scr_m = distance_table()

        def flip(raw, j, n, after, add=None):
            ms = []
            for c in range(n // 512):
                b, fr = take()
                m = mm(b[:, :], j, raw[:, 512 * c:512 * c + 512], True, True, after, fr, cst_m, sig=True)
                o = BIAS[:, 512 * c:512 * c + 512]
                if add is None:
                    m = evac(o, b[:, :], m)
                else:
                    m = V(lambda e, o=o, b=b: e.tensor_tensor(
                        o.rearrange("p (a k) -> p a k", k=64), b[:, :].rearrange("p (a k) -> p a k", k=64),
                        add[:, None, :].to_broadcast([128, 8, 64]), ALU.add), m)
                give(b, m)
                ms.append(m)
            return ms

        def bias_one(l, *waits):
            m = None
            for s in range(2):
                for h in range(8):
                    m = load("bias", U[64 * s:64 * s + 64, 384 * h:384 * h + 384].rearrange("p (j k) -> p j k", j=6),
                             bass.AP(relb_d.tensor, ((l * 8 + h) * 15 + 5 - s) * 127, [[1, 64], [127, 6], [1, 64]]),
                             *waits)
            return flip(U, CST[:, C_JJ:C_JJ + 128], 3072, m, CST[:, C_MB:C_MB + 64])

        def bias_two(*waits):
            m = load("bias", U[:, 0:2048].rearrange("p (h k) -> p h k", h=8),
                     bass.AP(scr.tensor, 0, [[1, 128], [384, 8], [1, 256]]), scr_m, *waits)
            return flip(U, CST[:, C_J:C_J + 128], 2048, m)

        def to_features(src, dst, marks, scale=None):
            out = []
            for c2 in range(4):
                b, fr = take()
                for c in (2 * c2, 2 * c2 + 1):
                    for t in range(2):
                        m = tr(b[:, 256 * (c % 2) + 128 * t:256 * (c % 2) + 128 * t + 128],
                               src[:, t, 128 * c:128 * c + 128], marks, fr, cst_m, sig=(c % 2 and t))
                ms = []
                for c in (2 * c2, 2 * c2 + 1):
                    ms.append(parts([d[:, c, :] for d in dst], b[:, 256 * (c % 2):256 * (c % 2) + 256], m, small_m,
                                    ms, scale=None if scale is None else scale[:, c:c + 1]))
                give(b, ms)
                out += ms
            return out

        def rms_features(g, x_m):
            ss, ms, rs = small(2), small(2), small(2)
            m = []
            for t in range(2):
                m.append(A(lambda e, t=t: e.activation(LB[0][:, 1024 * t:1024 * t + 1024], XV[:, t, :], ACT.Square,
                                                       accum_out=ss[:, t:t + 1]), x_m))
            m = V(lambda e: e.tensor_scalar(ms, ss, 1.0 / 1024, EPS, ALU.mult, ALU.add), m)
            m = rpow(rs, ms, m)
            hv = LB[0][:, :].rearrange("p (t n) -> p t n", t=2)
            hm = [A(lambda e: e.activation(hv[:, 0, :], XV[:, 0, :], ACT.Copy, scale=rs[:, 0:1]), m),
                  V(lambda e: e.tensor_scalar(hv[:, 1, :], XV[:, 1, :], rs[:, 1:2], None, ALU.mult), m)]
            return to_features(hv, HV, hm, scale=g)

        def wview(slot, k, a, n):
            return tuple(w[:, 0:k * a * n].rearrange("p (k a n) -> p k a n", k=k, a=a) for w in slot)

        def by_tokens(lhs, marks, n, sink):
            bs = [take() for _ in range(2)]
            rows = 8 if n <= 256 else 4
            for k0 in range(0, 8, rows):
                h, lo, wm, done = next_weights()
                w = wview((h, lo), rows, 1, n)
                for t in range(2):
                    b, fr = bs[t]
                    for k in range(rows):
                        kk = k0 + k
                        m = mm3(b[:, 0:n], [v[:, kk, 128 * t:128 * t + 128] for v in lhs],
                                [v[:, k, 0, :] for v in w], kk == 0, kk == 7, wm, marks[kk], fr, sig=(k == rows - 1))
                    bs[t] = (b, fr) if kk < 7 else (b, m)
                done(m)
            for t, (b, m) in enumerate(bs):
                give(b, sink(t, b, m))

        def by_features(rhs, marks, kt, parts, width, sink):
            h, lo, wm, done = next_weights()
            w = wview((h, lo), kt, parts, width)
            if parts == 1:
                sides = [[(0, 0), (0, 1)]]
            else:
                sides = [[(0, c), (1, c)] for c in range(width // 128)]
            for i, side in enumerate(sides):
                b, fr = take()
                for j, (a, c) in enumerate(side):
                    for k in range(kt):
                        m = mm3(b[:, 256 * j:256 * j + 256], [v[:, k, a, 128 * c:128 * c + 128] for v in w],
                                [v[:, k, :] for v in rhs[a]], k == 0, k == kt - 1, wm, marks[a][k], fr,
                                sig=(k == kt - 1 and j == 1))
                if i == len(sides) - 1:
                    done(m)
                give(b, sink(i, b, m))

        def down(src, marks, kts, tiles, sink, after_first=None):
            held = [[take() for _ in range(2)] for _ in range(tiles)]
            for k0 in range(0, kts, 2):
                h_, lo, wm, done = next_weights()
                w = wview((h_, lo), 2, 1, 1024)
                for k in (k0, k0 + 1):
                    for t in range(tiles):
                        for h in range(2):
                            b, fr = held[t][h]
                            last = k == kts - 1
                            m = mm3(b[:, :], [v[:, k, 128 * t:128 * t + 128] for v in src],
                                    [v[:, k - k0, 0, 512 * h:512 * h + 512] for v in w], k == 0, last,
                                    wm, marks(k), fr,
                                    sig=(last or (k > k0 and t == tiles - 1 and h == 1)))
                            if last:
                                give(b, sink(t, h, b, m))
                done(m)
                if k0 == 0 and after_first:
                    after_first()

        t_free = [[None, None, None] for _ in range(2)]

        def swiglu(lhs, marks, chunks, tiles, dst, before=None):
            out = {}
            left = []

            def turn():
                for c0, n, t, m in left:
                    b, fr = take()
                    for c in range(n // 128):
                        mt = tr(b[:, 128 * c:128 * c + 128], TU[t][:, 128 * c:128 * c + 128], m, fr,
                                sig=(c == n // 128 - 1))
                    f = c0 // 128
                    md = parts([d[:, f:f + n // 128, 128 * t:128 * t + 128] for d in dst],
                               b[:, 0:n].rearrange("p (c k) -> p c k", k=128), mt)
                    give(b, md)
                    t_free[t][2] = mt
                    for c in range(n // 128):
                        out.setdefault(f + c, []).append(md)
                left.clear()

            for c0, c1 in chunks:
                n = c1 - c0
                rows = 8 if n <= 256 else 4
                bs = {(a, t): take() for a in range(2) for t in range(tiles)}
                for a in range(2):
                    for k0 in range(0, 8, rows):
                        h, lo, wm, done = next_weights()
                        w = wview((h, lo), rows, 1, n)
                        for t in range(tiles):
                            b, fr = bs[a, t]
                            for k in range(rows):
                                kk = k0 + k
                                m = mm3(b[:, 0:n], [v[:, kk, 128 * t:128 * t + 128] for v in lhs],
                                        [v[:, k, 0, :] for v in w], kk == 0, kk == 7, wm, marks[kk], fr,
                                        sig=(k == rows - 1))
                            if k0 + rows == 8:
                                bs[a, t] = (b, m)
                        done(m)
                if before:
                    before()
                    before = None
                turn()
                for t in range(tiles):
                    (bg, mg), (bu, mu) = bs[0, t], bs[1, t]
                    T, M, W = (x[t][:, 0:n] for x in (TT, TM, TU))
                    fr = t_free[t]
                    m1 = A(lambda e: e.activation(T, bg[:, 0:n], ACT.Tanh, scale=0.5), mg, fr[0])
                    m2 = V(lambda e: e.scalar_tensor_tensor(M, T, 1.0, bg[:, 0:n], ALU.add, ALU.mult), m1, fr[1])
                    give(bg, m2)
                    m3 = V(lambda e: e.tensor_tensor(W, M, bu[:, 0:n], ALU.mult), m2, mu, fr[2])
                    give(bu, m3)
                    fr[0], fr[1] = m2, m3
                    left.append((c0, n, t, m3))
            return turn, lambda k: out[k]

        def add_to_x(x_marks, scale=0.5, alpha=None):
            new = []
            pre = x_marks
            if alpha is not None:
                pre = [V(lambda e: e.tensor_scalar(X[:, :], X[:, :], alpha, None, ALU.mult), x_marks)]

            def sink(t, h, b, m):
                o = XV[:, t, 512 * h:512 * h + 512]
                m = V(lambda e: e.scalar_tensor_tensor(o, b[:, :], scale, o, ALU.mult, ALU.add), m, pre)
                new.append(m)
                return m
            return sink, new

        def gates(lhs, marks, bias=None):
            for j in range(8):
                def sink(c, b, m, f=j):
                    if bias is None:
                        return A(lambda e: e.activation(GT[:, 512 * f:512 * f + 512], b[:, :], ACT.Tanh, scale=0.5), m)
                    for a in range(2):
                        r = A(lambda e, a=a: e.activation(GT[:, 512 * f + 256 * a:512 * f + 256 * a + 256],
                                                          b[:, 256 * a:256 * a + 256], ACT.Tanh, scale=0.5,
                                                          bias=bias[:, 8 * a + f:8 * a + f + 1]), m, bias_m)
                    return r
                by_features([lhs, lhs], [marks, marks], 8, 2, 128, sink)
                if j % 2:
                    yield

        def mix(oa, ob, ma, mb, gt_m):
            out = []
            for j in range(4):
                def sink(c, b, m, j=j):
                    f = 2 * j + c
                    g = GT[:, 512 * f:512 * f + 512]
                    m = V(lambda e: e.scalar_tensor_tensor(g, g, 1.0, b[:, :], ALU.add, ALU.mult), m, gt_m)
                    r = V(lambda e: e.tensor_tensor(g[:, 0:256], g[:, 0:256], g[:, 256:512], ALU.add), m)
                    out.append(parts([d[:, 256 * f:256 * f + 256] for d in (MH, ML)], g[:, 0:256], r))
                    return m
                by_features([oa, ob], [ma, mb], 4, 2, 256, sink)
            return out

        pt_free = [None]

        def transpose_p(src, heads, kts, m_src):
            marks = []
            blocks = [(h, i) for h in range(heads) for i in range(kts)]
            for c in range(0, len(blocks), 4):
                b, fr = take()
                part = blocks[c:c + 4]
                for n, (h, i) in enumerate(part):
                    m = tr(b[:, 128 * n:128 * n + 128], src(h, i), m_src[h], fr, cst_m, sig=(n == len(part) - 1))
                n = 128 * len(part)
                m = evac(PT[:, 128 * c:128 * c + n], b[:, 0:n], m, pt_free[0])
                give(b, m)
                marks += [m] * len(part)
            return marks

        def attention(q, k, v, bias, kts_of, q_m, k_m, v_m, sinks=None, l_free=None):
            state = {}

            def scores(t):
                kts = kts_of(t)
                n = 128 * kts
                L = LB[t]
                mx, nm, su = small(8), small(8), small(8)
                ms = []
                for h2 in range(4):
                    b, fr = take()
                    h0 = 4 * (h2 // 2) + h2 % 2
                    for i in range(2):
                        h = h0 + 2 * i
                        m = mm(b[:, 256 * i:256 * i + n], q(h, t), k(h)[:, 0:n], True, True,
                               q_m, k_m, fr, sig=(i == 1))
                    for i in range(2):
                        h = h0 + 2 * i
                        m = V(lambda e, h=h, b=b: e.tensor_tensor_reduce(
                            L[:, 256 * h:256 * h + n], b[:, 256 * i:256 * i + n], bias(h, t), 1.0,
                            NEG if sinks is None else sinks[:, h:h + 1], ALU.add, ALU.max, mx[:, h:h + 1]),
                            m, bias_marks, small_m)
                    give(b, m)
                m = V(lambda e: e.tensor_scalar(nm, mx, -1.0, None, ALU.mult), m)
                for h in range(8):
                    ms.append(A(lambda e, h=h: e.activation(L[:, 256 * h:256 * h + n], L[:, 256 * h:256 * h + n],
                                                            ACT.Exp, bias=nm[:, h:h + 1],
                                                            accum_out=su[:, h:h + 1]), m))
                last = ms[-1]
                if sinks is not None:
                    es = small(8)
                    m = V(lambda e: e.tensor_tensor(es, sinks, nm, ALU.add), m, small_m)
                    m = A(lambda e: e.activation(es, es, ACT.Exp), m)
                    last = V(lambda e: e.tensor_tensor(su, su, es, ALU.add), m, last)
                rs = small(8)
                last = V(lambda e: e.reciprocal(rs, su), last)
                state[t] = (ms, rs, last, kts)

            def values(t, dst):
                ms, rs, rm, kts = state[t]
                L = LB[t]
                pm = transpose_p(lambda h, i: L[:, 256 * h + 128 * i:256 * h + 128 * i + 128], 8, kts, ms)
                b, fr = take()
                for h in range(8):
                    for i in range(kts):
                        m = mm(b[:, 64 * h:64 * h + 64], PT[:, 128 * (h * kts + i):128 * (h * kts + i) + 128],
                               v(h, i), i == 0, i == kts - 1, pm[h * kts + i], v_m, fr,
                               sig=(h == 7 and i == kts - 1))
                pt_free[0] = m
                o = O[:, 512 * t:512 * t + 512]
                m = V(lambda e: e.tensor_tensor(o.rearrange("p (h d) -> p h d", h=8),
                                                b[:, :].rearrange("p (h d) -> p h d", h=8),
                                                rs[:, :, None].to_broadcast([128, 8, 64]), ALU.mult), m, rm)
                give(b, m)
                b, fr = take()
                for c in range(4):
                    m2 = tr(b[:, 128 * c:128 * c + 128], o[:, 128 * c:128 * c + 128], m, fr, sig=(c == 3))
                m2 = parts([d[:, :, 128 * t:128 * t + 128] for d in dst],
                           b[:, :].rearrange("p (c n) -> p c n", c=4), m2)
                give(b, m2)
                return m2
            return scores, values

        FV = [v[:, :].rearrange("p (f n) -> p f n", f=22) for v in (FH, FL_)]

        for i in (0, 2):
            c = VECS[:, VEC["qk_b"] + i:VEC["qk_b"] + i + 1]
            qkb_m = G(lambda e: e.tensor_scalar(c, c, 0.125, None, ALU.mult), small_m)
        for l in range(2):
            plan(layer_one_slots(l))
            bias_marks = bias_one(l, x_m if l else None)
            h_m = rms_features(VECS[:, VEC["attn_g"] + 8 * l:VEC["attn_g"] + 8 * l + 8], x_m)
            QA = [U[:, 768 * t:768 * t + 768] for t in range(2)]
            QB = [U[:, 1536 + 1536 * t:3072 + 1536 * t] for t in range(2)]
            free_m = bias_marks

            got = {}

            def keep(key, dst):
                def sink(t, b, m):
                    n = dst(t).shape[1]
                    got[key, t] = evac(dst(t), b[:, 0:n], m, free_m)
                    return got[key, t]
                return sink

            by_tokens(HV, h_m, 512, keep("qa", lambda t: QA[t][:, 0:512]))
            by_tokens(HV, h_m, 256, keep("kva", lambda t: QA[t][:, 512:768]))
            by_tokens(HV, h_m, 512, keep("qb", lambda t: QB[t][:, 0:512]))
            by_tokens(HV, h_m, 512, keep("kb", lambda t: QB[t][:, 512:1024]))
            by_tokens(HV, h_m, 512, keep("vb", lambda t: QB[t][:, 1024:1536]))
            gate_steps = gates(HV, h_m)

            rt_m = []
            for t in range(2):
                sn = TRIG[:, 64 + 32 * t:96 + 32 * t]
                co = TRIG[:, 128 + 32 * t:160 + 32 * t]
                for w in range(2):
                    g = ROW[:, 128 * l + 64 * w:128 * l + 64 * w + 64]
                    base = 256 * t + 128 * w
                    for hf in range(2):
                        a = base + 32 * hf
                        rt_m.append(G(lambda e, a=a, co=co, g=g, hf=hf: e.tensor_tensor(
                            CS[:, a:a + 32], co, g[:, 32 * hf:32 * hf + 32], ALU.mult), trig_m, small_m, x_m))
                        a = base + 64 + 32 * hf
                        m = G(lambda e, a=a, sn=sn, g=g, hf=hf: e.tensor_tensor(
                            CS[:, a:a + 32], sn, g[:, 32 - 32 * hf:64 - 32 * hf], ALU.mult), trig_m, small_m, x_m)
                        if hf == 0:
                            m = G(lambda e, a=a: e.tensor_scalar(CS[:, a:a + 32], CS[:, a:a + 32], -1.0, None,
                                                                 ALU.mult), m)
                        rt_m.append(m)

            def norm(view, heads, marks):
                sq = PT[:, 0:64 * heads]
                ss, ms, rs = small(heads), small(heads), small(heads)
                m = A(lambda e: e.activation(sq, view, ACT.Square), marks, pt_free[0])
                m = V(lambda e: e.tensor_reduce(ss, sq.rearrange("p (h d) -> p h d", h=heads), AX.X, ALU.add), m)
                pt_free[0] = [pt_free[0], m]
                m = V(lambda e: e.tensor_scalar(ms, ss, 1.0 / 64, EPS, ALU.mult, ALU.add), m)
                m = rpow(rs, ms, m)
                vv = view.rearrange("p (h d) -> p h d", h=heads)
                return V(lambda e: e.tensor_tensor(vv, vv, rs[:, :, None].to_broadcast([128, heads, 64]),
                                                   ALU.mult), m)

            KD = LB[0]
            qa_m, ka_m = [], []
            for t in range(2):
                m = norm(QA[t][:, 0:640], 10, [got["qa", t], got["kva", t]])
                tmp = LB[1][:, 0:640]
                tmp2 = LB[1][:, 640:1280]
                r = [m, qa_m, ka_m]
                for w, (h0, h1) in enumerate(((0, 8), (8, 10))):
                    n = h1 - h0
                    xq = QA[t][:, 64 * h0:64 * h1].rearrange("p (h d) -> p h d", h=n)
                    t1 = tmp[:, 64 * h0:64 * h1].rearrange("p (h d) -> p h d", h=n)
                    t2 = tmp2[:, 64 * h0:64 * h1].rearrange("p (h d) -> p h d", h=n)
                    cg = CS[:, 256 * t + 128 * w:256 * t + 128 * w + 64]
                    sg = CS[:, 256 * t + 128 * w + 64:256 * t + 128 * w + 128]
                    ms = [V(lambda e, t1=t1, xq=xq, cg=cg, n=n: e.tensor_tensor(
                        t1, xq, cg[:, None, :].to_broadcast([128, n, 64]), ALU.mult), r, rt_m)]
                    for hf in range(2):
                        ms.append(G(lambda e, t2=t2, xq=xq, sg=sg, n=n, hf=hf: e.tensor_tensor(
                            t2[:, :, 32 * hf:32 * hf + 32], xq[:, :, 32 - 32 * hf:64 - 32 * hf],
                            sg[:, None, 32 * hf:32 * hf + 32].to_broadcast([128, n, 32]), ALU.mult), r, rt_m))
                    if w == 0:
                        qa_m.append(V(lambda e, xq=xq, t1=t1, t2=t2: e.tensor_tensor(xq, t1, t2, ALU.add), ms))
                    else:
                        for d in range(2):
                            o = KD[:, 256 * t:256 * t + 256].rearrange("p (g d n) -> p g d n", g=2, d=2)[:, :, d, :]
                            ka_m.append(V(lambda e, o=o, t1=t1, t2=t2: e.tensor_tensor(o, t1, t2, ALU.add), ms, h_m))
            next(gate_steps)
            qb_m = []
            for t in range(2):
                qb_m.append(norm(QB[t][:, 0:1024], 16, [got["qb", t], got["kb", t]]))
            next(gate_steps)

            def fold(dst, srcs, marks, scale):
                out = []
                n = srcs[0].shape[1] // 128
                for c2 in range(n // 2):
                    b, fr = take()
                    for c in (2 * c2, 2 * c2 + 1):
                        for t in range(2):
                            m = tr(b[:, 256 * (c % 2) + 128 * t:256 * (c % 2) + 128 * t + 128],
                                   srcs[t][:, 128 * c:128 * c + 128], marks, fr, sig=(c % 2 and t))
                    m = evac(dst[:, 512 * c2:512 * c2 + 512], b[:, :], m, scale=scale)
                    give(b, m)
                    out.append(m)
                return out

            qta = fold(QT[:, 0:1024], [QA[t][:, 0:512] for t in range(2)], qa_m, 0.125)
            kta = fold(QT[:, 1024:1536], [KD[:, 256 * t:256 * t + 256] for t in range(2)], ka_m, None)
            qkb = VECS[:, VEC["qk_b"] + 2 * l:VEC["qk_b"] + 2 * l + 2]
            qtb = fold(QT[:, 1536:2560], [QB[t][:, 0:512] for t in range(2)], qb_m + [qkb_m], qkb[:, 0:1])
            ktb = fold(QT[:, 2560:3584], [QB[t][:, 512:1024] for t in range(2)], qb_m, qkb[:, 1:2])

            def qa_of(h, t):
                return QT[64 * (h % 2):64 * (h % 2) + 64, 256 * (h // 2) + 128 * t:256 * (h // 2) + 128 * t + 128]

            def ka_of(h):
                return QT[64 * (h % 2):64 * (h % 2) + 64, 1024 + 256 * (h // 4):1280 + 256 * (h // 4)]

            def qb_of(h, t):
                a = 1536 + 256 * (h // 2) + 128 * t
                return QT[64 * (h % 2):64 * (h % 2) + 64, a:a + 128]

            def kb_of(h):
                a = 2560 + 256 * (h // 2)
                return QT[64 * (h % 2):64 * (h % 2) + 64, a:a + 256]

            sc_a, va_a = attention(qa_of, ka_of, lambda h, i: QA[i][:, 640 + 64 * (h // 4):704 + 64 * (h // 4)],
                                   lambda h, t: CST[:, C_MA + 256 * t:C_MA + 256 * t + 256], lambda t: 2,
                                   qta, kta, [got["kva", 0], got["kva", 1]],
                                   sinks=ROW[:, 256 + 8 * l:264 + 8 * l])
            BV = BIAS[:, :].rearrange("p (h j k) -> p h j k", h=8, j=6)
            sc_b, va_b = attention(qb_of, kb_of, lambda h, i: QB[i][:, 1024 + 64 * h:1088 + 64 * h],
                                   lambda h, t: BIAS[:, 384 * h + 128 - 128 * t:384 * h + 384 - 128 * t],
                                   lambda t: 2, qtb, ktb, [got["vb", 0], got["vb", 1]])
            sc_a(0)
            next(gate_steps)
            sc_a(1)
            for _ in gate_steps:
                pass
            gt_m = (A.sem, A.n)
            oa = [v[:, 0:4, :] for v in HV]
            ob = [v[:, 4:8, :] for v in HV]
            oam = [va_a(0, oa)]
            sc_b(0)
            oam.append(va_a(1, oa))
            sc_b(1)
            obm = [va_b(0, ob), va_b(1, ob)]
            mm_ = mix(oa, ob, [oam] * 4, [obm] * 4, gt_m)
            sink, new = add_to_x([x_m])
            down([d[:, :].rearrange("p (c n) -> p c n", c=8) for d in (MH, ML)], lambda k: mm_[k], 8, 2, sink)
            x_m = new
            h_m = rms_features(VECS[:, VEC["ffn_g"] + 8 * l:VEC["ffn_g"] + 8 * l + 8], x_m)
            turn, u_m = swiglu(HV, h_m, F_CHUNKS, 2, FV)
            sink, new = add_to_x(x_m)
            down(FV, u_m, 22, 2, sink, turn)
            x_m = new

        def rest_of_tokens(first, pos, gw, flag_m, x_m):
            queues = (P, V, A, G, S)
            compute = (P, V, A, G)
            before = [(q.sem, q.n) for q in compute]
            for q in queues:
                q.wait([before, flag_m])
            flag = nc.values_load(FLAG[0:1, 0:1], min_val=0, max_val=1)
            kept = [(q.sem, q.n, dict(q.seen)) for q in queues]
            kept_raw = (list(raw_sem), list(count))
            with nc.If(flag):
                for q, name in zip(compute, ("p", "v", "a", "g")):
                    q.sem, q.n = rest_sems[name], 0
                raw_sem[:] = rest_raw
                count[:] = [0, 0]
                raw_free[:] = [None] * NRAW
                set_free[:] = [None] * NSET
                free_banks[:] = [(b, None) for b, _ in free_banks]
                t_free[:] = [[None, None, None] for _ in range(2)]
                offset[0] = first
                for i in range(8):
                    plan(expert_slots(i))
                experts(128, pos, gw, None, None, None, None)
                after = [(q.sem, q.n) for q in compute if q.n]
                for q in queues:
                    q.wait(after)
            for q, (sem, n, seen) in zip(queues, kept):
                q.sem, q.n, q.seen = sem, n, seen
            raw_sem[:], count[:] = kept_raw
            free_banks[:] = [(b, None) for b, _ in free_banks]
            return None

        def layer_norm(l, i, x_marks):
            gb = load("ln", PT[:, :], bass.AP(ln_d.tensor, (2 * l + i) * 2048, [[0, 128], [1, 2048]]),
                      x_marks, pt_free[0])
            out = []
            for t in range(2):
                st, ag, ve, rs = small(12), small(2), small(1), small(1)
                for h in range(2):
                    m = V(lambda e, h=h, t=t: e.bn_stats(st[:, 6 * h:6 * h + 6], XV[:, t, 512 * h:512 * h + 512]),
                          x_marks)
                m = V(lambda e: e.bn_aggr(ag, st), m)
                m = V(lambda e: e.tensor_scalar(ve, ag[:, 1:2], LN_EPS, None, ALU.add), m)
                m = rpow(rs, ve, m)
                xt = XV[:, t, :]
                m = V(lambda e: e.tensor_scalar(xt, xt, ag[:, 0:1], rs[:, 0:1], ALU.subtract, ALU.mult), m)
                m = V(lambda e: e.tensor_tensor(xt, xt, PT[:, 0:1024], ALU.mult), m, gb)
                m = V(lambda e: e.tensor_tensor(xt, xt, PT[:, 1024:2048], ALU.add), m)
                out.append(m)
            pt_free[0] = out
            return out

        EV = [v[:, :].rearrange("p (f n) -> p f n", f=28) for v in (EH, EL)]
        rws_m = parts([RWS[:, 0:64], RWS[:, 64:128]], RW[:, :], small_m)

        def experts(base, pos, gw, pos_m, gm, xs_m, x_m):
            g_free = [[None] * 4 for _ in range(2)]
            y_free = [None]
            got = {}

            def gather(e_):
                i = e_ % 2
                fr_ = g_free[i]
                ms, mt = [], []
                for t in range(2):
                    p = pos[:, 8 * t + e_:8 * t + e_ + 1]
                    row = CST[:, C_ROW:C_ROW + 128]
                    mt.append(V(lambda e: e.tensor_scalar(SEL[i][:, 128 * t:128 * t + 128], row, float(base), p,
                                                          ALU.add, ALU.is_equal), pos_m, fr_[0]))
                    ms.append(V(lambda e: e.tensor_scalar(SELR[i][:, 128 * t:128 * t + 128], row, float(base), p,
                                                          ALU.add, ALU.is_equal), pos_m, fr_[1]))
                b, fr = take()
                for t in range(2):
                    m = tr(b[:, 128 * t:128 * t + 128], SEL[i][:, 128 * t:128 * t + 128], mt, fr, sig=(t == 1))
                fr_[0] = m
                sel_m = evac(SELT[i][:, :], b[:, 0:256], m, fr_[2])
                give(b, sel_m)
                out = []
                for src, dst in ((XH, GH[i]), (XL, GL[i])):
                    for c4 in range(2):
                        b, fr = take()
                        for c in range(4 * c4, 4 * c4 + 4):
                            for t in range(2):
                                a = 1024 * t + 128 * c
                                m = P(lambda e: e.matmul(b[:, 128 * (c % 4):128 * (c % 4) + 128], src[:, a:a + 128],
                                                         SELR[i][:, 128 * t:128 * t + 128], start=(t == 0),
                                                         stop=(t == 1)), ms, xs_m, fr, sig=(c % 4 == 3 and t == 1))
                        m2 = evac(dst[:, 512 * c4:512 * c4 + 512], b[:, :], m)
                        give(b, m2)
                        out.append(m2)
                fr_[1] = m
                got[e_] = (out, sel_m)

            def scatter(e_, y_m, x_m):
                i = e_ % 2
                new = []
                for t in range(2):
                    for h in range(2):
                        b, fr = take()
                        w = SELT[i][:, 128 * t:128 * t + 128]
                        P(lambda e: e.matmul(b[:, :], w, YH[:, 512 * h:512 * h + 512], start=True, stop=False),
                          y_m, got[e_][1], fr, sig=False)
                        m = P(lambda e: e.matmul(b[:, :], w, YL[:, 512 * h:512 * h + 512], start=False, stop=True))
                        o = XV[:, t, 512 * h:512 * h + 512]
                        m2 = V(lambda e: e.scalar_tensor_tensor(o, b[:, :], gw[:, 8 * t + e_:8 * t + e_ + 1], o,
                                                                ALU.mult, ALU.add), m, gm, x_m)
                        give(b, m2)
                        new.append(m2)
                y_free[0] = m
                g_free[i][2] = m
                return new

            gather(0)
            late = None
            for e_ in range(8):
                lhs = [v[:, :].rearrange("p (k n) -> p k n", k=8) for v in (GH[e_ % 2], GL[e_ % 2])]
                turn, u_m = swiglu(lhs, [got[e_][0]] * 8, E_CHUNKS[:1], 1, EV)
                if late:
                    x_m = scatter(e_ - 1, late, x_m)
                if e_ < 7:
                    gather(e_ + 1)
                turn2, u_m2 = swiglu(lhs, [got[e_][0]] * 8, E_CHUNKS[1:], 1, EV, turn)
                y_m = []

                def sink(t, h, b, m):
                    y_m.append(parts([YH[:, 512 * h:512 * h + 512], YL[:, 512 * h:512 * h + 512]], b[:, :], m,
                                     y_free[0]))
                    return y_m[-1]
                down(EV, lambda k: u_m(k) if k < 4 else u_m2(k), 28, 1, sink, turn2)
                late = y_m
            return scatter(7, late, x_m)

        bg_m = G(lambda e: e.tensor_scalar(VECS[:, VEC["b_gate"]:VEC["b_gate"] + 32],
                                           VECS[:, VEC["b_gate"]:VEC["b_gate"] + 32], 0.5, None, ALU.mult), small_m)
        bias_m = bg_m
        bias_marks = bias_two(x_m)
        for l in range(2):
            plan(layer_two_slots(l))
            x_f = to_features(XV, HV, x_m)
            R = [U[:, 1024 * i:1024 * i + 1024] for i in range(7)]
            XM, XC, ZT, QM, KM, VM, VT = R

            def pairs(dst, out, scale=None, wait=None):
                def sink(c, b, m):
                    m = evac(dst[:, 512 * c:512 * c + 512], b[:, :], m, wait, scale=scale)
                    out.append(m)
                    return m
                return sink
            q_m, k_m, v_m, xm_m, z_m = [], [], [], [], []
            for c in range(2):
                by_features([HV], [x_f], 8, 1, 256, pairs(QT[:, 512 * c:512 * c + 512], q_m, 0.125))
            for c in range(2):
                by_features([HV], [x_f], 8, 1, 256, pairs(QT[:, 1024 + 512 * c:1536 + 512 * c], k_m))

            def vsink(t, b, m):
                m = evac(QT[:, 2048 + 512 * t:2560 + 512 * t], b[:, :], m)
                v_m.append(m)
                return m
            by_tokens(HV, x_f, 512, vsink)
            sc, va = attention(
                lambda h, t: QT[64 * (h % 2):64 * (h % 2) + 64,
                                256 * (h // 2) + 128 * t:256 * (h // 2) + 128 * t + 128],
                lambda h: QT[64 * (h % 2):64 * (h % 2) + 64, 1024 + 256 * (h // 2):1280 + 256 * (h // 2)],
                lambda h, i: QT[:, 2048 + 512 * i + 64 * h:2112 + 512 * i + 64 * h],
                lambda h, t: BIAS[:, 256 * h + 128 * (1 - t):256 * h + 256], lambda t: t + 1, q_m, k_m, v_m)
            sc(0)
            for c in range(2):
                by_features([HV], [x_f], 8, 1, 256, pairs(XM[:, 512 * c:512 * c + 512], xm_m, wait=bias_marks))

            def zsink(i, b, m):
                z = ZT[:, 512 * c:512 * c + 512]
                m = A(lambda e: e.activation(z, b[:, :], ACT.Tanh, scale=0.5), m, bias_marks)
                z_m.append(V(lambda e: e.tensor_scalar(z, z, 1.0, 0.5, ALU.add, ALU.mult), m))
                return m
            for c in range(2):
                by_features([HV], [x_f], 8, 1, 256, zsink)
            sc(1)
            gate_steps = gates(HV, x_f, VECS[:, VEC["b_gate"] + 16 * l:VEC["b_gate"] + 16 * l + 16])
            xc_m = []
            for h in range(4):
                c = XC[:, 256 * h:256 * h + 256]
                xm = XM[:, 256 * h:256 * h + 256]

                def cw(j, h=h):
                    a = VEC["conv_w"] + 16 * l + 4 * j + h
                    return VECS[:, a:a + 1]
                cb = VECS[:, VEC["conv_b"] + 4 * l + h:VEC["conv_b"] + 4 * l + h + 1]
                m = V(lambda e, c=c, xm=xm, cw=cw, cb=cb: e.tensor_scalar(c, xm, cw(3), cb, ALU.mult, ALU.add),
                      xm_m, small_m)
                for d in (1, 2, 3):
                    m = V(lambda e, c=c, xm=xm, cw=cw, d=d: e.scalar_tensor_tensor(
                        c[:, d:256], xm[:, 0:256 - d], cw(3 - d), c[:, d:256], ALU.mult, ALU.add), m)
                tt = KM[:, 256 * h:256 * h + 256]
                m1 = A(lambda e, c=c, tt=tt: e.activation(tt, c, ACT.Tanh, scale=0.5), m)
                xc_m.append(V(lambda e, c=c, tt=tt: e.scalar_tensor_tensor(c, tt, 1.0, c, ALU.add, ALU.mult), m1))
            next(gate_steps)
            next(gate_steps)
            next(gate_steps)
            next(gate_steps)
            gt_m = (A.sem, A.n)
            oa = [v[:, 0:4, :] for v in HV]
            ob = [v[:, 4:8, :] for v in HV]
            oam = [va(0, oa)]

            slot, _, wm, done = next_weights()
            wqk = slot[:, 0:1024].rearrange("p (a n) -> p a n", a=8)
            wv = slot[:, 1024:1536].rearrange("p (a n) -> p a n", a=4)
            wif = slot[:, 1536:1632].rearrange("p (a n) -> p a n", a=12)
            got = {}
            for key, w0, src, dst, scale, ms in (("q", 0, XC, QM, 0.5, xc_m), ("k", 4, XC, KM, 0.5, xc_m),
                                                 ("v", None, XM, VM, None, xm_m)):
                for h2 in range(2):
                    b, fr = take()
                    for h in (2 * h2, 2 * h2 + 1):
                        w = wv[:, h, :] if w0 is None else wqk[:, w0 + h, :]
                        m = mm(b[:, 256 * (h % 2):256 * (h % 2) + 256], w, src[:, 256 * h:256 * h + 256],
                               True, True, wm, ms, fr, sig=(h % 2 == 1))
                    m = evac(dst[:, 512 * h2:512 * h2 + 512], b[:, :], m, scale=scale)
                    give(b, m)
                    got.setdefault(key, []).append(m)
            vt_m = []
            for t in range(2):
                b, fr = take()
                for h in range(4):
                    m = mm(b[:, 128 * h:128 * h + 128], XM[:, 256 * h + 128 * t:256 * h + 128 * t + 128],
                           wv[:, h, :], True, True, wm, xm_m, fr, sig=(h == 3))
                m = evac(VT[:, 512 * t:512 * t + 512], b[:, :], m)
                give(b, m)
                vt_m.append(m)
            IF = SM[:, 484:500].rearrange("p (t n) -> p t n", t=2)
            FL = small(8).rearrange("p (t n) -> p t n", t=2)
            ab, lg = small(8), small(8)
            b, fr = take()
            for t in range(2):
                n = 0
                for key, src in (("q", QM), ("k", KM), ("v", VM)):
                    for h in range(4):
                        m = mm(b[:, 8 * t:8 * t + 8], src[:, 256 * h + 128 * t:256 * h + 128 * t + 128],
                               wif[:, n, :], n == 0, n == 11, got[key], fr, wm, sig=(n == 11 and t == 1))
                        n += 1
            done(m)
            m = V(lambda e, b=b: e.tensor_tensor(IF, b[:, 0:16].rearrange("p (t n) -> p t n", t=2),
                                            ROW[:, None, 272 + 8 * l:280 + 8 * l].to_broadcast([128, 2, 8]),
                                            ALU.add), m)
            give(b, m)
            fp = IF[:, :, 4:8]
            abv = ab.rearrange("p (t n) -> p t n", t=2)
            m1 = V(lambda e: e.scalar_tensor_tensor(abv, fp, -1.0, fp, ALU.mult, ALU.max), m)
            m1 = A(lambda e: e.activation(ab, ab, ACT.Exp, scale=-1.0), m1)
            m1 = A(lambda e: e.activation(lg, ab, ACT.Ln, bias=1.0), m1)
            if_m = V(lambda e: e.scalar_tensor_tensor(FL, fp, 0.0, lg.rearrange("p (t n) -> p t n", t=2),
                                                      ALU.min, ALU.subtract), m1)
            FN = small(8).rearrange("p (t n) -> p t n", t=2)
            fn_m = V(lambda e: e.tensor_scalar(FN, FL, -1.0, None, ALU.mult), if_m)
            oam.append(va(1, oa))
            b, fr = take()
            m = mm(b[:, 0:4], tri, FL[:, 0, :], True, True, if_m, fr)
            m = mm(b[:, 4:8], ones, FL[:, 0, :], True, False)
            m = mm(b[:, 4:8], tri, FL[:, 1, :], False, True, sig=True)
            BC = SM[:, 500:508]
            bc_m = V(lambda e, b=b: e.tensor_copy(BC, b[:, 0:8]), m)
            give(b, bc_m)
            rows = []
            for h2 in range(2):
                b, fr = take()
                for h in (2 * h2, 2 * h2 + 1):
                    o = 256 * (h % 2)

                    def bc(v, t, c):
                        return v[:, t, c:c + 1].to_broadcast([128, 128])
                    mm(b[:, o:o + 128], bc(IF, 0, h), ident, True, False, fn_m, fr)
                    mm(b[:, o:o + 128], bc(FN, 0, h), tri, False, True)
                    mm(b[:, o + 128:o + 256], bc(IF, 1, h), ident, True, False)
                    mm(b[:, o + 128:o + 256], bc(FN, 0, h), ones, False, False)
                    m = mm(b[:, o + 128:o + 256], bc(FN, 1, h), tri, False, True, sig=(h % 2 == 1))
                rows.append((b, m))
            mst = {}
            for t in range(2):
                n = 128 * (t + 1)
                mx, nm = small(4), small(4)
                L = LB[t]
                for h in range(4):
                    b, rm = rows[h // 2]
                    m = V(lambda e, h=h, b=b: e.tensor_tensor_reduce(
                        L[:, 256 * h:256 * h + n], b[:, 256 * (h % 2):256 * (h % 2) + n],
                        CST[:, C_CAUS + 256 - n:C_CAUS + 256], 1.0, 0.0, ALU.add, ALU.max, mx[:, h:h + 1]),
                        rm, oam)
                    if t == 1 and h % 2:
                        give(b, m)
                m = V(lambda e: e.tensor_scalar(nm, mx, -1.0, None, ALU.mult), m)
                em = []
                for h in range(4):
                    em.append(A(lambda e, h=h: e.activation(L[:, 256 * h:256 * h + n], L[:, 256 * h:256 * h + n],
                                                            ACT.Exp, bias=nm[:, h:h + 1]), m))
                gd = small(4)
                m = V(lambda e, t=t: e.tensor_tensor(gd, nm, BC[:, 4 * t:4 * t + 4], ALU.subtract), m, bc_m)
                gd_m = A(lambda e: e.activation(gd, gd, ACT.Exp), m)
                nq = small(4)
                pm = []
                for h2 in range(2):
                    b, fr = take()
                    for h in (2 * h2, 2 * h2 + 1):
                        o = 256 * (h % 2)
                        m = mm(b[:, o:o + n], QM[:, 256 * h + 128 * t:256 * h + 128 * t + 128],
                               KM[:, 256 * h:256 * h + n], True, True, fr, sig=(h % 2 == 1))
                    for h in (2 * h2, 2 * h2 + 1):
                        o = 256 * (h % 2)
                        m = V(lambda e, h=h, b=b, o=o: e.scalar_tensor_tensor(
                            L[:, 256 * h:256 * h + n], b[:, o:o + n], 128 ** -0.5, L[:, 256 * h:256 * h + n],
                            ALU.mult, ALU.mult, accum_out=nq[:, h:h + 1]), m, em[h])
                        pm.append(m)
                    give(b, m)
                m = V(lambda e: e.scalar_tensor_tensor(nq, nq, -1.0, nq, ALU.mult, ALU.max), m)
                m = V(lambda e: e.tensor_tensor(nq, nq, gd, ALU.max), m, gd_m)
                rq = small(4)
                m = V(lambda e: e.reciprocal(rq, nq), m)
                mst[t] = (pm, rq, m)
            obm = []
            for t in range(2):
                pm, rq, rqm = mst[t]
                L = LB[t]
                kts = t + 1
                tm = transpose_p(lambda h, i: L[:, 256 * h + 128 * i:256 * h + 128 * i + 128], 4, kts, pm)
                b, fr = take()
                for h in range(4):
                    for i in range(kts):
                        m = mm(b[:, 128 * h:128 * h + 128], PT[:, 128 * (h * kts + i):128 * (h * kts + i) + 128],
                               VT[:, 512 * i + 128 * h:512 * i + 128 * h + 128], i == 0, i == kts - 1,
                               tm[h * kts + i], vt_m, fr, sig=(h == 3 and i == kts - 1))
                pt_free[0] = m
                o = O[:, 512 * t:512 * t + 512]
                ov = o.rearrange("p (h d) -> p h d", h=4)
                m = V(lambda e, ov=ov, b=b, rq=rq: e.tensor_tensor(
                    ov, b[:, :].rearrange("p (h d) -> p h d", h=4),
                    rq[:, :, None].to_broadcast([128, 4, 128]), ALU.mult), m, rqm, oam)
                give(b, m)
                st, ag, ve, rs = small(24), small(8), small(4), small(4)
                for h in range(4):
                    m2 = V(lambda e, h=h: e.bn_stats(st[:, 6 * h:6 * h + 6], o[:, 128 * h:128 * h + 128]), m)
                for h in range(4):
                    m3 = V(lambda e, h=h: e.bn_aggr(ag[:, 2 * h:2 * h + 2], st[:, 6 * h:6 * h + 6]), m2)
                m4 = V(lambda e: e.tensor_scalar(ve, ag.rearrange("p (h a) -> p h a", a=2)[:, :, 1], LN_EPS, None,
                                                 ALU.add), m3)
                m4 = rpow(rs, ve, m4)
                for h in range(4):
                    m = V(lambda e, h=h: e.tensor_scalar(o[:, 128 * h:128 * h + 128], o[:, 128 * h:128 * h + 128],
                                                         ag[:, 2 * h:2 * h + 1], rs[:, h:h + 1],
                                                         ALU.subtract, ALU.mult), m4)
                b, fr = take()
                for c in range(4):
                    m2 = tr(b[:, 128 * c:128 * c + 128], o[:, 128 * c:128 * c + 128], m, fr, sig=(c == 3))
                for h in range(4):
                    g = VECS[:, VEC["m_g"] + 4 * l + h:VEC["m_g"] + 4 * l + h + 1]
                    m = V(lambda e, h=h, g=g, b=b, t=t: e.scalar_tensor_tensor(
                        o[:, 128 * h:128 * h + 128], b[:, 128 * h:128 * h + 128], g,
                        ZT[:, 256 * h + 128 * t:256 * h + 128 * t + 128], ALU.mult, ALU.mult), m2, z_m)
                give(b, m)
                obm.append(parts([d[:, :, 128 * t:128 * t + 128] for d in ob],
                                 o.rearrange("p (c n) -> p c n", c=4), m))

            mm_ = mix(oa, ob, [oam] * 4, [obm] * 4, gt_m)
            sink, new = add_to_x(x_m, alpha=ALPHA)
            down([d[:, :].rearrange("p (c n) -> p c n", c=8) for d in (MH, ML)], lambda k: mm_[k], 8, 2, sink)
            x_m = layer_norm(l, 0, new)
            x_f = to_features(XV, HV, x_m)
            if l == 0:
                turn, u_m = swiglu(HV, x_f, F_CHUNKS, 2, FV)
                sink, new = add_to_x([x_m, x_f], alpha=ALPHA)
                down(FV, u_m, 22, 2, sink, turn)
                x_m = new
            else:
                gw, pos = SM[:, 484:500], SM[:, 512:528]
                gm = []
                sm = []
                se = small(16)
                xs_m = [parts([d[:, 1024 * t:1024 * t + 1024] for d in (XH, XL)], XV[:, t, :], x_m) for t in range(2)]
                for t in range(2):
                    b, fr = take()
                    for k in range(8):
                        m = mm3(b[:, 0:8], [v[:, k, 128 * t:128 * t + 128] for v in HV],
                                [RWS[:, 64 * i + 8 * k:64 * i + 8 * k + 8] for i in range(2)], k == 0, k == 7,
                                x_f[k], fr, rws_m, sig=(k == 7))
                    lo, s1, f1, s2, tmp = small(8), small(8), small(8), small(8), small(8)
                    v1, v2, d, a1, a2, i1 = (small(1) for _ in range(6))
                    io = CST[:, C_IOTA:C_IOTA + 8]
                    m = V(lambda e, b=b: e.tensor_tensor(lo, b[:, 0:8], ROW[:, 288:296], ALU.add), m)
                    give(b, m)

                    def first_of(src, val, sel, m):
                        m = V(lambda e: e.tensor_reduce(val, src, AX.X, ALU.max), m)
                        m = V(lambda e: e.scalar_tensor_tensor(tmp, src, val[:, 0:1], io, ALU.is_equal, ALU.mult), m)
                        m = V(lambda e: e.tensor_reduce(i1, tmp, AX.X, ALU.max), m)
                        return V(lambda e: e.tensor_scalar(sel, io, i1[:, 0:1], None, ALU.is_equal), m)
                    m = first_of(lo, v1, s1, m)
                    m = V(lambda e: e.scalar_tensor_tensor(f1, s1, -3e38, lo, ALU.mult, ALU.add), m)
                    m = first_of(f1, v2, s2, m)
                    sm.append(V(lambda e, t=t: e.tensor_tensor(se[:, 8 * t:8 * t + 8], s1, s2, ALU.add), m))
                    m = V(lambda e: e.tensor_tensor(d, v2, v1, ALU.subtract), m)
                    m = A(lambda e: e.activation(d, d, ACT.Exp), m)
                    m = V(lambda e: e.tensor_scalar(a1, d, 2.0, 2.0, ALU.mult, ALU.add), m)
                    m = V(lambda e: e.reciprocal(a1, a1), m)
                    m = V(lambda e: e.tensor_tensor(a2, a1, d, ALU.mult), m)
                    m = V(lambda e: e.tensor_scalar(s1, s1, a1[:, 0:1], None, ALU.mult), m)
                    m = V(lambda e, t=t: e.scalar_tensor_tensor(gw[:, 8 * t:8 * t + 8], s2, a2[:, 0:1], s1,
                                                                ALU.mult, ALU.add), m)
                    gm.append(m)
                b, fr = take()
                mm(b[:, 0:8], tri, se[:, 0:8], True, True, sm, fr)
                mm(b[:, 8:16], ones, se[:, 0:8], True, False)
                m = mm(b[:, 8:16], tri, se[:, 8:16], False, True, sig=True)
                m = V(lambda e: e.tensor_tensor(pos, b[:, 0:16], se, ALU.mult), m)
                pos_m = V(lambda e: e.tensor_scalar(pos, pos, -1.0, None, ALU.add), m)
                give(b, m)
                pre = V(lambda e: e.tensor_scalar(X[:, :], X[:, :], ALPHA, None, ALU.mult), x_m, x_f, xs_m)
                b, fr = take()
                mm(b[:, 0:8], ones, se[:, 0:8], True, False, sm, fr)
                m = mm(b[:, 0:8], ones, se[:, 8:16], False, True, sig=True)
                most = small(1)
                m = V(lambda e: e.tensor_reduce(most, b[:, 0:8], AX.X, ALU.max), m)
                give(b, m)
                flag_m = V(lambda e: e.tensor_scalar(FLAG[:, :], most, 128.0, None, ALU.is_gt), m)
                first = ws_d.shape[0] - 128 * sum(slot_words(s) for i in range(8) for s in expert_slots(i))
                x_m = experts(0, pos, gw, pos_m, gm, xs_m, [pre])
                x_m = rest_of_tokens(first, pos, gw, flag_m, x_m)
            x_m = layer_norm(l, 1, x_m)

        out_m = load("out", out_d.rearrange("a (t p) n -> p (a t) n", p=128), XV, x_m, q=S)

        S.wait([out_m, scr_m])


def kernel(**inputs):
    import numpy as _np
    import concourse.bacc as _bacc
    from concourse import mybir as _mybir
    from concourse.bass_utils import run_bass_kernel_spmd as _run

    I = {k: _np.asarray(v) for k, v in inputs.items()}

    def tiles(w):
        return w.reshape(w.shape[0] // 128, 128, w.shape[1]).transpose(1, 0, 2)

    def lay(s, l):
        if s != "mlstm":
            return _np.stack([tiles(I[n][idx][128 * r0:128 * r1, c0:c1]) for n, idx, r0, r1, c0, c1 in s], axis=2)
        return _np.concatenate([I["w_qk_m_2"][l].reshape(8, 128, 128).transpose(1, 0, 2).reshape(128, -1),
                                I["w_v_m_2"][l].transpose(1, 0, 2).reshape(128, -1),
                                tiles(I["w_if_2"][l]).reshape(128, -1)], axis=1)

    ws = _np.concatenate([lay(s, l).ravel() for f in (layer_one_slots, layer_two_slots) for l in range(2)
                          for s in f(l)])

    def cols(a):
        return a.reshape(-1, 128).T
    twice = lambda a: _np.concatenate([a, a])
    vec = _np.ascontiguousarray(_np.concatenate(
        [cols(I[n]) for n in ("attn_norm_g", "ffn_norm_g", "b_gate_2", "conv_w_2", "conv_b_2", "m_norm_g_2")]
        + [_np.stack([twice(I[n][l]) for l in range(2) for n in ("q_norm_b", "k_norm_b")], axis=1)], axis=1))
    row = _np.concatenate([I["q_norm_a"][0], I["k_norm_a"][0], I["q_norm_a"][1], I["k_norm_a"][1],
                           I["sink_a"].ravel(), I["b_if_2"].ravel(), I["router_b_2"].ravel()])
    ln = _np.ascontiguousarray(_np.stack([I["ln_g_2"], I["ln_b_2"]], axis=2)).ravel()
    relb = _np.zeros((2, 8, 15, 127), _np.float32)
    relb[..., 48:79] = I["rel_bias_b"]
    one, lnc = distance_constants()
    arrays = {"x": I["x"], "pos": _np.ascontiguousarray(I["positions"].reshape(2, 128).T), "ws": ws, "vec": vec, "row": row, "ln": ln,
              "rel": I["rel_bias_2"], "relb": relb,
              "rw": _np.ascontiguousarray(tiles(I["router_w_2"][0]).reshape(128, 64)),
              "cst": constants(), "one": one, "lnc": lnc}
    nc = _bacc.Bacc("TRN2", target_bir_lowering=False, num_devices=1)
    ins, args = {}, []
    for name, a in arrays.items():
        a = _np.ascontiguousarray(a)
        ins[f"in_{name}"] = a
        args.append(nc.dram_tensor(f"in_{name}", a.shape, _mybir.dt.from_np(a.dtype), kind="ExternalInput").ap())
    out = nc.dram_tensor("out_0", (1, 256, 1024), _mybir.dt.float32, kind="ExternalOutput").ap()
    program(nc, *args, out)
    r = _run(nc, [ins], core_ids=[0])
    return r.results[0]["out_0"]
```

```python
import concourse.bass as bass
from concourse import mybir
from contextlib import ExitStack
import math
import numpy as np

NEG = -1e30
EPS = 1e-6
LN_EPS = 1e-5
ALPHA = 4.0 ** 0.25
NRAW = 3
NSET = 3
SLOT = 2048
F_CHUNKS = [(512 * i, 512 * i + 512) for i in range(5)] + [(2560, 2816)]
E_CHUNKS = [(512 * i, 512 * i + 512) for i in range(7)]



def tall(name, index, c0, c1):
    if c1 - c0 <= 256:
        return [[(name, index, 0, 8, c0, c1)]]
    return [[(name, index, 4 * i, 4 * i + 4, c0, c1)] for i in range(2)]


def wide(name, index, tiles):
    return [[(name, index, k, k + 2, 0, 1024)] for k in range(0, tiles, 2)]


def hidden(gate, up, chunks):
    s = []
    for c0, c1 in chunks:
        for name, index, off in (gate, up):
            s += tall(name, index, off + c0, off + c1)
    return s


def layer_one_slots(l):
    i = (l,)
    s = []
    for a, b in ((0, 512), (512, 768), (768, 1280), (1280, 1792), (1792, 2304)):
        s += tall("w_in", i, a, b)
    for j in range(8):
        s.append([("w_in", i, 0, 8, 2304 + 128 * j, 2432 + 128 * j), ("w_in", i, 0, 8, 3328 + 128 * j, 3456 + 128 * j)])
    for j in range(4):
        s.append([(n, i, 0, 4, 256 * j, 256 * j + 256) for n in ("w_proj_a", "w_proj_b")])
    s += wide("w_out", i, 8)
    s += hidden(("w_gate", i, 0), ("w_up", i, 0), F_CHUNKS)
    return s + wide("w_down", i, 22)


def expert_slots(e):
    i = (0, e)
    return hidden(("exp_w13_2", i, 0), ("exp_w13_2", i, 3584), E_CHUNKS) + wide("exp_w2_2", i, 28)


def layer_two_slots(l):
    i = (l,)
    s = []
    s += tall("w_in_2", i, 1024, 1536)
    for j in range(4):
        s += tall("w_in_2", i, 256 * j, 256 * j + 256)
    for j in range(4):
        s += tall("w_in_2", i, 1536 + 256 * j, 1792 + 256 * j)
    for j in range(8):
        s.append([("w_gate_2", i, 0, 8, 1024 * k + 128 * j, 1024 * k + 128 * j + 128) for k in range(2)])
        if j == 2:
            s.append("mlstm")
    for j in range(4):
        s.append([(n, i, 0, 4, 256 * j, 256 * j + 256) for n in ("w_br_a_2", "w_br_m_2")])
    s += wide("w_o_2", i, 8)
    if l == 0:
        s += hidden(("ffn_w13_2", (0,), 0), ("ffn_w13_2", (0,), 2816), F_CHUNKS)
        s += wide("ffn_w2_2", (0,), 22)
    else:
        for e in range(8):
            s += expert_slots(e)
    return s


def slot_words(s):
    if s == "mlstm":
        return 8 * 128 + 4 * 128 + 96
    return sum((r1 - r0) * (c1 - c0) for _, _, r0, r1, c0, c1 in s)


VEC = {}
_at = 0
for _n, _c in (("b_gate", 32), ("conv_w", 32), ("conv_b", 8), ("m_g", 8), ("qk_b", 4)):
    VEC[_n] = _at
    _at += _c
NVEC = _at
ROWV = 4 * 64 + 16 + 16 + 8
C_ID, C_J, C_JJ, C_ONE, C_TRI, C_CAUS, C_MA, C_MB, C_INV, C_IOTA, C_ROW = 0, 128, 256, 384, 512, 640, 896, 1408, 1472, 1504, 1512
NCONST = 1640


def constants():
    c = np.zeros((128, NCONST), np.float32)
    p = np.arange(128)[:, None]
    q = np.arange(128)[None, :]
    c[:, C_ID:C_ID + 128] = p == q
    c[:, C_J:C_J + 128] = p + q == 127
    c[:, C_JJ:C_JJ + 128] = (p // 64 == q // 64) & (p % 64 + q % 64 == 63)
    c[:, C_ONE:C_ONE + 128] = 1.0
    c[:, C_TRI:C_TRI + 128] = p <= q
    c[:, C_CAUS + 128:C_CAUS + 256] = np.where(q <= p, 0.0, NEG)
    c[:, C_MA + 128:C_MA + 256] = np.where(q <= p, 0.0, NEG)
    c[:, C_MA + 256:C_MA + 384] = np.where(q >= p, 0.0, NEG)
    k = np.arange(64)[None, :]
    cs = np.clip(p % 64 - 8, 0, 48)
    c[:, C_MB:C_MB + 64] = np.where((k >= cs) & (k < cs + 16), 0.0, NEG)
    c[:, C_INV:C_INV + 32] = (10000.0 ** (-np.arange(32) / 32)).astype(np.float32)[None, :]
    c[:, C_IOTA:C_IOTA + 8] = 8.0 - np.arange(8)[None, :]
    c[:, C_ROW:C_ROW + 128] = q
    return c


def distance_constants():
    one = np.zeros((32, 384), np.float32)
    ln = np.full((8, 384), NEG, np.float32)
    for j in range(256):
        d = 255 - j
        if d < 16:
            b = d
        else:
            b = min(31, 16 + int(np.float32(np.log(np.float32(d) / np.float32(16))) / math.log(2048 / 16) * 16))
        one[b, j] = 1.0
        n = (d <= 128) + (d % 4 == 0) + (d % 16 == 0)
        if n:
            ln[:, j] = math.log(n)
    return one, ln


def program(nc, x_d, pos_d, ws_d, vec_d, row_d, ln_d, rel_d, relb_d, rw_d, cst_d, one_d, lnc_d, out_d):
    f32 = mybir.dt.float32
    ALU = mybir.AluOpType
    ACT = mybir.ActivationFunctionType
    AX = mybir.AxisListType

    scr = nc.dram_tensor("scratch_rel", (8, 384), f32).ap()

    ctx = ExitStack()
    with ctx:
        def sb(name, n, dt=f32):
            return ctx.enter_context(nc.sbuf_tensor(name, [128, n], dt))

        class Queue:

            def __init__(self, engine, name):
                self.e = engine
                self.sem = ctx.enter_context(nc.semaphore(name))
                self.n = 0
                self.seen = {}

            def wait(self, waits):
                for sem, v in flat(waits):
                    if self.seen.get(id(sem), 0) < v:
                        self.e.wait_ge(sem, v)
                        self.seen[id(sem)] = v

            def __call__(self, fn, *waits, sig=True):
                self.wait(waits)
                ins = fn(self.e)
                if sig:
                    ins.then_inc(self.sem, 1)
                    self.n += 1
                    return (self.sem, self.n)

            def dma(self, out, in_, mark, *waits):
                self.wait(waits)
                self.e.dma_start(out, in_).then_inc(mark[0], 16)
                return mark

        def flat(ws):
            out = []
            for w in ws:
                if w is None:
                    continue
                if isinstance(w, list):
                    out += flat(w)
                else:
                    out.append(w)
            return out

        P, V, A = Queue(nc.tensor, "s_pe"), Queue(nc.vector, "s_dve"), Queue(nc.scalar, "s_act")
        G, S = Queue(nc.gpsimd, "s_pool"), Queue(nc.sync, "s_sp")

        f32r = mybir.dt.float32r
        class Slot:

            def __init__(self, name, room, once=False):
                self.room = room
                self.once = once
                self.sem = ctx.enter_context(nc.semaphore("s_" + name))
                self.n = 0
                self.free = None

        slots = [Slot(f"raw{i}", sb(f"raw{i}", SLOT)) for i in range(NRAW)]
        sets = [(sb(f"wh{i}", SLOT, f32r), sb(f"wl{i}", SLOT, f32r)) for i in range(NSET)]
        set_free = [None] * NSET
        rest_sems = {n: ctx.enter_context(nc.semaphore("s_rest_" + n)) for n in "pvag"}
        X = sb("X", 2048)
        h_at = (nc.sbuf_base + 31) // 32 * 32
        HH, HL = sb("HH", 2048, f32r), sb("HL", 2048, f32r)
        BIAS = sb("BIAS", 3072)
        CST = sb("CST", NCONST)
        VECS = sb("VECS", NVEC)
        ROW = sb("ROW", ROWV)
        RW = sb("RW", 64)
        RWS = sb("RWS", 128, f32r)
        CS = sb("CS", 512)
        TRIG = sb("TRIG", 192)
        SM = sb("SM", 544)
        FLAG = sb("FLAG", 1, mybir.dt.int32)
        POSI = sb("POSI", 2, mybir.dt.int32)
        arena_at = (nc.sbuf_base + 31) // 32 * 32
        ARENA = sb("ARENA", 22016)

        def at(name, offset, n, dt=f32):
            assert offset + n <= 22016
            return nc.alloc_sbuf_tensor_at(name, [128, n], dt, offset=arena_at + 4 * offset)

        U = at("U", 0, 7168)
        GT = at("GT", 7168, 4096)
        LB = [at("L0", 11264, 2048), at("L1", 13312, 2048)]
        PT = at("PT", 15360, 2048)
        QT = at("QT", 17408, 3584)
        O = at("O", 20992, 1024)
        MH, ML = at("MH", 0, 2048, f32r), at("ML", 2048, 2048, f32r)
        FH, FL_ = at("FH", 0, 5632, f32r), at("FL", 5632, 5632, f32r)
        TT = [at("TT0", 11264, 512), at("TT1", 11776, 512)]
        LNB = at("LNB", 14336, 2048)
        GR = LNB[:, 0:1024]
        more = [Slot(f"more{i}", at(f"more{i}", 16384 + 2048 * i, SLOT)) for i in range(2)]
        TU = [at("TU0", 13312, 512), at("TU1", 13824, 512)]
        spare = [Slot(f"spare{i}", nc.alloc_sbuf_tensor_at(f"spare{i}", [128, SLOT], f32, offset=h_at + 4 * SLOT * i))
                for i in range(2)]
        once = [Slot(f"once{i}", at(f"once{i}", a, SLOT), True) for i, a in enumerate((0, 2048, 4096, 14336))]
        EH, EL = at("EH", 0, 3584, f32r), at("EL", 3584, 3584, f32r)
        XH, XL = at("XH", 7168, 2048, f32r), at("XL", 9216, 2048, f32r)
        YH, YL = at("YH", 14336, 1024, f32r), at("YL", 15360, 1024, f32r)
        GH = [at(f"GH{i}", 16384 + 1024 * i, 1024, f32r) for i in range(2)]
        GL = [at(f"GL{i}", 18432 + 1024 * i, 1024, f32r) for i in range(2)]
        SEL = [at(f"SEL{i}", 20480 + 256 * i, 256) for i in range(2)]
        SELR = [at(f"SELR{i}", 20992 + 256 * i, 256, f32r) for i in range(2)]
        SELT = [at(f"SELT{i}", 21504 + 256 * i, 256, f32r) for i in range(2)]
        banks = [ctx.enter_context(nc.psum_tensor(f"bank{i}", [128, 512], f32)) for i in range(8)]
        free_banks = [(b, None) for b in banks]

        def take():
            return free_banks.pop(0)

        def give(b, *marks):
            free_banks.append((b, flat(marks)))

        ident = CST[:, C_ID:C_ID + 128]
        ones = CST[:, C_ONE:C_ONE + 128]
        tri = CST[:, C_TRI:C_TRI + 128]
        XV = X[:, :].rearrange("p (t n) -> p t n", t=2)
        HV = tuple(h[:, :].rearrange("p (k n) -> p k n", k=8) for h in (HH, HL))

        small_at = [0]

        def small(n):
            if small_at[0] + n > 448:
                small_at[0] = 0
            a = small_at[0]
            small_at[0] += n
            return SM[:, a:a + n]

        HALF = SM[:, 448:449]
        PW = SM[:, 449:481]

        one_sem = {}

        def load(name, out, in_, *waits, q=None):
            if name not in one_sem:
                one_sem[name] = [ctx.enter_context(nc.semaphore("s_" + name)), 0]
            one_sem[name][1] += 16
            (q or A).dma(out, in_, (one_sem[name][0], one_sem[name][1]), *waits)
            return (one_sem[name][0], one_sem[name][1])

        x_m = [load(f"x{t}", XV[:, t, :], x_d[0, 128 * t:128 * t + 128, :], q=S) for t in range(2)]
        cst_m = load("cst", CST[:, :], cst_d)
        load("small", VECS[:, :], vec_d)
        load("small", ROW[:, :], bass.AP(row_d.tensor, 0, [[0, 128], [1, ROWV]]))
        load("small", RW[:, :], rw_d)
        load("small", POSI[:, :], pos_d)
        load("small", PT[0:32, 0:384], one_d)
        load("small", PT[0:32, 384:392], rel_d)
        small_m = load("small", PT[0:8, 512:896], lnc_d)

        offset = [0]
        count = [0]
        held = [0]
        pending = []
        ready = []

        def plan(slots):
            pending.extend(slots)

        def fetch():
            s = pending.pop(0)
            n = slot_words(s)
            r = slots.pop(0)
            if not r.once:
                slots.append(r)
            r.n += 16
            mark = (r.sem, r.n)
            raw = r.room
            S.dma(raw[:, 0:n], bass.AP(ws_d.tensor, offset[0], [[n, 128], [1, n]]), mark, r.free)
            offset[0] += 128 * n
            if s == "mlstm":
                def done(m):
                    r.free = m
                ready.append((raw, None, mark, done))
                return
            j = count[0] % NSET
            count[0] += 1
            h, lo = sets[j]
            ms = []
            for a, b in ((0, n // 2), (n // 2, n)):
                mh = A(lambda e: e.activation(h[:, a:b], raw[:, a:b], ACT.Copy), mark, set_free[j])
                ms.append(mh)
            for i, (a, b) in enumerate(((0, n // 2), (n // 2, n))):
                ml = V(lambda e: e.tensor_tensor(lo[:, a:b], raw[:, a:b], h[:, a:b].bitcast(f32), ALU.subtract),
                       ms[i], mark, set_free[j])
                ms[i] = [ms[i], ml]
            r.free = ml

            def done(m):
                set_free[j] = m
            half = sum(r1 - r0 for _, _, r0, r1, _, _ in s[:1]) // 2
            ready.append((h, lo, lambda k: ms[k // half], done))

        def prefill():
            while len(ready) + held[0] < NSET and pending:
                fetch()

        def next_weights():
            prefill()
            h, lo, wm, done = ready.pop(0)
            held[0] += 1

            def end(m):
                held[0] -= 1
                done(m)
            return h, lo, wm, end

        alt = [0]

        def evac(out, in_, *waits, scale=None, eng=None):
            alt[0] += 1
            if eng is None:
                eng = A if alt[0] % 2 else V
            if eng is A:
                return A(lambda e: e.activation(out, in_, ACT.Copy, scale=1.0 if scale is None else scale), *waits)
            if scale is None:
                return V(lambda e: e.tensor_copy(out, in_), *waits)
            return V(lambda e: e.tensor_scalar(out, in_, scale, None, ALU.mult), *waits)

        def mm(out, l, r, st, sp, *waits, sig=False):
            return P(lambda e: e.matmul(out, l, r, start=st, stop=sp), *waits, sig=sig)

        def mm3(out, l, r, st, sp, *waits, sig=False):
            P(lambda e: e.matmul(out, l[0], r[0], start=st, stop=False), *waits, sig=False)
            P(lambda e: e.matmul(out, l[0], r[1], start=False, stop=False), sig=False)
            return P(lambda e: e.matmul(out, l[1], r[0], start=False, stop=sp), sig=sig)

        def parts(dst, src, *waits, scale=None):
            m = A(lambda e: e.activation(dst[0], src, ACT.Copy, scale=1.0 if scale is None else scale), *waits)
            hi = dst[0].bitcast(f32)
            if scale is None:
                return V(lambda e: e.tensor_tensor(dst[1], src, hi, ALU.subtract), m, *waits)
            return V(lambda e: e.scalar_tensor_tensor(dst[1], src, scale, hi, ALU.mult, ALU.subtract), m, *waits)

        def tr(out, in_, *waits, sig=False):
            return P(lambda e: e.transpose(out, in_, ident), *waits, sig=sig)

        zero = V(lambda e: e.memset(HALF, 0.0))
        zero = V(lambda e: e.memset(PW, -0.5), zero)

        def rpow(out, in_, *waits):
            n = in_.shape[1]
            return G(lambda e: e.tensor_tensor(out, in_, PW[:, 0:n], ALU.pow), zero, *waits)

        def rope_tables():
            F = small(2)
            m = V(lambda e: e.tensor_copy(F, POSI[:, :]), small_m)
            ang = TRIG[:, 0:64]
            for t in range(2):
                m2 = V(lambda e, t=t: e.tensor_scalar(TRIG[:, 32 * t:32 * t + 32], CST[:, C_INV:C_INV + 32],
                                                      F[:, t:t + 1], None, ALU.mult), m, cst_m)
            two_pi = 2 * math.pi
            parts = []
            rest = two_pi
            for _ in range(3):
                e2 = 2.0 ** (math.floor(math.log2(rest)) - 7)
                c = math.floor(rest / e2) * e2
                parts.append(c)
                rest -= c
            parts.append(rest)
            tabs = []
            for j, quarter in enumerate((0.0, 0.25)):
                K = LB[1][:, 64 * j:64 * j + 64]
                R = LB[1][:, 128 + 64 * j:192 + 64 * j]
                m = V(lambda e: e.tensor_scalar(K, ang, 1.0 / two_pi, quarter, ALU.mult, ALU.add), m2)
                m = V(lambda e: e.tensor_scalar(K, K, 12582912.0, None, ALU.add), m)
                m = V(lambda e: e.tensor_scalar(K, K, -12582912.0, None, ALU.add), m)
                src = ang
                for c in parts:
                    m = V(lambda e, c=c, src=src: e.scalar_tensor_tensor(R, K, -c, src, ALU.mult, ALU.add), m)
                    src = R
                if quarter:
                    m = V(lambda e: e.tensor_scalar(R, R, math.pi / 2, None, ALU.add), m)
                pi = 3.1415925
                m = V(lambda e: e.tensor_scalar(R, R, pi, -pi, ALU.min, ALU.max), m)
                dst = TRIG[:, 64 + 64 * j:128 + 64 * j]
                tabs.append(A(lambda e: e.activation(dst, R, ACT.Sin), m))
            return tabs

        def distance_table():
            b, fr = take()
            m = mm(b[0:8, 0:384], PT[0:32, 384:392], PT[0:32, 0:384], True, True, small_m, fr, sig=True)
            m = V(lambda e: e.tensor_tensor(PT[0:8, 512:896], b[0:8, 0:384], PT[0:8, 512:896], ALU.add), m)
            give(b, m)
            return load("scr", scr, PT[0:8, 512:896], m)

        def flip(raw, j, n, after, add=None):
            ms = []
            for c in range(n // 512):
                b, fr = take()
                m = mm(b[:, :], j, raw[:, 512 * c:512 * c + 512], True, True, after, fr, cst_m, sig=True)
                o = BIAS[:, 512 * c:512 * c + 512]
                if add is None:
                    m = evac(o, b[:, :], m)
                else:
                    m = V(lambda e, o=o, b=b: e.tensor_tensor(
                        o.rearrange("p (a k) -> p a k", k=64), b[:, :].rearrange("p (a k) -> p a k", k=64),
                        add[:, None, :].to_broadcast([128, 8, 64]), ALU.add), m)
                give(b, m)
                ms.append(m)
            return ms

        def bias_one_rows(l, waits):
            for s in range(2):
                m = load("bias", QT[64 * s:64 * s + 64, 0:3072].rearrange("p (h k) -> p h k", h=48),
                         bass.AP(relb_d.tensor, (2 * l + s) * 48 * 127, [[1, 64], [127, 48], [1, 64]]), waits, q=S)
            return m

        def bias_two_rows(waits):
            return load("bias", GT[:, 0:2048].rearrange("p (h k) -> p h k", h=8),
                        bass.AP(scr.tensor, 0, [[1, 128], [384, 8], [1, 256]]), scr_m, waits, q=S)

        class Tiles(list):
            pass

        def of(marks, k, t):
            return marks[k][t] if isinstance(marks[k], Tiles) else marks[k]

        def boundary(norm):
            marks = [Tiles([None, None]) for _ in range(8)]
            n_m, src = Tiles([None, None]), [None, None]

            def turn(t):
                for c4 in range(2):
                    b, fr = take()
                    for c in range(4):
                        a = 512 * c4 + 128 * c
                        m = tr(b[:, 128 * c:128 * c + 128], src[t][:, a:a + 128], n_m[t], fr, cst_m, sig=(c == 3))
                    m = parts([d[:, 4 * c4:4 * c4 + 4, 128 * t:128 * t + 128] for d in HV],
                              b[:, :].rearrange("p (c n) -> p c n", c=4), m)
                    give(b, m)
                    for c in range(4):
                        marks[4 * c4 + c][t] = m

            def on_tile(t, m):
                if t == 1:
                    turn(0)
                n_m[t], src[t] = norm(t, m)
            return on_tile, lambda: turn(1), marks, n_m

        def plain(t, m):
            return m, XV[:, t, :]

        def rms(which, l, waits, q=None):
            g_m = load("g", GR, bass.AP(ln_d.tensor, 8192 + 2048 * which + 1024 * l, [[0, 128], [1, 1024]]), waits, q=q)

            def norm(t, m0):
                ss, ms, rs = small(1), small(1), small(1)
                hv = LB[0][:, 1024 * t:1024 * t + 1024]
                m = A(lambda e: e.activation(hv, XV[:, t, :], ACT.Square, accum_out=ss), m0)
                m = V(lambda e: e.tensor_scalar(ms, ss, 1.0 / 1024, EPS, ALU.mult, ALU.add), m)
                m = rpow(rs, ms, m)
                m = V(lambda e: e.scalar_tensor_tensor(hv, XV[:, t, :], rs[:, 0:1], GR, ALU.mult, ALU.mult), m, g_m)
                return m, hv
            return norm

        def wview(slot, k, a, n):
            return tuple(w[:, 0:k * a * n].rearrange("p (k a n) -> p k a n", k=k, a=a) for w in slot)

        def first_products(lhs, marks, n, bs, between):
            ws = [next_weights() for _ in range(2)]
            for t in range(2):
                b, fr = bs[t]
                for i, (h, lo, wm, done) in enumerate(ws):
                    w = wview((h, lo), 4, 1, n)
                    for k in range(4):
                        m = mm3(b[:, 0:n], [v[:, 4 * i + k, 128 * t:128 * t + 128] for v in lhs],
                                [v[:, k, 0, :] for v in w], i + k == 0, i == 1 and k == 3, wm(k),
                                of(marks, 4 * i + k, t), fr, sig=(k == 3))
                    if t == 1:
                        done(m)
                bs[t] = (b, m)
                if t == 0:
                    between()

        def by_tokens(lhs, marks, n, sink, between=None):
            bs = [take() for _ in range(2)]
            if between:
                first_products(lhs, marks, n, bs, between)
                for t, (b, m) in enumerate(bs):
                    give(b, sink(t, b, m))
                return
            rows = 8 if n <= 256 else 4
            for k0 in range(0, 8, rows):
                h, lo, wm, done = next_weights()
                w = wview((h, lo), rows, 1, n)
                for t in range(2):
                    b, fr = bs[t]
                    for k in range(rows):
                        kk = k0 + k
                        m = mm3(b[:, 0:n], [v[:, kk, 128 * t:128 * t + 128] for v in lhs],
                                [v[:, k, 0, :] for v in w], kk == 0, kk == 7, wm(k), of(marks, kk, t), fr,
                                sig=(k == rows - 1))
                    bs[t] = (b, fr) if kk < 7 else (b, m)
                done(m)
            for t, (b, m) in enumerate(bs):
                give(b, sink(t, b, m))

        def by_features(rhs, marks, kt, parts, width, sink):
            h, lo, wm, done = next_weights()
            w = wview((h, lo), kt, parts, width)
            if parts == 1:
                sides = [[(0, 0), (0, 1)]]
            else:
                sides = [[(0, c), (1, c)] for c in range(width // 128)]
            for i, side in enumerate(sides):
                b, fr = take()
                for j, (a, c) in enumerate(side):
                    for k in range(kt):
                        m = mm3(b[:, 256 * j:256 * j + 256], [v[:, k, a, 128 * c:128 * c + 128] for v in w],
                                [v[:, k, :] for v in rhs[a]], k == 0, k == kt - 1, wm(k), marks[a][k], fr,
                                sig=(k == kt - 1 and j == 1))
                if i == len(sides) - 1:
                    done(m)
                give(b, sink(i, b, m))

        def down(src, marks, kts, tiles, sink, after_first=None, on_tile=None):
            bs = [[take() for _ in range(2)] for _ in range(tiles)]

            def rows(t, k0, h_, lo, wm, ks, last_sig):
                w = wview((h_, lo), 2, 1, 1024)
                new = []
                for k in ks:
                    for h in range(2):
                        b, fr = bs[t][h]
                        last = k == kts - 1
                        m = mm3(b[:, :], [v[:, k, 128 * t:128 * t + 128] for v in src],
                                [v[:, k - k0, 0, 512 * h:512 * h + 512] for v in w], k == 0, last,
                                wm(k - k0), marks(k), fr, sig=(last or (last_sig and k == ks[-1] and h == 1)))
                        if last:
                            new.append(sink(t, h, b, m))
                            give(b, new[-1])
                return m, new

            split = kts - 4 if on_tile else kts
            for k0 in range(0, split, 2):
                h_, lo, wm, done = next_weights()
                for k in (k0, k0 + 1):
                    for t in range(tiles):
                        m, _ = rows(t, k0, h_, lo, wm, (k,), k > k0 and t == tiles - 1)
                done(m)
                if k0 == 0 and after_first:
                    after_first()
            if on_tile:
                ws = [next_weights() for _ in range(2)]
                for t in range(2):
                    for i, (h_, lo, wm, done) in enumerate(ws):
                        k0 = split + 2 * i
                        m, new = rows(t, k0, h_, lo, wm, (k0, k0 + 1), True)
                        if t == 1:
                            done(m)
                            if i == 0:
                                prefill()
                    on_tile(t, new)

        t_free = [[None, None] for _ in range(2)]

        def swiglu(lhs, marks, chunks, tiles, dst, between=(), first=None):
            out = {}
            left = []

            def turn():
                for c0, n, t, m in left:
                    b, fr = take()
                    for c in range(n // 128):
                        mt = tr(b[:, 128 * c:128 * c + 128], TU[t][:, 128 * c:128 * c + 128], m, fr,
                                sig=(c == n // 128 - 1))
                    f = c0 // 128
                    md = parts([d[:, f:f + n // 128, 128 * t:128 * t + 128] for d in dst],
                               b[:, 0:n].rearrange("p (c k) -> p c k", k=128), mt)
                    give(b, md)
                    t_free[t][1] = mt
                    for c in range(n // 128):
                        out.setdefault(f + c, []).append(md)
                left.clear()

            for c0, c1 in chunks:
                n = c1 - c0
                rows = 8 if n <= 256 else 4
                bs = {(a, t): take() for a in range(2) for t in range(tiles)}
                for a in range(2):
                    if first and a == 0:
                        two = [bs[0, t] for t in range(2)]
                        first_products(lhs, marks, n, two, first)
                        bs[0, 0], bs[0, 1] = two
                        first = None
                        continue
                    for k0 in range(0, 8, rows):
                        h, lo, wm, done = next_weights()
                        w = wview((h, lo), rows, 1, n)
                        for t in range(tiles):
                            b, fr = bs[a, t]
                            for k in range(rows):
                                kk = k0 + k
                                m = mm3(b[:, 0:n], [v[:, kk, 128 * t:128 * t + 128] for v in lhs],
                                        [v[:, k, 0, :] for v in w], kk == 0, kk == 7, wm(k), of(marks, kk, t), fr,
                                        sig=(k == rows - 1))
                            if k0 + rows == 8:
                                bs[a, t] = (b, m)
                        done(m)
                turn()
                if between:
                    between.pop(0)()
                for t in range(tiles):
                    (bg, mg), (bu, mu) = bs[0, t], bs[1, t]
                    T, W = TT[t][:, 0:n], TU[t][:, 0:n]
                    fr = t_free[t]
                    m1 = A(lambda e: e.activation(T, bg[:, 0:n], ACT.Silu), mg, fr[0])
                    give(bg, m1)
                    m2 = V(lambda e: e.tensor_tensor(W, T, bu[:, 0:n], ALU.mult), m1, mu, fr[1])
                    give(bu, m2)
                    fr[0] = m2
                    left.append((c0, n, t, m2))
            return turn, lambda k: out[k]

        def add_to_x(x_marks, scale=0.5, alpha=None):
            new = []
            pre = x_marks
            if alpha is not None:
                pre = [V(lambda e: e.tensor_scalar(X[:, :], X[:, :], alpha, None, ALU.mult), x_marks)]

            def sink(t, h, b, m):
                o = XV[:, t, 512 * h:512 * h + 512]
                m = V(lambda e: e.scalar_tensor_tensor(o, b[:, :], scale, o, ALU.mult, ALU.add), m, pre)
                new.append(m)
                return m
            return sink, new

        def gates(lhs, marks, bias=None):
            for j in range(8):
                def sink(c, b, m, f=j):
                    if bias is None:
                        return A(lambda e: e.activation(GT[:, 512 * f:512 * f + 512], b[:, :], ACT.Tanh, scale=0.5), m)
                    for a in range(2):
                        r = A(lambda e, a=a: e.activation(GT[:, 512 * f + 256 * a:512 * f + 256 * a + 256],
                                                          b[:, 256 * a:256 * a + 256], ACT.Tanh, scale=0.5,
                                                          bias=bias[:, 8 * a + f:8 * a + f + 1]), m, bias_m)
                    return r
                by_features([lhs, lhs], [marks, marks], 8, 2, 128, sink)
                yield

        def mix(oa, ob, ma, mb, gt_m):
            out = []
            for j in range(4):
                def sink(c, b, m, j=j):
                    f = 2 * j + c
                    g = GT[:, 512 * f:512 * f + 512]
                    m = V(lambda e: e.scalar_tensor_tensor(g, g, 1.0, b[:, :], ALU.add, ALU.mult), m, gt_m)
                    r = V(lambda e: e.tensor_tensor(g[:, 0:256], g[:, 0:256], g[:, 256:512], ALU.add), m)
                    out.append(parts([d[:, 256 * f:256 * f + 256] for d in (MH, ML)], g[:, 0:256], r))
                    return m
                by_features([oa, ob], [ma, mb], 4, 2, 256, sink)
            return out

        pt_free = [None]

        def so_far():
            return [(q.sem, q.n) for q in (P, V, A, G)]

        def add_slots(extra, marks, last=False):
            for r in extra:
                r.free = [r.free, marks]
            slots[:] = slots + extra if last else extra + slots

        def drop_slots(extra):
            slots[:] = [r for r in slots if r not in extra]

        def transpose_p(src, heads, kts, m_src):
            marks = []
            blocks = [(h, i) for h in range(heads) for i in range(kts)]
            for c in range(0, len(blocks), 4):
                b, fr = take()
                part = blocks[c:c + 4]
                for n, (h, i) in enumerate(part):
                    m = tr(b[:, 128 * n:128 * n + 128], src(h, i), m_src[h], fr, cst_m, sig=(n == len(part) - 1))
                n = 128 * len(part)
                m = evac(PT[:, 128 * c:128 * c + n], b[:, 0:n], m, pt_free[0])
                give(b, m)
                marks += [m] * len(part)
            return marks

        def turn_o(o, t, dst, m):
            b, fr = take()
            for c in range(4):
                m2 = tr(b[:, 128 * c:128 * c + 128], o[:, 512 * t + 128 * c:512 * t + 128 * c + 128], m, fr,
                        sig=(c == 3))
            m2 = parts([d[:, :, 128 * t:128 * t + 128] for d in dst],
                       b[:, :].rearrange("p (c n) -> p c n", c=4), m2)
            give(b, m2)
            return m2

        def attention(q, k, v, bias, kts_of, q_m, k_m, v_m, sinks=None, l_free=None):
            state = {}

            def scores(t):
                kts = kts_of(t)
                n = 128 * kts
                L = LB[t]
                mx, nm, su = small(8), small(8), small(8)
                ms = []
                for h2 in range(4):
                    b, fr = take()
                    h0 = 4 * (h2 // 2) + h2 % 2
                    for i in range(2):
                        h = h0 + 2 * i
                        m = mm(b[:, 256 * i:256 * i + n], q(h, t), k(h)[:, 0:n], True, True,
                               q_m, k_m, fr, sig=(i == 1))
                    for i in range(2):
                        h = h0 + 2 * i
                        m = V(lambda e, h=h, b=b: e.tensor_tensor_reduce(
                            L[:, 256 * h:256 * h + n], b[:, 256 * i:256 * i + n], bias(h, t), 1.0,
                            NEG if sinks is None else sinks[:, h:h + 1], ALU.add, ALU.max, mx[:, h:h + 1]),
                            m, bias_marks, small_m)
                    give(b, m)
                m = V(lambda e: e.tensor_scalar(nm, mx, -1.0, None, ALU.mult), m)
                for h in range(8):
                    ms.append(A(lambda e, h=h: e.activation(L[:, 256 * h:256 * h + n], L[:, 256 * h:256 * h + n],
                                                            ACT.Exp, bias=nm[:, h:h + 1],
                                                            accum_out=su[:, h:h + 1]), m))
                last = ms[-1]
                if sinks is not None:
                    es = small(8)
                    m = V(lambda e: e.tensor_tensor(es, sinks, nm, ALU.add), m, small_m)
                    m = A(lambda e: e.activation(es, es, ACT.Exp), m)
                    last = V(lambda e: e.tensor_tensor(su, su, es, ALU.add), m, last)
                rs = small(8)
                last = V(lambda e: e.reciprocal(rs, su), last)
                state[t] = (ms, rs, last, kts)

            def values(t, out, *waits):
                ms, rs, rm, kts = state[t]
                L = LB[t]
                pm = transpose_p(lambda h, i: L[:, 256 * h + 128 * i:256 * h + 128 * i + 128], 8, kts, ms)
                b, fr = take()
                for h in range(8):
                    for i in range(kts):
                        m = mm(b[:, 64 * h:64 * h + 64], PT[:, 128 * (h * kts + i):128 * (h * kts + i) + 128],
                               v(h, i), i == 0, i == kts - 1, pm[h * kts + i], v_m, fr,
                               sig=(h == 7 and i == kts - 1))
                pt_free[0] = m
                o = out[:, 512 * t:512 * t + 512]
                m = V(lambda e: e.tensor_tensor(o.rearrange("p (h d) -> p h d", h=8),
                                                b[:, :].rearrange("p (h d) -> p h d", h=8),
                                                rs[:, :, None].to_broadcast([128, 8, 64]), ALU.mult), m, rm, *waits)
                give(b, m)
                return m
            return scores, values

        FV = [v[:, :].rearrange("p (f n) -> p f n", f=22) for v in (FH, FL_)]

        for f in (layer_one_slots, layer_two_slots):
            for l in range(2):
                plan(f(l))
        on_tile, finish, h_m, _ = boundary(rms(0, 0, None, S))
        for t in range(2):
            on_tile(t, x_m[t])
        for i in (0, 2):
            c = VECS[:, VEC["qk_b"] + i:VEC["qk_b"] + i + 1]
            qkb_m = G(lambda e: e.tensor_scalar(c, c, 0.125, None, ALU.mult), small_m)
        for l in range(2):
            QA = [U[:, 768 * t:768 * t + 768] for t in range(2)]
            QB = [U[:, 1536 + 1536 * t:3072 + 1536 * t] for t in range(2)]
            free_m = x_m

            got = {}

            def keep(key, dst):
                def sink(t, b, m):
                    n = dst(t).shape[1]
                    got[key, t] = evac(dst(t), b[:, 0:n], m, free_m)
                    return got[key, t]
                return sink

            by_tokens(HV, h_m, 512, keep("qa", lambda t: QA[t][:, 0:512]), finish)
            if l == 0:
                trig_m = rope_tables()
                scr_m = distance_table()
                pt_free[0] = scr_m
            raw_m = bias_one_rows(l, x_m)
            by_tokens(HV, h_m, 256, keep("kva", lambda t: QA[t][:, 512:768]))
            by_tokens(HV, h_m, 512, keep("qb", lambda t: QB[t][:, 0:512]))

            rt_m = []
            for t in range(2):
                sn = TRIG[:, 64 + 32 * t:96 + 32 * t]
                co = TRIG[:, 128 + 32 * t:160 + 32 * t]
                for w in range(2):
                    g = ROW[:, 128 * l + 64 * w:128 * l + 64 * w + 64]
                    base = 256 * t + 128 * w
                    for hf in range(2):
                        a = base + 32 * hf
                        rt_m.append(G(lambda e, a=a, co=co, g=g, hf=hf: e.tensor_tensor(
                            CS[:, a:a + 32], co, g[:, 32 * hf:32 * hf + 32], ALU.mult), trig_m, small_m, x_m))
                        a = base + 64 + 32 * hf
                        m = G(lambda e, a=a, sn=sn, g=g, hf=hf: e.tensor_tensor(
                            CS[:, a:a + 32], sn, g[:, 32 - 32 * hf:64 - 32 * hf], ALU.mult), trig_m, small_m, x_m)
                        if hf == 0:
                            m = G(lambda e, a=a: e.tensor_scalar(CS[:, a:a + 32], CS[:, a:a + 32], -1.0, None,
                                                                 ALU.mult), m)
                        rt_m.append(m)

            def norm(view, heads, marks):
                sq = PT[:, 0:64 * heads]
                ss, ms, rs = small(heads), small(heads), small(heads)
                m = A(lambda e: e.activation(sq, view, ACT.Square), marks, pt_free[0])
                m = V(lambda e: e.tensor_reduce(ss, sq.rearrange("p (h d) -> p h d", h=heads), AX.X, ALU.add), m)
                pt_free[0] = [pt_free[0], m]
                m = V(lambda e: e.tensor_scalar(ms, ss, 1.0 / 64, EPS, ALU.mult, ALU.add), m)
                m = rpow(rs, ms, m)
                vv = view.rearrange("p (h d) -> p h d", h=heads)
                return V(lambda e: e.tensor_tensor(vv, vv, rs[:, :, None].to_broadcast([128, heads, 64]),
                                                   ALU.mult), m)

            KD = LB[0]
            qa_m, ka_m, sums = [], [], []
            for t in range(2):
                m = norm(QA[t][:, 0:640], 10, [got["qa", t], got["kva", t]])
                room = (LB[1][:, 0:1280], LB[0][:, 512:1792])[t]
                tmp, tmp2 = room[:, 0:640], room[:, 640:1280]
                r = [m, h_m]
                for w, (h0, h1) in enumerate(((0, 8), (8, 10))):
                    n = h1 - h0
                    xq = QA[t][:, 64 * h0:64 * h1].rearrange("p (h d) -> p h d", h=n)
                    t1 = tmp[:, 64 * h0:64 * h1].rearrange("p (h d) -> p h d", h=n)
                    t2 = tmp2[:, 64 * h0:64 * h1].rearrange("p (h d) -> p h d", h=n)
                    cg = CS[:, 256 * t + 128 * w:256 * t + 128 * w + 64]
                    sg = CS[:, 256 * t + 128 * w + 64:256 * t + 128 * w + 128]
                    ms = [V(lambda e, t1=t1, xq=xq, cg=cg, n=n: e.tensor_tensor(
                        t1, xq, cg[:, None, :].to_broadcast([128, n, 64]), ALU.mult), r, rt_m)]
                    for hf in range(2):
                        ms.append(G(lambda e, t2=t2, xq=xq, sg=sg, n=n, hf=hf: e.tensor_tensor(
                            t2[:, :, 32 * hf:32 * hf + 32], xq[:, :, 32 - 32 * hf:64 - 32 * hf],
                            sg[:, None, 32 * hf:32 * hf + 32].to_broadcast([128, n, 32]), ALU.mult), r, rt_m))
                    if w == 0:
                        sums.append((qa_m, xq, t1, t2, ms))
                    else:
                        for d in range(2):
                            o = KD[:, 256 * t:256 * t + 256].rearrange("p (g d n) -> p g d n", g=2, d=2)[:, :, d, :]
                            sums.append((ka_m, o, t1, t2, ms))
            by_tokens(HV, h_m, 512, keep("kb", lambda t: QB[t][:, 512:1024]))
            for marks, o, t1, t2, ms in sums:
                marks.append(V(lambda e: e.tensor_tensor(o, t1, t2, ALU.add), ms, h_m))
            by_tokens(HV, h_m, 512, keep("vb", lambda t: QB[t][:, 1024:1536]))
            bias_marks = flip(QT, CST[:, C_JJ:C_JJ + 128], 3072, raw_m, CST[:, C_MB:C_MB + 64])
            gate_steps = gates(HV, h_m)

            def fold(dst, srcs, marks, scale):
                out = []
                n = srcs[0].shape[1] // 128
                for c2 in range(n // 2):
                    b, fr = take()
                    for c in (2 * c2, 2 * c2 + 1):
                        for t in range(2):
                            m = tr(b[:, 256 * (c % 2) + 128 * t:256 * (c % 2) + 128 * t + 128],
                                   srcs[t][:, 128 * c:128 * c + 128], marks, fr, sig=(c % 2 and t))
                    m = evac(dst[:, 512 * c2:512 * c2 + 512], b[:, :], m, bias_marks, scale=scale)
                    give(b, m)
                    out.append(m)
                return out

            qta = fold(QT[:, 0:1024], [QA[t][:, 0:512] for t in range(2)], qa_m, 0.125)
            kta = fold(QT[:, 1024:1536], [KD[:, 256 * t:256 * t + 256] for t in range(2)], ka_m, None)
            qkb = VECS[:, VEC["qk_b"] + 2 * l:VEC["qk_b"] + 2 * l + 2]
            qb_m = []
            for t in range(2):
                qb_m.append(norm(QB[t][:, 0:1024], 16, [got["qb", t], got["kb", t]]))

            def qa_of(h, t):
                return QT[64 * (h % 2):64 * (h % 2) + 64, 256 * (h // 2) + 128 * t:256 * (h // 2) + 128 * t + 128]

            def ka_of(h):
                return QT[64 * (h % 2):64 * (h % 2) + 64, 1024 + 256 * (h // 4):1280 + 256 * (h // 4)]

            sc_a, va_a = attention(qa_of, ka_of, lambda h, i: QA[i][:, 640 + 64 * (h // 4):704 + 64 * (h // 4)],
                                   lambda h, t: CST[:, C_MA + 256 * t:C_MA + 256 * t + 256], lambda t: 2,
                                   qta, kta, [got["kva", 0], got["kva", 1]],
                                   sinks=ROW[:, 256 + 8 * l:264 + 8 * l])
            next(gate_steps)
            sc_a(0)
            next(gate_steps)
            sc_a(1)
            last_a = (P.sem, P.n)
            next(gate_steps)
            qtb = fold(QT[:, 1536:2560], [QB[t][:, 0:512] for t in range(2)], qb_m + [qkb_m], qkb[:, 0:1])
            ktb = fold(QT[:, 2560:3584], [QB[t][:, 512:1024] for t in range(2)], qb_m, qkb[:, 1:2])

            def qb_of(h, t):
                a = 1536 + 256 * (h // 2) + 128 * t
                return QT[64 * (h % 2):64 * (h % 2) + 64, a:a + 128]

            def kb_of(h):
                a = 2560 + 256 * (h // 2)
                return QT[64 * (h % 2):64 * (h % 2) + 64, a:a + 256]

            BV = BIAS[:, :].rearrange("p (h j k) -> p h j k", h=8, j=6)
            sc_b, va_b = attention(qb_of, kb_of, lambda h, i: QB[i][:, 1024 + 64 * h:1088 + 64 * h],
                                   lambda h, t: BIAS[:, 384 * h + 128 - 128 * t:384 * h + 384 - 128 * t],
                                   lambda t: 2, qtb, ktb, [got["vb", 0], got["vb", 1]])
            OB = QT[:, 0:1024]
            oa = [v[:, 0:4, :] for v in HV]
            ob = [v[:, 4:8, :] for v in HV]
            next(gate_steps)
            oam = [va_a(0, O)]
            next(gate_steps)
            oam.append(va_a(1, O))
            sc_b(0)
            next(gate_steps)
            sc_b(1)
            for _ in gate_steps:
                pass
            gt_m = (A.sem, A.n)
            prefill()
            oam = [turn_o(O, t, oa, oam[t]) for t in range(2)]
            obm = [va_b(0, OB, last_a), va_b(1, OB, last_a)]
            obm = [turn_o(OB, t, ob, obm[t]) for t in range(2)]
            ended = so_far()
            add_slots(more, ended)
            mm_ = mix(oa, ob, [oam] * 4, [obm] * 4, gt_m)
            on_tile, finish, h_m, n_m = boundary(rms(1, l, ended))
            sink, new = add_to_x([x_m])
            down([d[:, :].rearrange("p (c n) -> p c n", c=8) for d in (MH, ML)], lambda k: mm_[k], 8, 2, sink,
                 on_tile=on_tile)
            x_m = new
            turn, u_m = swiglu(HV, h_m, F_CHUNKS, 2, FV, first=finish)
            on_tile, finish, h_m, n_m = boundary(rms(0, 1, n_m) if l == 0 else plain)
            sink, new = add_to_x(x_m, 1.0)
            down(FV, u_m, 22, 2, sink, turn, on_tile)
            drop_slots(more)
            x_m = new

        def rest_of_tokens(first, pos, gw, flag_m, x_m):
            queues = (P, V, A, G, S)
            compute = (P, V, A, G)
            before = [(q.sem, q.n) for q in compute]
            for q in queues:
                q.wait([before, flag_m])
            flag = nc.values_load(FLAG[0:1, 0:1], min_val=0, max_val=1)
            kept = [(q.sem, q.n, dict(q.seen)) for q in queues]
            kept_slots = list(slots)
            with nc.If(flag):
                for q, name in zip(compute, ("p", "v", "a", "g")):
                    q.sem, q.n = rest_sems[name], 0
                slots[:] = [Slot(f"rest{i}", r.room) for i, r in enumerate(slots)]
                count[:] = [0]
                set_free[:] = [None] * NSET
                free_banks[:] = [(b, None) for b, _ in free_banks]
                t_free[:] = [[None, None] for _ in range(2)]
                offset[0] = first
                for i in range(8):
                    plan(expert_slots(i))
                experts(128, pos, gw, None, None, None, None)
                after = [(q.sem, q.n) for q in compute if q.n]
                for q in queues:
                    q.wait(after)
            for q, (sem, n, seen) in zip(queues, kept):
                q.sem, q.n, q.seen = sem, n, seen
            slots[:] = kept_slots
            count[:] = [0]
            free_banks[:] = [(b, None) for b, _ in free_banks]
            return None

        def norm_rows(l, i, dst, marks):
            return load("ln", dst[:, 0:2048], bass.AP(ln_d.tensor, (2 * l + i) * 2048, [[0, 128], [1, 2048]]), marks)

        def layer_norm(gb, gb_m):
            def norm(t, x_marks):
                st, ag, ve, rs = small(12), small(2), small(1), small(1)
                for h in range(2):
                    m = V(lambda e, h=h, t=t: e.bn_stats(st[:, 6 * h:6 * h + 6], XV[:, t, 512 * h:512 * h + 512]),
                          x_marks)
                m = V(lambda e: e.bn_aggr(ag, st), m)
                m = V(lambda e: e.tensor_scalar(ve, ag[:, 1:2], LN_EPS, None, ALU.add), m)
                m = rpow(rs, ve, m)
                xt = XV[:, t, :]
                m = V(lambda e: e.tensor_scalar(xt, xt, ag[:, 0:1], rs[:, 0:1], ALU.subtract, ALU.mult), m)
                m = V(lambda e: e.tensor_tensor(xt, xt, gb[:, 0:1024], ALU.mult), m, gb_m)
                m = V(lambda e: e.tensor_tensor(xt, xt, gb[:, 1024:2048], ALU.add), m)
                return m, xt
            return norm

        EV = [v[:, :].rearrange("p (f n) -> p f n", f=28) for v in (EH, EL)]
        rws_m = parts([RWS[:, 0:64], RWS[:, 64:128]], RW[:, :], small_m)

        def experts(base, pos, gw, pos_m, gm, xs_m, x_m):
            g_free = [[None] * 4 for _ in range(2)]
            y_free = [None]
            got = {}

            def gather(e_):
                i = e_ % 2
                fr_ = g_free[i]
                ms, mt, out, sel_m = [], [], [], []
                got[e_] = (out, sel_m)

                def select():
                    for t in range(2):
                        p = pos[:, 8 * t + e_:8 * t + e_ + 1]
                        row = CST[:, C_ROW:C_ROW + 128]
                        mt.append(V(lambda e: e.tensor_scalar(SEL[i][:, 128 * t:128 * t + 128], row, float(base), p,
                                                              ALU.add, ALU.is_equal), pos_m, fr_[0]))
                        ms.append(V(lambda e: e.tensor_scalar(SELR[i][:, 128 * t:128 * t + 128], row, float(base), p,
                                                              ALU.add, ALU.is_equal), pos_m, fr_[1]))

                def step(src, dst, c4):
                    b, fr = take()
                    for c in range(4 * c4, 4 * c4 + 4):
                        for t in range(2):
                            a = 1024 * t + 128 * c
                            m = P(lambda e: e.matmul(b[:, 128 * (c % 4):128 * (c % 4) + 128], src[:, a:a + 128],
                                                     SELR[i][:, 128 * t:128 * t + 128], start=(t == 0),
                                                     stop=(t == 1)), ms, xs_m, fr, sig=(c % 4 == 3 and t == 1))
                    m2 = evac(dst[:, 512 * c4:512 * c4 + 512], b[:, :], m, eng=A)
                    give(b, m2)
                    out.append(m2)
                    fr_[1] = m

                def turn():
                    b, fr = take()
                    for t in range(2):
                        m = tr(b[:, 128 * t:128 * t + 128], SEL[i][:, 128 * t:128 * t + 128], mt, fr, sig=(t == 1))
                    fr_[0] = m
                    sel_m.append(evac(SELT[i][:, :], b[:, 0:256], m, fr_[2], eng=A))
                    give(b, sel_m[0])

                def last():
                    step(XL, GL[i], 1)
                    turn()
                return [select, lambda: step(XH, GH[i], 0), lambda: step(XH, GH[i], 1),
                        lambda: step(XL, GL[i], 0), last]

            def scatter(e_, t, y_m, x_m):
                i = e_ % 2
                new = []
                for h in range(2):
                    b, fr = take()
                    w = SELT[i][:, 128 * t:128 * t + 128]
                    P(lambda e: e.matmul(b[:, :], w, YH[:, 512 * h:512 * h + 512], start=True, stop=False),
                      y_m, got[e_][1], fr, sig=False)
                    m = P(lambda e: e.matmul(b[:, :], w, YL[:, 512 * h:512 * h + 512], start=False, stop=True))
                    o = XV[:, t, 512 * h:512 * h + 512]
                    m2 = V(lambda e: e.scalar_tensor_tensor(o, b[:, :], gw[:, 8 * t + e_:8 * t + e_ + 1], o,
                                                            ALU.mult, ALU.add), m, gm, x_m[t])
                    give(b, m2)
                    new.append(m2)
                y_free[0] = m
                g_free[i][2] = m
                x_m[t] = new

            x_m = [x_m, x_m]
            for f in gather(0):
                f()
            late = None
            for e_ in range(8):
                lhs = [v[:, :].rearrange("p (k n) -> p k n", k=8) for v in (GH[e_ % 2], GL[e_ % 2])]
                between = []
                if late:
                    for t in range(2):
                        between.append(lambda t=t, y=late: scatter(e_ - 1, t, y, x_m))
                if e_ < 7:
                    between += gather(e_ + 1)
                turn, u_m = swiglu(lhs, [got[e_][0]] * 8, E_CHUNKS, 1, EV, between)
                y_m = []

                def sink(t, h, b, m):
                    y_m.append(parts([YH[:, 512 * h:512 * h + 512], YL[:, 512 * h:512 * h + 512]], b[:, :], m,
                                     y_free[0]))
                    return y_m[-1]
                down(EV, u_m, 28, 1, sink, turn)
                late = y_m
            for t in range(2):
                scatter(7, t, late, x_m)
            return [x_m]

        bg_m = G(lambda e: e.tensor_scalar(VECS[:, VEC["b_gate"]:VEC["b_gate"] + 32],
                                           VECS[:, VEC["b_gate"]:VEC["b_gate"] + 32], 0.5, None, ALU.mult), small_m)
        bias_m = bg_m
        for l in range(2):
            x_f = h_m
            R = [U[:, 1024 * i:1024 * i + 1024] for i in range(7)]
            XM, XC, ZT, QM, KM, VM, VT = R

            def pairs(dst, out, scale=None, wait=None):
                def sink(c, b, m):
                    m = evac(dst[:, 512 * c:512 * c + 512], b[:, :], m, wait, scale=scale)
                    out.append(m)
                    return m
                return sink
            q_m, k_m, v_m, xm_m, z_m = [], [], [], [], []

            def vsink(t, b, m):
                m = evac(QT[:, 2048 + 512 * t:2560 + 512 * t], b[:, :], m)
                v_m.append(m)
                return m
            by_tokens(HV, x_f, 512, vsink, finish)
            for c in range(2):
                by_features([HV], [x_f], 8, 1, 256, pairs(QT[:, 512 * c:512 * c + 512], q_m, 0.125))
            if l == 0:
                raw_m = bias_two_rows(x_m)
            for c in range(2):
                by_features([HV], [x_f], 8, 1, 256, pairs(QT[:, 1024 + 512 * c:1536 + 512 * c], k_m))

            if l == 0:
                bias_marks = flip(GT, CST[:, C_J:C_J + 128], 2048, raw_m)
            sc, va = attention(
                lambda h, t: QT[64 * (h % 2):64 * (h % 2) + 64,
                                256 * (h // 2) + 128 * t:256 * (h // 2) + 128 * t + 128],
                lambda h: QT[64 * (h % 2):64 * (h % 2) + 64, 1024 + 256 * (h // 2):1280 + 256 * (h // 2)],
                lambda h, i: QT[:, 2048 + 512 * i + 64 * h:2112 + 512 * i + 64 * h],
                lambda h, t: BIAS[:, 256 * h + 128 * (1 - t):256 * h + 256], lambda t: t + 1, q_m, k_m, v_m)
            sc(0)
            for c in range(2):
                by_features([HV], [x_f], 8, 1, 256, pairs(XM[:, 512 * c:512 * c + 512], xm_m, wait=bias_marks))

            def zsink(i, b, m):
                z = ZT[:, 512 * c:512 * c + 512]
                m = A(lambda e: e.activation(z, b[:, :], ACT.Tanh, scale=0.5), m, bias_marks)
                z_m.append(V(lambda e: e.tensor_scalar(z, z, 1.0, 0.5, ALU.add, ALU.mult), m))
                return m
            for c in range(2):
                by_features([HV], [x_f], 8, 1, 256, zsink)
            sc(1)
            gate_steps = gates(HV, x_f, VECS[:, VEC["b_gate"] + 16 * l:VEC["b_gate"] + 16 * l + 16])
            xc_m = []

            def conv(h):
                c = XC[:, 256 * h:256 * h + 256]
                xm = XM[:, 256 * h:256 * h + 256]

                def cw(j, h=h):
                    a = VEC["conv_w"] + 16 * l + 4 * j + h
                    return VECS[:, a:a + 1]
                cb = VECS[:, VEC["conv_b"] + 4 * l + h:VEC["conv_b"] + 4 * l + h + 1]
                m = V(lambda e, c=c, xm=xm, cw=cw, cb=cb: e.tensor_scalar(c, xm, cw(3), cb, ALU.mult, ALU.add),
                      xm_m, small_m)
                for d in (1, 2, 3):
                    m = V(lambda e, c=c, xm=xm, cw=cw, d=d: e.scalar_tensor_tensor(
                        c[:, d:256], xm[:, 0:256 - d], cw(3 - d), c[:, d:256], ALU.mult, ALU.add), m)
                tt = KM[:, 256 * h:256 * h + 256]
                m1 = A(lambda e, c=c, tt=tt: e.activation(tt, c, ACT.Tanh, scale=0.5), m)
                xc_m.append(V(lambda e, c=c, tt=tt: e.scalar_tensor_tensor(c, tt, 1.0, c, ALU.add, ALU.mult), m1))
            next(gate_steps)
            conv(0)
            next(gate_steps)
            conv(1)
            oam = [va(0, O)]
            conv(2)
            next(gate_steps)
            oam.append(va(1, O))
            conv(3)
            oa = [v[:, 0:4, :] for v in HV]
            ob = [v[:, 4:8, :] for v in HV]
            OM = QT[:, 0:1024]
            q_read = (P.sem, P.n)

            slot, _, wm, done = next_weights()
            wqk = slot[:, 0:1024].rearrange("p (a n) -> p a n", a=8)
            wv = slot[:, 1024:1536].rearrange("p (a n) -> p a n", a=4)
            wif = slot[:, 1536:1632].rearrange("p (a n) -> p a n", a=12)
            got = {}

            def heads(key, w0, src, dst, scale, ms):
                for h2 in range(2):
                    b, fr = take()
                    for h in (2 * h2, 2 * h2 + 1):
                        w = wv[:, h, :] if w0 is None else wqk[:, w0 + h, :]
                        m = mm(b[:, 256 * (h % 2):256 * (h % 2) + 256], w, src[:, 256 * h:256 * h + 256],
                               True, True, wm, ms, fr, sig=(h % 2 == 1))
                    m = evac(dst[:, 512 * h2:512 * h2 + 512], b[:, :], m, scale=scale)
                    give(b, m)
                    got.setdefault(key, []).append(m)

            heads("v", None, XM, VM, None, xm_m)
            vt_m = []
            for t in range(2):
                b, fr = take()
                for h in range(4):
                    m = mm(b[:, 128 * h:128 * h + 128], XM[:, 256 * h + 128 * t:256 * h + 128 * t + 128],
                           wv[:, h, :], True, True, wm, xm_m, fr, sig=(h == 3))
                m = evac(VT[:, 512 * t:512 * t + 512], b[:, :], m)
                give(b, m)
                vt_m.append(m)
            heads("q", 0, XC, QM, 0.5, xc_m)
            heads("k", 4, XC, KM, 0.5, xc_m)
            IF = SM[:, 484:500].rearrange("p (t n) -> p t n", t=2)
            FL = small(8).rearrange("p (t n) -> p t n", t=2)
            ab, lg = small(8), small(8)
            b, fr = take()
            for t in range(2):
                n = 0
                for key, src in (("q", QM), ("k", KM), ("v", VM)):
                    for h in range(4):
                        m = mm(b[:, 8 * t:8 * t + 8], src[:, 256 * h + 128 * t:256 * h + 128 * t + 128],
                               wif[:, n, :], n == 0, n == 11, got[key], fr, wm, sig=(n == 11 and t == 1))
                        n += 1
            done(m)
            m = V(lambda e, b=b: e.tensor_tensor(IF, b[:, 0:16].rearrange("p (t n) -> p t n", t=2),
                                            ROW[:, None, 272 + 8 * l:280 + 8 * l].to_broadcast([128, 2, 8]),
                                            ALU.add), m)
            give(b, m)
            fp = IF[:, :, 4:8]
            abv = ab.rearrange("p (t n) -> p t n", t=2)
            m1 = V(lambda e: e.scalar_tensor_tensor(abv, fp, -1.0, fp, ALU.mult, ALU.max), m)
            m1 = A(lambda e: e.activation(ab, ab, ACT.Exp, scale=-1.0), m1)
            m1 = A(lambda e: e.activation(lg, ab, ACT.Ln, bias=1.0), m1)
            if_m = V(lambda e: e.scalar_tensor_tensor(FL, fp, 0.0, lg.rearrange("p (t n) -> p t n", t=2),
                                                      ALU.min, ALU.subtract), m1)
            FN = small(8).rearrange("p (t n) -> p t n", t=2)
            fn_m = V(lambda e: e.tensor_scalar(FN, FL, -1.0, None, ALU.mult), if_m)
            next(gate_steps)
            b, fr = take()
            m = mm(b[:, 0:4], tri, FL[:, 0, :], True, True, if_m, fr)
            m = mm(b[:, 4:8], ones, FL[:, 0, :], True, False)
            m = mm(b[:, 4:8], tri, FL[:, 1, :], False, True, sig=True)
            BC = SM[:, 500:508]
            bc_m = V(lambda e, b=b: e.tensor_copy(BC, b[:, 0:8]), m)
            give(b, bc_m)
            rows = []
            for h2 in range(2):
                b, fr = take()
                for h in (2 * h2, 2 * h2 + 1):
                    o = 256 * (h % 2)

                    def bc(v, t, c):
                        return v[:, t, c:c + 1].to_broadcast([128, 128])
                    mm(b[:, o:o + 128], bc(IF, 0, h), ident, True, False, fn_m, fr)
                    mm(b[:, o:o + 128], bc(FN, 0, h), tri, False, True)
                    mm(b[:, o + 128:o + 256], bc(IF, 1, h), ident, True, False)
                    mm(b[:, o + 128:o + 256], bc(FN, 0, h), ones, False, False)
                    m = mm(b[:, o + 128:o + 256], bc(FN, 1, h), tri, False, True, sig=(h % 2 == 1))
                rows.append((b, m))
            mst = {}
            for t in range(2):
                n = 128 * (t + 1)
                mx, nm = small(4), small(4)
                L = LB[t]
                for h in range(4):
                    b, rm = rows[h // 2]
                    m = V(lambda e, h=h, b=b: e.tensor_tensor_reduce(
                        L[:, 256 * h:256 * h + n], b[:, 256 * (h % 2):256 * (h % 2) + n],
                        CST[:, C_CAUS + 256 - n:C_CAUS + 256], 1.0, 0.0, ALU.add, ALU.max, mx[:, h:h + 1]),
                        rm, oam)
                    if t == 1 and h % 2:
                        give(b, m)
                m = V(lambda e: e.tensor_scalar(nm, mx, -1.0, None, ALU.mult), m)
                em = []
                for h in range(4):
                    em.append(A(lambda e, h=h: e.activation(L[:, 256 * h:256 * h + n], L[:, 256 * h:256 * h + n],
                                                            ACT.Exp, bias=nm[:, h:h + 1]), m))
                gd = small(4)
                m = V(lambda e, t=t: e.tensor_tensor(gd, nm, BC[:, 4 * t:4 * t + 4], ALU.subtract), m, bc_m)
                gd_m = A(lambda e: e.activation(gd, gd, ACT.Exp), m)
                nq = small(4)
                pm = []
                for h2 in range(2):
                    b, fr = take()
                    for h in (2 * h2, 2 * h2 + 1):
                        o = 256 * (h % 2)
                        m = mm(b[:, o:o + n], QM[:, 256 * h + 128 * t:256 * h + 128 * t + 128],
                               KM[:, 256 * h:256 * h + n], True, True, fr, sig=(h % 2 == 1))
                    for h in (2 * h2, 2 * h2 + 1):
                        o = 256 * (h % 2)
                        m = V(lambda e, h=h, b=b, o=o: e.scalar_tensor_tensor(
                            L[:, 256 * h:256 * h + n], b[:, o:o + n], 128 ** -0.5, L[:, 256 * h:256 * h + n],
                            ALU.mult, ALU.mult, accum_out=nq[:, h:h + 1]), m, em[h])
                        pm.append(m)
                    give(b, m)
                m = V(lambda e: e.scalar_tensor_tensor(nq, nq, -1.0, nq, ALU.mult, ALU.max), m)
                m = V(lambda e: e.tensor_tensor(nq, nq, gd, ALU.max), m, gd_m)
                rq = small(4)
                m = V(lambda e: e.reciprocal(rq, nq), m)
                mst[t] = (pm, rq, m)
                next(gate_steps)
            mn = []
            for t in range(2):
                pm, rq, rqm = mst[t]
                L = LB[t]
                kts = t + 1
                tm = transpose_p(lambda h, i: L[:, 256 * h + 128 * i:256 * h + 128 * i + 128], 4, kts, pm)
                b, fr = take()
                for h in range(4):
                    for i in range(kts):
                        m = mm(b[:, 128 * h:128 * h + 128], PT[:, 128 * (h * kts + i):128 * (h * kts + i) + 128],
                               VT[:, 512 * i + 128 * h:512 * i + 128 * h + 128], i == 0, i == kts - 1,
                               tm[h * kts + i], vt_m, fr, sig=(h == 3 and i == kts - 1))
                pt_free[0] = m
                o = OM[:, 512 * t:512 * t + 512]
                ov = o.rearrange("p (h d) -> p h d", h=4)
                m = V(lambda e, ov=ov, b=b, rq=rq: e.tensor_tensor(
                    ov, b[:, :].rearrange("p (h d) -> p h d", h=4),
                    rq[:, :, None].to_broadcast([128, 4, 128]), ALU.mult), m, rqm, q_read)
                give(b, m)
                st, ag, ve, rs = small(24), small(8), small(4), small(4)
                for h in range(4):
                    m2 = V(lambda e, h=h: e.bn_stats(st[:, 6 * h:6 * h + 6], o[:, 128 * h:128 * h + 128]), m)
                for h in range(4):
                    m3 = V(lambda e, h=h: e.bn_aggr(ag[:, 2 * h:2 * h + 2], st[:, 6 * h:6 * h + 6]), m2)
                m4 = V(lambda e: e.tensor_scalar(ve, ag.rearrange("p (h a) -> p h a", a=2)[:, :, 1], LN_EPS, None,
                                                 ALU.add), m3)
                m4 = rpow(rs, ve, m4)
                for h in range(4):
                    m = V(lambda e, h=h: e.tensor_scalar(o[:, 128 * h:128 * h + 128], o[:, 128 * h:128 * h + 128],
                                                         ag[:, 2 * h:2 * h + 1], rs[:, h:h + 1],
                                                         ALU.subtract, ALU.mult), m4)
                mn.append(m)
                next(gate_steps)
            for _ in gate_steps:
                pass
            gt_m = (A.sem, A.n)
            prefill()
            oam = [turn_o(O, t, oa, oam[t]) for t in range(2)]
            obm = []
            for t in range(2):
                o = OM[:, 512 * t:512 * t + 512]
                m = mn[t]
                b, fr = take()
                for c in range(4):
                    m2 = tr(b[:, 128 * c:128 * c + 128], o[:, 128 * c:128 * c + 128], m, fr, sig=(c == 3))
                for h in range(4):
                    g = VECS[:, VEC["m_g"] + 4 * l + h:VEC["m_g"] + 4 * l + h + 1]
                    m = V(lambda e, h=h, g=g, b=b, t=t: e.scalar_tensor_tensor(
                        o[:, 128 * h:128 * h + 128], b[:, 128 * h:128 * h + 128], g,
                        ZT[:, 256 * h + 128 * t:256 * h + 128 * t + 128], ALU.mult, ALU.mult), m2, z_m)
                give(b, m)
                obm.append(parts([d[:, :, 128 * t:128 * t + 128] for d in ob],
                                 o.rearrange("p (c n) -> p c n", c=4), m))

            if l == 0:
                add_slots(more, so_far())
            ended = so_far()
            mm_ = mix(oa, ob, [oam] * 4, [obm] * 4, gt_m)
            gb_m = norm_rows(l, 0, LNB, ended)
            sink, new = add_to_x(x_m, alpha=ALPHA)
            on_tile, finish, x_f, n_m = boundary(layer_norm(LNB, gb_m))
            down([d[:, :].rearrange("p (c n) -> p c n", c=8) for d in (MH, ML)], lambda k: mm_[k], 8, 2, sink,
                 on_tile=on_tile)
            x_m = n_m
            if l == 0:
                turn, u_m = swiglu(HV, x_f, F_CHUNKS, 2, FV, first=finish)
                gb_m = norm_rows(l, 1, LNB, x_m)
                sink, new = add_to_x([x_m, x_f], 1.0, ALPHA)
                on_tile, finish, h_m, x_m = boundary(layer_norm(LNB, gb_m))
                down(FV, u_m, 22, 2, sink, turn, on_tile)
                drop_slots(more)
            else:
                add_slots(once, so_far())
                gw, pos = SM[:, 484:500], SM[:, 512:528]
                gm = []
                sm = []
                se = small(16)
                for t in range(2):
                    if t == 1:
                        finish()
                    b, fr = take()
                    for k in range(8):
                        m = mm3(b[:, 0:8], [v[:, k, 128 * t:128 * t + 128] for v in HV],
                                [RWS[:, 64 * i + 8 * k:64 * i + 8 * k + 8] for i in range(2)], k == 0, k == 7,
                                of(x_f, k, t), fr, rws_m, sig=(k == 7))
                    lo, s1, f1, s2, tmp = small(8), small(8), small(8), small(8), small(8)
                    v1, v2, d, a1, a2, i1 = (small(1) for _ in range(6))
                    io = CST[:, C_IOTA:C_IOTA + 8]
                    m = V(lambda e, b=b: e.tensor_tensor(lo, b[:, 0:8], ROW[:, 288:296], ALU.add), m)
                    give(b, m)

                    def first_of(src, val, sel, m):
                        m = V(lambda e: e.tensor_reduce(val, src, AX.X, ALU.max), m)
                        m = V(lambda e: e.scalar_tensor_tensor(tmp, src, val[:, 0:1], io, ALU.is_equal, ALU.mult), m)
                        m = V(lambda e: e.tensor_reduce(i1, tmp, AX.X, ALU.max), m)
                        return V(lambda e: e.tensor_scalar(sel, io, i1[:, 0:1], None, ALU.is_equal), m)
                    m = first_of(lo, v1, s1, m)
                    m = V(lambda e: e.scalar_tensor_tensor(f1, s1, -3e38, lo, ALU.mult, ALU.add), m)
                    m = first_of(f1, v2, s2, m)
                    sm.append(V(lambda e, t=t: e.tensor_tensor(se[:, 8 * t:8 * t + 8], s1, s2, ALU.add), m))
                    m = V(lambda e: e.tensor_tensor(d, v2, v1, ALU.subtract), m)
                    m = A(lambda e: e.activation(d, d, ACT.Exp), m)
                    m = V(lambda e: e.tensor_scalar(a1, d, 1.0, None, ALU.add), m)
                    m = V(lambda e: e.reciprocal(a1, a1), m)
                    m = V(lambda e: e.tensor_tensor(a2, a1, d, ALU.mult), m)
                    m = V(lambda e: e.tensor_scalar(s1, s1, a1[:, 0:1], None, ALU.mult), m)
                    m = V(lambda e, t=t: e.scalar_tensor_tensor(gw[:, 8 * t:8 * t + 8], s2, a2[:, 0:1], s1,
                                                                ALU.mult, ALU.add), m)
                    gm.append(m)
                b, fr = take()
                mm(b[:, 0:8], tri, se[:, 0:8], True, True, sm, fr)
                mm(b[:, 8:16], ones, se[:, 0:8], True, False)
                m = mm(b[:, 8:16], tri, se[:, 8:16], False, True, sig=True)
                m = V(lambda e: e.tensor_tensor(pos, b[:, 0:16], se, ALU.mult), m)
                pos_m = V(lambda e: e.tensor_scalar(pos, pos, -1.0, None, ALU.add), m)
                give(b, m)
                xs_m = [parts([d[:, 1024 * t:1024 * t + 1024] for d in (XH, XL)], XV[:, t, :], x_m) for t in range(2)]
                pre = V(lambda e: e.tensor_scalar(X[:, :], X[:, :], ALPHA, None, ALU.mult), x_m, x_f, xs_m)
                b, fr = take()
                mm(b[:, 0:8], ones, se[:, 0:8], True, False, sm, fr)
                m = mm(b[:, 0:8], ones, se[:, 8:16], False, True, sig=True)
                most = small(1)
                m = V(lambda e: e.tensor_reduce(most, b[:, 0:8], AX.X, ALU.max), m)
                give(b, m)
                flag_m = V(lambda e: e.tensor_scalar(FLAG[:, :], most, 128.0, None, ALU.is_gt), m)
                first = ws_d.shape[0] - 128 * sum(slot_words(s) for i in range(8) for s in expert_slots(i))
                gb_m = norm_rows(l, 1, BIAS, so_far())
                add_slots(spare, so_far(), True)
                x_m = experts(0, pos, gw, pos_m, gm, xs_m, [pre])
                x_m = rest_of_tokens(first, pos, gw, flag_m, x_m)

        norm = layer_norm(BIAS, gb_m)
        out_m = [load("out", out_d[0, 128 * t:128 * t + 128, :], XV[:, t, :], norm(t, x_m)[0], q=S) for t in range(2)]

        S.wait([out_m, scr_m])


def kernel(**inputs):
    import numpy as _np
    import concourse.bacc as _bacc
    from concourse import mybir as _mybir
    from concourse.bass_utils import run_bass_kernel_spmd as _run

    I = {k: _np.asarray(v) for k, v in inputs.items()}

    def tiles(w):
        return w.reshape(w.shape[0] // 128, 128, w.shape[1]).transpose(1, 0, 2)

    def lay(s, l):
        if s != "mlstm":
            return _np.stack([tiles(I[n][idx][128 * r0:128 * r1, c0:c1]) for n, idx, r0, r1, c0, c1 in s], axis=2)
        return _np.concatenate([I["w_qk_m_2"][l].reshape(8, 128, 128).transpose(1, 0, 2).reshape(128, -1),
                                I["w_v_m_2"][l].transpose(1, 0, 2).reshape(128, -1),
                                tiles(I["w_if_2"][l]).reshape(128, -1)], axis=1)

    ws = _np.concatenate([lay(s, l).ravel() for f in (layer_one_slots, layer_two_slots) for l in range(2)
                          for s in f(l)])

    def cols(a):
        return a.reshape(-1, 128).T
    twice = lambda a: _np.concatenate([a, a])
    vec = _np.ascontiguousarray(_np.concatenate(
        [cols(I[n]) for n in ("b_gate_2", "conv_w_2", "conv_b_2", "m_norm_g_2")]
        + [_np.stack([twice(I[n][l]) for l in range(2) for n in ("q_norm_b", "k_norm_b")], axis=1)], axis=1))
    row = _np.concatenate([I["q_norm_a"][0], I["k_norm_a"][0], I["q_norm_a"][1], I["k_norm_a"][1],
                           I["sink_a"].ravel(), I["b_if_2"].ravel(), I["router_b_2"].ravel()])
    ln = _np.concatenate([_np.stack([I["ln_g_2"], I["ln_b_2"]], axis=2).ravel(),
                          I["attn_norm_g"].ravel(), I["ffn_norm_g"].ravel()])
    relb = _np.zeros((2, 8, 15, 127), _np.float32)
    relb[..., 48:79] = I["rel_bias_b"]
    relb = _np.stack([relb[:, :, 5 - s:11 - s] for s in range(2)], axis=1)
    one, lnc = distance_constants()
    arrays = {"x": I["x"], "pos": _np.ascontiguousarray(I["positions"].reshape(2, 128).T), "ws": ws, "vec": vec, "row": row, "ln": ln,
              "rel": I["rel_bias_2"], "relb": relb,
              "rw": _np.ascontiguousarray(tiles(I["router_w_2"][0]).reshape(128, 64)),
              "cst": constants(), "one": one, "lnc": lnc}
    nc = _bacc.Bacc("TRN2", target_bir_lowering=False, num_devices=1)
    ins, args = {}, []
    for name, a in arrays.items():
        a = _np.ascontiguousarray(a)
        ins[f"in_{name}"] = a
        args.append(nc.dram_tensor(f"in_{name}", a.shape, _mybir.dt.from_np(a.dtype), kind="ExternalInput").ap())
    out = nc.dram_tensor("out_0", (1, 256, 1024), _mybir.dt.float32, kind="ExternalOutput").ap()
    program(nc, *args, out)
    r = _run(nc, [ins], core_ids=[0])
    return r.results[0]["out_0"]
```
